# Optimizing a Trainium2 kernel written in Bass

```python
import jax, jax.numpy as jnp
from jax import lax
import numpy as np
import math

D_MODEL = 1024
BATCH = 1
SEQ = 512
DEPTH = 2

GRID_W = 64
CTX_LEN = 256
EPS = 1e-6
NEG_INF = -1e30
MIX_WIDTH = D_MODEL
A_GROUPS = 4
A_CHUNK = 128
A_WIDTH = MIX_WIDTH // 2
A_GDIM = A_WIDTH // A_GROUPS
B_HEADS = 8
B_WIDTH = MIX_WIDTH - A_WIDTH
B_HDIM = B_WIDTH // B_HEADS
NA_ROWS = 8
NA_COLS = 16
NA_QCB = NA_COLS
NA_KCB = 2 * NA_COLS
C_HEADS = 16
C_KV_HEADS = 4
C_HDIM = D_MODEL // C_HEADS
C_QBLOCK = 128
ROPE_THETA = 10000.0
D_FF = 2816
CONV_W = 3
N_EVEN = (DEPTH + 1) // 2
N_ODD = DEPTH // 2
IN_AB = 2 * A_WIDTH + 3 * B_WIDTH
IN_C = (C_HEADS + 2 * C_KV_HEADS) * C_HDIM


def rms_norm(x, g):
    xf = x.astype(jnp.float32)
    y = xf * lax.rsqrt(jnp.mean(xf * xf, axis=-1, keepdims=True) + EPS)
    return (y * g.astype(jnp.float32)).astype(x.dtype)

def layer_norm(x, g):
    xf = x.astype(jnp.float32)
    mu = jnp.mean(xf, axis=-1, keepdims=True)
    var = jnp.mean(jnp.square(xf - mu), axis=-1, keepdims=True)
    return ((xf - mu) * lax.rsqrt(var + EPS) * g.astype(jnp.float32)).astype(x.dtype)

def ada_chunks(cvec, w, b):
    m = jax.nn.silu(cvec) @ w + b
    return jnp.split(m[..., None, :], 6, axis=-1)

def modulate(x, g, shift, scale):
    return rms_norm(x, g) * (1 + scale) + shift

def axial_rope(n_tokens, head_dim):
    t = jnp.arange(n_tokens)
    quarter = head_dim // 4
    inv = ROPE_THETA ** (-jnp.arange(quarter, dtype=jnp.float32) / quarter)
    rows = (t // GRID_W).astype(jnp.float32)[:, None] * inv
    cols = (t % GRID_W).astype(jnp.float32)[:, None] * inv
    ang = jnp.concatenate([rows, cols], axis=-1)
    return jnp.cos(ang), jnp.sin(ang)

def apply_rope(x, cos, sin):
    xf = x.astype(jnp.float32)
    x1, x2 = jnp.split(xf, 2, axis=-1)
    cs, sn = cos[:, None, :], sin[:, None, :]
    return jnp.concatenate([x1 * cs - x2 * sn, x1 * sn + x2 * cs], axis=-1).astype(x.dtype)

def gqa_attend(q, k, v):
    bn, lq, hq, dh = q.shape
    hkv = k.shape[2]
    qg = q.reshape(bn, lq, hkv, hq // hkv, dh)
    s = jnp.einsum('bqhgd,bkhd->bhgqk', qg, k).astype(jnp.float32) * (dh ** -0.5)
    p = jax.nn.softmax(s, axis=-1).astype(v.dtype)
    return jnp.einsum('bhgqk,bkhd->bqhgd', p, v).reshape(bn, lq, hq * dh)

def gqa_blocked(q, k, v, k_ctx, v_ctx):
    bn, s_len, hq, dh = q.shape
    keys = jnp.concatenate([k, k_ctx], axis=1)
    vals = jnp.concatenate([v, v_ctx], axis=1)
    qb = q.reshape(bn, s_len // C_QBLOCK, C_QBLOCK, hq, dh).transpose(1, 0, 2, 3, 4)
    ob = lax.map(lambda qi: gqa_attend(qi, keys, vals), qb)
    return ob.transpose(1, 0, 2, 3).reshape(bn, s_len, hq * dh)

def chunk_gmlp(u, v, w_s, b_s, g_v):
    bn, length, _ = u.shape
    u = jax.nn.gelu(u)
    v = layer_norm(jax.nn.gelu(v), g_v)
    v = v.reshape(bn, length // A_CHUNK, A_CHUNK, A_GROUPS, A_GDIM)
    s = jnp.einsum('gij,bnjgc->bnigc', w_s, v) + b_s.T[None, None, :, :, None]
    return u * s.reshape(bn, length, A_WIDTH)

def neighbourhood_attention(q, k, v, k_ctx, v_ctx, rpb):
    bn, s_len, nh, dh = q.shape
    rows = s_len // GRID_W
    kr = min(NA_ROWS, rows)
    ncb = GRID_W // NA_QCB
    qcol = np.arange(GRID_W).reshape(ncb, NA_QCB)
    kstart = np.clip(np.arange(ncb) * NA_QCB - NA_COLS // 2, 0, GRID_W - NA_KCB)
    kcol = kstart[:, None] + np.arange(NA_KCB)
    c0 = np.clip(qcol - NA_COLS // 2, 0, GRID_W - NA_COLS)
    kc3 = kcol[:, None, :]
    in_win = (kc3 >= c0[..., None]) & (kc3 < c0[..., None] + NA_COLS)
    dc_idx = np.clip(kc3 - qcol[..., None], -(NA_COLS - 1), NA_COLS - 1) + NA_COLS - 1
    mask = in_win[:, :, None, :]
    qg = q.reshape(bn, rows, ncb, NA_QCB, nh, dh)
    kgc = k.reshape(bn, rows, GRID_W, nh, dh)[:, :, kcol]
    vgc = v.reshape(bn, rows, GRID_W, nh, dh)[:, :, kcol]
    scale = dh ** -0.5
    s_ctx_all = None
    n_loc = kr * NA_KCB

    def row_block(r):
        r0 = jnp.clip(r - kr // 2, 0, rows - kr)
        q_r = lax.dynamic_index_in_dim(qg, r, axis=1, keepdims=False)
        k_r = lax.dynamic_slice_in_dim(kgc, r0, kr, axis=1)
        v_r = lax.dynamic_slice_in_dim(vgc, r0, kr, axis=1)
        s_loc = jnp.einsum('bnqhd,brnkhd->bhnqrk', q_r, k_r).astype(jnp.float32) * scale
        dr_idx = r0 + jnp.arange(kr) - r + NA_ROWS - 1
        bias = rpb[:, dr_idx][:, :, dc_idx].transpose(0, 2, 3, 1, 4)
        s_loc = jnp.where(mask, s_loc + bias.astype(jnp.float32)[None], NEG_INF)
        s_ctx = jnp.einsum('bnqhd,bchd->bhnqc', q_r, k_ctx).astype(jnp.float32) * scale
        s = jnp.concatenate([s_loc.reshape(bn, nh, ncb, NA_QCB, n_loc), s_ctx], axis=-1)
        p = jax.nn.softmax(s, axis=-1).astype(v.dtype)
        p_loc = p[..., :n_loc].reshape(bn, nh, ncb, NA_QCB, kr, NA_KCB)
        o = jnp.einsum('bhnqrk,brnkhd->bnqhd', p_loc, v_r)
        return o + jnp.einsum('bhnqc,bchd->bnqhd', p[..., n_loc:], v_ctx)

    o = lax.map(row_block, jnp.arange(rows))
    return o.transpose(1, 0, 2, 3, 4, 5).reshape(bn, s_len, nh * dh)

def even_mixer(xm, cm, w_in, w_s, b_s, g_v, rpb, w_out, with_ctx):
    splits = [A_WIDTH, 2 * A_WIDTH, 2 * A_WIDTH + B_WIDTH, 2 * A_WIDTH + 2 * B_WIDTH]

    def proj(t):
        u, va, q, k, vb = jnp.split(t @ w_in, splits, axis=-1)
        hd = lambda z: z.reshape(*z.shape[:-1], B_HEADS, B_HDIM)
        return u, va, hd(q), hd(k), hd(vb)

    u, va, q, k, vb = proj(xm)
    uc, vac, qc, kc, vbc = proj(cm)
    y_a = chunk_gmlp(u, va, w_s, b_s, g_v)
    y_b = neighbourhood_attention(q, k, vb, kc, vbc, rpb)
    y = jnp.concatenate([y_a, y_b], axis=-1) @ w_out
    yc = None
    if with_ctx:
        yc_a = chunk_gmlp(uc, vac, w_s, b_s, g_v)
        yc_b = gqa_attend(qc, kc, vbc)
        yc = jnp.concatenate([yc_a, yc_b], axis=-1) @ w_out
    return y, yc

def odd_mixer(xm, cm, w_qkv, q_g, k_g, w_out, cos, sin, with_ctx):
    splits = [C_HEADS * C_HDIM, (C_HEADS + C_KV_HEADS) * C_HDIM]

    def proj(t):
        q, k, v = jnp.split(t @ w_qkv, splits, axis=-1)
        q = rms_norm(q.reshape(*q.shape[:-1], C_HEADS, C_HDIM), q_g)
        k = rms_norm(k.reshape(*k.shape[:-1], C_KV_HEADS, C_HDIM), k_g)
        return q, k, v.reshape(*v.shape[:-1], C_KV_HEADS, C_HDIM)

    q, k, v = proj(xm)
    qc, kc, vc = proj(cm)
    q = apply_rope(q, cos, sin)
    k = apply_rope(k, cos, sin)
    y = gqa_blocked(q, k, v, kc, vc) @ w_out
    yc = gqa_attend(qc, kc, vc) @ w_out if with_ctx else None
    return y, yc

def conv_ffn(x, w_up, conv_w, conv_b, w_down):
    h = x @ w_up
    h = lax.conv_general_dilated(h, conv_w[:, None, :], window_strides=(1,),
                                 padding=((CONV_W // 2, CONV_W // 2),),
                                 dimension_numbers=('NWC', 'WIO', 'NWC'),
                                 feature_group_count=h.shape[-1]) + conv_b
    a, g = jnp.split(h, 2, axis=-1)
    return (jax.nn.silu(g) * a) @ w_down

def first_inputs(seed: int = 0) -> dict:
    key = jax.random.key(seed)
    ks = jax.random.split(key, 24)
    nrm = lambda k, shape, s: jax.random.normal(k, shape, jnp.float32) * s
    return {
        "x": nrm(ks[0], (BATCH, SEQ, D_MODEL), 1.0),
        "c": nrm(ks[1], (BATCH, D_MODEL), 1.0),
        "ctx": nrm(ks[2], (BATCH, CTX_LEN, D_MODEL), 1.0),
        "c_ctx": nrm(ks[3], (D_MODEL,), 1.0),
        "w_ada": nrm(ks[4], (DEPTH, D_MODEL, 6 * D_MODEL), 0.5 * D_MODEL ** -0.5),
        "b_ada": nrm(ks[5], (DEPTH, 6 * D_MODEL), 0.02),
        "norm_g": 1.0 + nrm(ks[6], (DEPTH, 4, D_MODEL), 0.05),
        "w_in_ab": nrm(ks[7], (N_EVEN, D_MODEL, IN_AB), D_MODEL ** -0.5),
        "a_w_s": nrm(ks[8], (N_EVEN, A_GROUPS, A_CHUNK, A_CHUNK), A_CHUNK ** -0.5),
        "a_b_s": 1.0 + nrm(ks[9], (N_EVEN, A_GROUPS, A_CHUNK), 0.1),
        "a_v_g": 1.0 + nrm(ks[10], (N_EVEN, A_WIDTH), 0.05),
        "b_rpb": nrm(ks[11], (N_EVEN, B_HEADS, 2 * NA_ROWS - 1, 2 * NA_COLS - 1), 0.5),
        "w_out_ab": nrm(ks[12], (N_EVEN, MIX_WIDTH, D_MODEL), MIX_WIDTH ** -0.5),
        "w_qkv_c": nrm(ks[13], (N_ODD, D_MODEL, IN_C), D_MODEL ** -0.5),
        "c_q_g": 1.0 + nrm(ks[14], (N_ODD, C_HDIM), 0.05),
        "c_k_g": 1.0 + nrm(ks[15], (N_ODD, C_HDIM), 0.05),
        "w_out_c": nrm(ks[16], (N_ODD, C_HEADS * C_HDIM, D_MODEL), (C_HEADS * C_HDIM) ** -0.5),
        "w_up": nrm(ks[17], (DEPTH, D_MODEL, 2 * D_FF), D_MODEL ** -0.5),
        "conv_w": nrm(ks[18], (DEPTH, CONV_W, 2 * D_FF), CONV_W ** -0.5),
        "conv_b": nrm(ks[19], (DEPTH, 2 * D_FF), 0.02),
        "w_down": nrm(ks[20], (DEPTH, D_FF, D_MODEL), D_FF ** -0.5),
    }

def first_block(x, c, ctx, c_ctx, w_ada, b_ada, norm_g, w_in_ab, a_w_s, a_b_s, a_v_g, b_rpb,
              w_out_ab, w_qkv_c, c_q_g, c_k_g, w_out_c, w_up, conv_w, conv_b, w_down):
    cos, sin = axial_rope(x.shape[1], C_HDIM)
    h, hc = x, ctx
    for layer in range(DEPTH):
        with_ctx = layer < DEPTH - 1
        sh_m, sc_m, gt_m, sh_f, sc_f, gt_f = ada_chunks(c, w_ada[layer], b_ada[layer])
        csh_m, csc_m, cgt_m, csh_f, csc_f, cgt_f = ada_chunks(c_ctx, w_ada[layer], b_ada[layer])
        g_pre_m, g_post_m, g_pre_f, g_post_f = norm_g[layer]
        xm = modulate(h, g_pre_m, sh_m, sc_m)
        cm = modulate(hc, g_pre_m, csh_m, csc_m)
        if layer % 2 == 0:
            e = layer // 2
            y, yc = even_mixer(xm, cm, w_in_ab[e], a_w_s[e], a_b_s[e], a_v_g[e], b_rpb[e],
                               w_out_ab[e], with_ctx)
        else:
            o = layer // 2
            y, yc = odd_mixer(xm, cm, w_qkv_c[o], c_q_g[o], c_k_g[o], w_out_c[o], cos, sin, with_ctx)
        h = h + gt_m * rms_norm(y, g_post_m)
        f = conv_ffn(modulate(h, g_pre_f, sh_f, sc_f), w_up[layer], conv_w[layer], conv_b[layer], w_down[layer])
        h = h + gt_f * rms_norm(f, g_post_f)
        if with_ctx:
            hc = hc + cgt_m * rms_norm(yc, g_post_m)
            fc = conv_ffn(modulate(hc, g_pre_f, csh_f, csc_f), w_up[layer], conv_w[layer], conv_b[layer], w_down[layer])
            hc = hc + cgt_f * rms_norm(fc, g_post_f)
    return h


HEAD_DIM = 64
MLA_HEADS = 6
MLA_NOPE = 64
MLA_ROPE = 32
MLA_V = 64
MLA_QK = MLA_NOPE + MLA_ROPE
Q_LORA = 256
KV_LORA = 128
SWA_HEADS = 6
SWA_KV_HEADS = 2
SWA_GROUP = SWA_HEADS // SWA_KV_HEADS
WINDOW = 128
SB_HEADS = 4
BLOCK = 128
NUM_BUCKETS = 32
MAX_DISTANCE = 128

MLA_WIDTH = MLA_HEADS * MLA_V
SWA_WIDTH = SWA_HEADS * HEAD_DIM
SB_WIDTH = SB_HEADS * HEAD_DIM
D_MIX = MLA_WIDTH + SWA_WIDTH + SB_WIDTH
IN_SIZES = (Q_LORA, KV_LORA, MLA_ROPE,
            SWA_HEADS * HEAD_DIM, SWA_KV_HEADS * HEAD_DIM, SWA_KV_HEADS * HEAD_DIM,
            3 * SB_HEADS * HEAD_DIM)
D_IN = Q_LORA + KV_LORA + MLA_ROPE + (SWA_HEADS + 2 * SWA_KV_HEADS) * HEAD_DIM + 3 * SB_HEADS * HEAD_DIM


def _split_cols(x, sizes):
    offs = np.cumsum(np.array(sizes))[:-1].tolist()
    return jnp.split(x, offs, axis=-1)

def rms_norm_2(x, g):
    xf = x.astype(jnp.float32)
    y = xf * lax.rsqrt(jnp.mean(xf * xf, axis=-1, keepdims=True) + EPS)
    return (y * g.astype(jnp.float32)).astype(x.dtype)

def modulate_2(x, g, shift, scale):
    return rms_norm_2(x, g) * (1.0 + scale[:, None, :]) + shift[:, None, :]

def rope(x, pos):
    half = x.shape[-1] // 2
    freqs = ROPE_THETA ** (-jnp.arange(half, dtype=jnp.float32) / half)
    ang = pos.astype(jnp.float32)[:, :, None, None] * freqs
    cos, sin = jnp.cos(ang), jnp.sin(ang)
    xf = x.astype(jnp.float32)
    x1, x2 = xf[..., :half], xf[..., half:]
    return jnp.concatenate([x1 * cos - x2 * sin, x2 * cos + x1 * sin], axis=-1).astype(x.dtype)

def t5_bucket(rel):
    n = jnp.maximum(rel, 0)
    max_exact = NUM_BUCKETS // 2
    nf = jnp.maximum(n, 1).astype(jnp.float32)
    large = max_exact + (jnp.log(nf / max_exact) / math.log(MAX_DISTANCE / max_exact)
                         * (NUM_BUCKETS - max_exact)).astype(jnp.int32)
    large = jnp.minimum(large, NUM_BUCKETS - 1)
    return jnp.where(n < max_exact, n, large)

def swiglu(h, w_gu, w_down):
    g, u = jnp.split(h @ w_gu, 2, axis=-1)
    return (jax.nn.silu(g) * u) @ w_down

def mla_attention(q, k, v):
    B, S, H, Dq = q.shape
    nb = S // BLOCK
    qb = q.reshape(B, nb, BLOCK, H, Dq).transpose(1, 0, 2, 3, 4)
    key_idx = jnp.arange(S)
    scale = Dq ** -0.5

    def one_block(args):
        i, qi = args
        s = jnp.einsum('bqhd,bkhd->bhqk', qi, k).astype(jnp.float32) * scale
        q_idx = i * BLOCK + jnp.arange(BLOCK)
        mask = key_idx[None, :] <= q_idx[:, None]
        p = jax.nn.softmax(jnp.where(mask, s, -jnp.inf), axis=-1)
        return jnp.einsum('bhqk,bkhd->bqhd', p.astype(v.dtype), v)

    out = lax.map(one_block, (jnp.arange(nb), qb))
    return out.transpose(1, 0, 2, 3, 4).reshape(B, S, H * v.shape[-1])

def swa_attention(q, k, v, pos, sinks, rel_table):
    B, S, Hq, D = q.shape
    nb = S // WINDOW

    def band(x):
        xb = x.reshape((B, nb, WINDOW) + x.shape[2:])
        prev = jnp.concatenate([jnp.zeros_like(xb[:, :1]), xb[:, :-1]], axis=1)
        return jnp.concatenate([prev, xb], axis=2)

    kb, vb = band(k), band(v)
    qb = q.reshape(B, nb, WINDOW, SWA_KV_HEADS, SWA_GROUP, D)
    s = jnp.einsum('bnqkgd,bnskd->bnkgqs', qb, kb).astype(jnp.float32) * (D ** -0.5)
    rel = pos.reshape(B, nb, WINDOW)[..., :, None] - band(pos)[..., None, :]
    bias = rel_table[t5_bucket(rel)].astype(jnp.float32)
    bias = bias.reshape(B, nb, WINDOW, 2 * WINDOW, SWA_KV_HEADS, SWA_GROUP).transpose(0, 1, 4, 5, 2, 3)
    q_in = jnp.arange(WINDOW)[:, None] + WINDOW
    k_in = jnp.arange(2 * WINDOW)[None, :]
    d = q_in - k_in
    in_win = (d >= 0) & (d < WINDOW)
    not_pad = (jnp.arange(nb)[:, None, None] > 0) | (k_in[None] >= WINDOW)
    mask = (in_win[None] & not_pad)[None, :, None, None]
    s = jnp.where(mask, s + bias, -jnp.inf)
    sink = sinks.astype(jnp.float32).reshape(SWA_KV_HEADS, SWA_GROUP)[None, None, :, :, None, None]
    m = jnp.maximum(jnp.max(s, axis=-1, keepdims=True), sink)
    p = jnp.exp(s - m)
    p = p / (jnp.sum(p, axis=-1, keepdims=True) + jnp.exp(sink - m))
    o = jnp.einsum('bnkgqs,bnskd->bnqkgd', p.astype(v.dtype), vb)
    return o.reshape(B, S, Hq * D)

def stick_breaking_attention(q, k, v):
    B, S, H, D = q.shape
    nb = S // BLOCK
    qb = q.reshape(B, nb, BLOCK, H, D).transpose(1, 0, 2, 3, 4)
    key_idx = jnp.arange(S)
    scale = D ** -0.5

    def one_block(args):
        i, qi = args
        z = jnp.einsum('bqhd,bkhd->bhqk', qi, k).astype(jnp.float32) * scale
        q_idx = i * BLOCK + jnp.arange(BLOCK)
        mask = key_idx[None, :] < q_idx[:, None]
        log_not = jnp.where(mask, jax.nn.log_sigmoid(-z), 0.0)
        after = lax.cumsum(log_not, axis=3, reverse=True) - log_not
        a = jnp.where(mask, jnp.exp(jax.nn.log_sigmoid(z) + after), 0.0)
        return jnp.einsum('bhqk,bkhd->bqhd', a.astype(v.dtype), v)

    out = lax.map(one_block, (jnp.arange(nb), qb))
    return out.transpose(1, 0, 2, 3, 4).reshape(B, S, H * D)

def second_inputs(seed: int = 0) -> dict:
    key = jax.random.key(seed)
    ks = jax.random.split(key, 24)
    f32 = jnp.float32

    def nrm(k, shape, scale):
        return jax.random.normal(k, shape, f32) * scale

    def gain(k, shape):
        return 1.0 + 0.1 * jax.random.normal(k, shape, f32)

    x = jax.random.normal(ks[0], (BATCH, SEQ, D_MODEL), f32)
    c = jax.random.normal(ks[1], (BATCH, D_MODEL), f32)
    offset = jax.random.randint(ks[2], (BATCH, 1), 0, 4096, dtype=jnp.int32)
    positions = offset + jnp.arange(SEQ, dtype=jnp.int32)[None, :]
    return {
        "x": x,
        "c": c,
        "positions": positions,
        "rel_bias": nrm(ks[3], (NUM_BUCKETS, SWA_HEADS), 0.5),
        "norm_g": gain(ks[4], (DEPTH, 3, D_MODEL)),
        "w_mod": nrm(ks[5], (DEPTH, D_MODEL, 9 * D_MODEL), 0.5 * D_MODEL ** -0.5),
        "b_mod": nrm(ks[6], (DEPTH, 9 * D_MODEL), 0.02),
        "w_ffn1_gu": nrm(ks[7], (DEPTH, D_MODEL, 2 * D_FF), D_MODEL ** -0.5),
        "w_ffn1_down": nrm(ks[8], (DEPTH, D_FF, D_MODEL), D_FF ** -0.5),
        "w_in": nrm(ks[9], (DEPTH, D_MODEL, D_IN), D_MODEL ** -0.5),
        "q_a_norm": gain(ks[10], (DEPTH, Q_LORA)),
        "kv_a_norm": gain(ks[11], (DEPTH, KV_LORA)),
        "w_uq": nrm(ks[12], (DEPTH, Q_LORA, MLA_HEADS * MLA_QK), Q_LORA ** -0.5),
        "w_ukv": nrm(ks[13], (DEPTH, KV_LORA, MLA_HEADS * (MLA_NOPE + MLA_V)), KV_LORA ** -0.5),
        "mla_q_norm": gain(ks[14], (DEPTH, MLA_QK)),
        "mla_k_norm": gain(ks[15], (DEPTH, MLA_QK)),
        "swa_q_norm": gain(ks[16], (DEPTH, HEAD_DIM)),
        "swa_k_norm": gain(ks[17], (DEPTH, HEAD_DIM)),
        "sinks": nrm(ks[18], (DEPTH, SWA_HEADS), 0.5),
        "out_norm": gain(ks[19], (DEPTH, D_MIX)),
        "w_out": nrm(ks[20], (DEPTH, D_MIX, D_MODEL), D_MIX ** -0.5),
        "w_ffn2_gu": nrm(ks[21], (DEPTH, D_MODEL, 2 * D_FF), D_MODEL ** -0.5),
        "w_ffn2_down": nrm(ks[22], (DEPTH, D_FF, D_MODEL), D_FF ** -0.5),
    }

def second_block(x, c, positions, rel_bias, norm_g, w_mod, b_mod, w_ffn1_gu, w_ffn1_down,
              w_in, q_a_norm, kv_a_norm, w_uq, w_ukv, mla_q_norm, mla_k_norm,
              swa_q_norm, swa_k_norm, sinks, out_norm, w_out, w_ffn2_gu, w_ffn2_down):
    B, S, _ = x.shape
    cond = jax.nn.silu(c)
    for l in range(DEPTH):
        mod = cond @ w_mod[l] + b_mod[l]
        sh1, sc1, g1, sh2, sc2, g2, sh3, sc3, g3 = jnp.split(mod, 9, axis=-1)

        h = modulate_2(x, norm_g[l, 0], sh1, sc1)
        x = x + 0.5 * g1[:, None, :] * swiglu(h, w_ffn1_gu[l], w_ffn1_down[l])

        h = modulate_2(x, norm_g[l, 1], sh2, sc2)
        proj = h @ w_in[l]
        c_q, c_kv, k_pe, q_s, k_s, v_s, qkv_sb = _split_cols(proj, IN_SIZES)

        qa = (rms_norm_2(c_q, q_a_norm[l]) @ w_uq[l]).reshape(B, S, MLA_HEADS, MLA_QK)
        qa = rms_norm_2(qa, mla_q_norm[l])
        qa = jnp.concatenate([qa[..., :MLA_NOPE], rope(qa[..., MLA_NOPE:], positions)], axis=-1)
        kv = (rms_norm_2(c_kv, kv_a_norm[l]) @ w_ukv[l]).reshape(B, S, MLA_HEADS, MLA_NOPE + MLA_V)
        k_nope, va = kv[..., :MLA_NOPE], kv[..., MLA_NOPE:]
        k_pe_h = jnp.broadcast_to(k_pe[:, :, None, :], (B, S, MLA_HEADS, MLA_ROPE))
        ka = rms_norm_2(jnp.concatenate([k_nope, k_pe_h], axis=-1), mla_k_norm[l])
        ka = jnp.concatenate([ka[..., :MLA_NOPE], rope(ka[..., MLA_NOPE:], positions)], axis=-1)
        o_a = mla_attention(qa, ka, va)

        qb = rms_norm_2(q_s.reshape(B, S, SWA_HEADS, HEAD_DIM), swa_q_norm[l])
        kb = rms_norm_2(k_s.reshape(B, S, SWA_KV_HEADS, HEAD_DIM), swa_k_norm[l])
        vb = v_s.reshape(B, S, SWA_KV_HEADS, HEAD_DIM)
        o_b = swa_attention(qb, kb, vb, positions, sinks[l], rel_bias)

        qc, kc, vc = jnp.split(qkv_sb.reshape(B, S, 3, SB_HEADS, HEAD_DIM), 3, axis=2)
        o_c = stick_breaking_attention(qc[:, :, 0], kc[:, :, 0], vc[:, :, 0])

        on = out_norm[l]
        mix = jnp.concatenate([
            rms_norm_2(o_a, on[:MLA_WIDTH]),
            rms_norm_2(o_b, on[MLA_WIDTH:MLA_WIDTH + SWA_WIDTH]),
            rms_norm_2(o_c, on[MLA_WIDTH + SWA_WIDTH:]),
        ], axis=-1)
        x = x + g2[:, None, :] * (mix @ w_out[l])

        h = modulate_2(x, norm_g[l, 2], sh3, sc3)
        x = x + 0.5 * g3[:, None, :] * swiglu(h, w_ffn2_gu[l], w_ffn2_down[l])
    return x


def setup_inputs(seed=0):
    out = dict(first_inputs(seed))
    for name, value in second_inputs(seed + 1).items():
        if name != "x":
            out[name + "_2"] = value
    return out


def reference(
    x, c, ctx, c_ctx, w_ada, b_ada, norm_g, w_in_ab, a_w_s, a_b_s, a_v_g, b_rpb, w_out_ab,
    w_qkv_c, c_q_g, c_k_g, w_out_c, w_up, conv_w, conv_b, w_down, c_2, positions_2, rel_bias_2,
    norm_g_2, w_mod_2, b_mod_2, w_ffn1_gu_2, w_ffn1_down_2, w_in_2, q_a_norm_2, kv_a_norm_2,
    w_uq_2, w_ukv_2, mla_q_norm_2, mla_k_norm_2, swa_q_norm_2, swa_k_norm_2, sinks_2,
    out_norm_2, w_out_2, w_ffn2_gu_2, w_ffn2_down_2,
):
    x = first_block(
        x, c, ctx, c_ctx, w_ada, b_ada, norm_g, w_in_ab, a_w_s, a_b_s, a_v_g, b_rpb, w_out_ab,
        w_qkv_c, c_q_g, c_k_g, w_out_c, w_up, conv_w, conv_b, w_down,
    )
    return second_block(
        x, c_2, positions_2, rel_bias_2, norm_g_2, w_mod_2, b_mod_2, w_ffn1_gu_2, w_ffn1_down_2,
        w_in_2, q_a_norm_2, kv_a_norm_2, w_uq_2, w_ukv_2, mla_q_norm_2, mla_k_norm_2,
        swa_q_norm_2, swa_k_norm_2, sinks_2, out_norm_2, w_out_2, w_ffn2_gu_2, w_ffn2_down_2,
    )


_drawn_inputs = setup_inputs


def setup_inputs(seed=0):
    import zlib

    import numpy as np

    out = dict(_drawn_inputs(seed))
    spreads = {}
    factors = {'a_b_s': 2.946,
     'a_v_g': 5.291,
     'b_rpb': 5.953,
     'c_q_g': 8.0,
     'c_k_g': 8.0,
     'conv_b': 5.393,
     'q_a_norm_2': 8.0,
     'mla_q_norm_2': 8.0,
     'mla_k_norm_2': 8.0,
     'swa_q_norm_2': 7.894,
     'swa_k_norm_2': 8.0,
     'sinks_2': 200.0,
     'rel_bias_2': 2.862}
    for name, (base, spread) in spreads.items():
        noise = np.random.default_rng([zlib.crc32(name.encode()), seed]).standard_normal(out[name].shape)
        drawn = base * np.exp(spread * noise) if base else spread * noise
        out[name] = __import__('jax').numpy.asarray(drawn.astype(out[name].dtype))
    for name, factor in factors.items():
        out[name] = (out[name] * factor).astype(out[name].dtype)
    return out
```

```python
import concourse.bass as bass
from concourse import mybir
import numpy as np
from collections import deque
import math

F32 = mybir.dt.float32
F32R = mybir.dt.float32r
BF16 = mybir.dt.bfloat16
I32 = mybir.dt.int32
ACT = mybir.ActivationFunctionType
ALU = mybir.AluOpType
AX = mybir.AxisListType

EPS = 1e-6
KC = 8
NX = 512
NC = 256
FC = 22
DOWN = (8, 7, 7)


class Line:

    def __init__(self, sem):
        self.ops, self.sem, self.count, self.passed = [], sem, 0, {}

    def wait(self, *tickets):
        for t in tickets:
            if t is None:
                continue
            if isinstance(t, list):
                self.wait(*t)
                continue
            sem, value = t
            if self.passed.get(sem.name, 0) < value:
                self.passed[sem.name] = value
                self.ops.append(lambda e, s=sem, v=value: e.wait_ge(s, v))

    def put(self, fn):
        self.ops.append(fn)

    def run(self, fn, *tickets):
        self.wait(*tickets)
        self.count += 1
        self.ops.append(lambda e, s=self.sem: fn(e).then_inc(s, 1))
        return (self.sem, self.count)

    def dma(self, out, in_, slot, *tickets):
        self.wait(*tickets)
        slot[1] += 16
        self.ops.append(lambda e, s=slot[0]: e.dma_start(out, in_).then_inc(s, 16))
        return (slot[0], slot[1])


def weave(main, side, every):
    for n, _ in enumerate(main):
        if side is not None and n % every == every - 1:
            next(side, None)
    if side is not None:
        for _ in side:
            pass


def drain(gen):
    for _ in gen:
        pass


class Prog:

    RR, RH = 4, 4

    def __init__(self, nc, A):
        self.nc, self.A = nc, A
        self.names = 0
        self.base = (nc.sbuf_base + 127) // 128 * 128
        self.PE, self.AC, self.VE, self.GP, self.SP = (
            Line(nc.alloc_semaphore(n)) for n in ("pe_done", "act_done", "dve_done", "pool_done", "sp_done"))
        self.lines = {"tensor": self.PE, "scalar": self.AC, "vector": self.VE, "gpsimd": self.GP, "sync": self.SP}
        self.psum = nc.alloc_psum_tensor("psum", [128, 8 * 512], F32)
        self.bank_free = [None] * 8
        self.plan, self.loaded, self.prepped, self.released = [], 0, 0, {}
        self.fifo, self.w_count, self.w_done = deque(), 0, {}
        self.raw_slots = [[nc.alloc_semaphore(f"raw{i}_in"), 0] for i in range(self.RR)]
        self.raw_ticket = {}

        at = self.at
        self.X = at("X", [128, KC, NX], F32, 0)
        self.C = at("C", [128, KC, NC], F32, 16384)
        self.XM = 24576
        self.XH = at("XH", [128, KC, NX], F32R, self.XM)
        self.XL = at("XL", [128, KC, NX], F32R, self.XM + 16384)
        self.XHf = at("XHf", [128, KC, NX], F32, self.XM)
        self.XLf = at("XLf", [128, KC, NX], F32, self.XM + 16384)
        self.RAW = at("RAW", [128, self.RR, 1024], F32, 57344)
        self.WH = at("WH", [128, self.RH, 1024], F32R, 73728)
        self.WL = at("WL", [128, self.RH, 1024], F32R, 90112)
        self.BIG = 106496
        self.cst = 196608
        const = self.const
        self.ident = const("ident", [128, 128], F32)
        self.ones = const("ones", [128, 8], F32)
        self.half = const("half", [128, 16], F32)
        self.ADA1 = const("ADA1", [128, 2, 2, 48], F32)
        self.ADA2 = const("ADA2", [128, 2, 72], F32)
        self.B1 = const("B1", [128, 2, 48], F32)
        self.B2 = const("B2", [128, 2, 72], F32)
        self.NG1 = const("NG1", [128, 2, 4, 8], F32)
        self.NG2 = const("NG2", [128, 2, 3, 8], F32)
        self.DER1 = const("DER1", [128, 2, 4, 2, 8], F32)
        self.DER2 = const("DER2", [128, 2, 6, 8], F32)
        self.CW = const("CW", [128, 4, 44], F32)
        self.CC = const("CC", [128, 8, 2], F32)
        self.CCS = const("CCS", [128, 8, 2], F32)
        self.NM, self.RS, self.RC = (const(n, [128, 4, 8], F32) for n in ("NM", "RS", "RC"))
        self.BI = const("BI2", [128, 2], F32)
        self.MS = const("MS", [128, 16], F32)
        self.RSQ = const("RSQ", [128, 16], F32)
        self.crow_off = self.cst
        self.crow = const("crow", [128, 2, 1024], F32)
        self.junk = const("junk", [128, 1024], BF16)
        self.t_ada1, self.t_ada2, self.t_der1, self.t_der2 = {}, {}, {}, {}
        self.rsq_free = self.ms_free = self.t_rb = self.t_junk = None

    def at(self, name, shape, dtype, off):
        return self.nc.alloc_sbuf_tensor_at(name, shape, dtype, offset=self.base + off)

    def const(self, name, shape, dtype):
        n = 1
        for s in shape[1:]:
            n *= s
        n *= 2 if dtype == BF16 else 4
        t = self.at(name, shape, dtype, self.cst)
        self.cst += (n + 31) // 32 * 32
        assert self.base + self.cst <= self.nc.sbuf_usable_end
        return t

    def slot(self, name):
        return [self.nc.alloc_semaphore(name), 0]

    def bank(self, b, lo=0, hi=512):
        return self.psum[:, b * 512 + lo:b * 512 + hi]

    def act(self, out, in_, func, *tickets, **kw):
        return self.AC.run(lambda e: e.activation(out, in_, func, **kw), *tickets)

    def tt(self, out, a, b, op, *tickets):
        return self.VE.run(lambda e: e.tensor_tensor(out, a, b, op), *tickets)

    def ts(self, out, a, s1, s2, op0, op1, *tickets):
        return self.VE.run(lambda e: e.tensor_scalar(out, a, s1, s2, op0, op1), *tickets)

    def stt(self, out, a, s, b, op0, op1, *tickets):
        return self.VE.run(lambda e: e.scalar_tensor_tensor(out, a, s, b, op0, op1), *tickets)

    def t_last_act(self):
        return (self.AC.sem, self.AC.count)

    def t_last_dve(self):
        return (self.VE.sem, self.VE.count)

    def mm(self, out, lhsT, rhs, start, tick=False):
        fn = lambda e: e.matmul(out, lhsT, rhs, start=start, stop=True, skip_group_check=True)
        if tick:
            return self.PE.run(fn)
        self.PE.put(fn)

    def tr(self, out, in_, tick=False, ident=None):
        idt = self.ident[:, :] if ident is None else ident
        fn = lambda e: e.transpose(out, in_, idt)
        if tick:
            return self.PE.run(fn)
        self.PE.put(fn)

    def load_next(self):
        i = self.loaded
        if i >= len(self.plan):
            return
        kind, ap, n = self.plan[i][:3]
        self.loaded += 1
        s = i % self.RR
        self.raw_ticket[i] = self.SP.dma(self.RAW[:, s, :n], ap, self.raw_slots[s],
                                         self.released.get(i - self.RR))

    def process_next(self):
        i = self.prepped
        self.prepped += 1
        kind, ap, n, fn = self.plan[i]
        s = i % self.RR
        raw = self.RAW[:, s, :n]
        if kind == "W":
            w = self.w_count
            self.w_count += 1
            h = w % self.RH
            hi, lo = self.WH[:, h, :n], self.WL[:, h, :n]
            free = self.w_done.get(w - self.RH)
            t_hi = self.act(hi, raw, ACT.Copy, self.raw_ticket[i], free)
            t_lo = self.tt(lo, raw, hi.bitcast(F32), ALU.subtract, t_hi, self.raw_ticket[i], free)
            self.fifo.append((w, hi, lo, t_hi, t_lo))
            self.released[i] = t_lo
        else:
            self.released[i] = fn(raw, self.raw_ticket[i])
        self.load_next()

    def ahead(self):
        while self.prepped < len(self.plan):
            if self.plan[self.prepped][0] == "P":
                return
            if self.plan[self.prepped][0] == "W":
                w = self.w_count
                if w >= self.RH and (w - self.RH) not in self.w_done:
                    return
            self.process_next()

    def weights(self):
        while not self.fifo:
            assert self.plan[self.prepped][0] != "P"
            w = self.w_count
            assert w < self.RH or (w - self.RH) in self.w_done
            self.process_next()
        return self.fifo.popleft()

    def gemm(self, tiles, units, xh, xl, xt, n, evac, banks, lead=0, pre=None):
        i, turn = 0, 0
        while i < tiles:
            g = lead if i == 0 and lead else 1
            bs = [banks[(turn + j) % len(banks)] for j in range(g)]
            turn += g
            if g > 1:
                us = [self.weights() for _ in range(g)]
                self.ahead()
                for b in bs:
                    self.PE.wait(self.bank_free[b])
                for k in range(units[0]):
                    self.PE.wait(*xt(k))
                    for j in range(g):
                        w, hi, lo, t_hi, t_lo = us[j]
                        last = k == units[0] - 1
                        o = self.bank(bs[j], 0, n)
                        self.PE.wait(t_hi)
                        self.mm(o, hi[:, k * 128:k * 128 + 128], xh(k), k == 0)
                        yield
                        self.mm(o, hi[:, k * 128:k * 128 + 128], xl(k), False)
                        yield
                        self.PE.wait(t_lo)
                        t = self.mm(o, lo[:, k * 128:k * 128 + 128], xh(k), False, last)
                        if last:
                            self.w_done[w] = t
                            self.ahead()
                            self.bank_free[bs[j]] = evac(i + j, bs[j], t)
                        yield
            else:
                b = bs[0]
                self.PE.wait(self.bank_free[b])
                o = self.bank(b, 0, n)
                k0 = 0
                for u, cnt in enumerate(units):
                    w, hi, lo, t_hi, t_lo = self.weights()
                    self.ahead()
                    self.PE.wait(t_hi)
                    for k in range(cnt):
                        self.PE.wait(*xt(k0 + k))
                        self.mm(o, hi[:, k * 128:k * 128 + 128], xh(k0 + k), k0 + k == 0)
                        yield
                        self.mm(o, hi[:, k * 128:k * 128 + 128], xl(k0 + k), False)
                        yield
                    self.PE.wait(t_lo)
                    for k in range(cnt):
                        t = self.mm(o, lo[:, k * 128:k * 128 + 128], xh(k0 + k), False, k == cnt - 1)
                        yield
                    self.w_done[w] = t
                    k0 += cnt
                    self.ahead()
                self.bank_free[b] = evac(i, b, t)
            i += g

    def gemm_t(self, units, cols, xh, xl, xt, toks, evac, banks):
        k0 = 0
        for t in range(toks):
            self.PE.wait(self.bank_free[banks[t]])
        for u, cnt in enumerate(units):
            w, hi, lo, t_hi, t_lo = self.weights()
            self.ahead()
            last = u == len(units) - 1
            for part in range(2):
                self.PE.wait(t_lo if part else t_hi)
                for t in range(toks):
                    o = self.bank(banks[t], 0, cols)
                    for k in range(cnt):
                        kk = k0 + k
                        self.PE.wait(*xt(kk))
                        cs = slice(k * cols, k * cols + cols)
                        ts = slice(t * 128, t * 128 + 128)
                        end = part == 1 and k == cnt - 1
                        if part == 0:
                            self.mm(o, xh(kk)[:, ts], hi[:, cs], kk == 0)
                            yield
                            self.mm(o, xl(kk)[:, ts], hi[:, cs], False)
                        else:
                            tk = self.mm(o, xh(kk)[:, ts], lo[:, cs], False, end)
                        yield
                    if last and part == 1:
                        if t == toks - 1:
                            self.w_done[w] = tk
                            self.ahead()
                        self.bank_free[banks[t]] = evac(t, banks[t], tk)
            if not last:
                self.w_done[w] = tk
                self.ahead()
            k0 += cnt

    def ssq_part(self, sq, n, first, small, *tickets):
        self.PE.wait(*tickets)
        nt = n // 128
        for j in range(nt):
            tk = self.mm(self.bank(small, j, j + 1), sq[:, j * 128:j * 128 + 128], self.ones[:, 0:1],
                         first and j == 0, j == nt - 1)
        return tk

    def rinv(self, tk, n, dim, rb, small):
        nt = n // 128
        t = self.ts(self.MS[:, :nt], self.bank(small, 0, nt), 1.0 / dim, EPS, ALU.mult, ALU.add, tk, self.ms_free)
        self.bank_free[small] = t
        t = self.pow(self.RSQ[:, :nt], self.MS[:, :nt], t, self.rsq_free)
        self.ms_free = t
        for _ in range(4):
            yield
        self.PE.wait(t, self.bank_free[rb])
        for j in range(nt):
            tk = self.mm(self.bank(rb, j * 128, j * 128 + 128),
                         self.RSQ[:, j:j + 1].broadcast_to([128, 128]), self.ident[:, :], j == 0, j == nt - 1)
        self.rsq_free = self.t_rb = tk
        yield

    def pow(self, out, in_, *tickets):
        h = self.half[:, :in_.shape[1]]
        return self.GP.run(lambda e: e.tensor_tensor(out, in_, h, ALU.pow), *tickets)

    def apply(self, src, t_src, n, g1, sh, hi, lo, lof, rb, war, out):
        r = self.bank(rb, 0, n)
        t_rb = self.t_rb
        pend = None
        for k in range(KC + 1):
            if k < KC:
                t = self.stt(lof(k), src(k), g1(k), r, ALU.mult, ALU.mult, t_rb, t_src(k), war)
                if k == KC - 1:
                    self.bank_free[rb] = t
                t_hi = self.act(hi(k), lof(k), ACT.Identity, t, war, bias=sh(k))
            if pend:
                j, tj = pend
                t_lo = self.stt(lo(j), lof(j), sh(j), hi(j).bitcast(F32), ALU.add, ALU.subtract, tj)
                out[j] = (tj, t_lo)
            pend = (k, t_hi) if k < KC else None
            yield

    def squares(self, src, t_src, n, sq, acc, tk, war=None):
        t = self.act(sq, src, ACT.Square, t_src, war)
        if tk is None:
            return t
        return self.tt(acc, acc, sq, ALU.add, t, tk)

    def residual(self, y, t_y, n, gp, x, t_x, sq, small, rb, out, t_g):
        r, t_rb = self.bank(rb, 0, n), self.t_rb
        free = [None] * len(sq)
        self.PE.wait(self.bank_free[small])
        for m in range(KC):
            t = self.stt(y(m), y(m), gp(m), r, ALU.mult, ALU.mult, t_rb, t_y[m], t_g)
            if m == KC - 1:
                self.bank_free[rb] = t
            out[m] = t = self.tt(x(m), x(m), y(m), ALU.add, t, t_x[m])
            i = m % len(sq)
            t = self.act(sq[i], x(m), ACT.Square, t, free[i])
            free[i] = self.t_ssq = self.ssq_part(sq[i], n, m == 0, small, t)
            yield

    def attend(self, units, fill=None, step=0):
        n = len(units)
        for i in range(n + 2):
            if i < n:
                units[i][0]()
                units[i][1]()
            yield
            if fill is not None:
                for _ in range(step):
                    next(fill, None)
            if 1 <= i <= n:
                units[i - 1][2]()
            if i >= 2:
                units[i - 2][3]()
            yield

    def ttr(self, out, a, b, scale, init, op0, op1, acc, *tickets):
        return self.VE.run(lambda e: e.tensor_tensor_reduce(out, a, b, scale, init, op0, op1, acc), *tickets)

    def reduce_max(self, out, in_, negate, *tickets):
        return self.VE.run(lambda e: e.tensor_reduce(out, in_, AX.X, ALU.max, negate=negate), *tickets)

    def recip(self, out, in_, *tickets):
        return self.VE.run(lambda e: e.reciprocal(out, in_), *tickets)

    def copy(self, out, in_, *tickets):
        return self.VE.run(lambda e: e.tensor_copy(out, in_), *tickets)

    def product(self, out, a, b, first, tick=False):
        self.mm(out, a[0], b[0], first)
        self.mm(out, a[0], b[1], False)
        return self.mm(out, a[1], b[0], False, tick)

    def ada1_item(self, layer, col, both):
        def fn(raw, t_raw):
            for w in range(2 if both else 1):
                t = self.ttr(self.junk[:, :], raw, self.crow[:, w, :], 1.0, self.B1[:, layer, col:col + 1],
                             ALU.mult, ALU.add, self.ADA1[:, layer, w, col:col + 1], t_raw, self.t_crow, self.t_junk)
                self.t_junk = t
                self.t_ada1[layer, w, col // 8] = t
            if (layer, col) == (1, 47):
                t2 = self.SP.dma(self.crow[:, 0, :], self.A["crow2"], self.slot("crow2_in"), t)
                self.t_crow2 = self.act(self.crow[:, 0, :], self.crow[:, 0, :], ACT.Silu, t2)
            return t
        return fn

    def ada2_item(self, layer, col):
        def fn(raw, t_raw):
            t = self.ttr(self.junk[:, :], raw, self.crow[:, 0, :], 1.0, self.B2[:, layer, col:col + 1],
                         ALU.mult, ALU.add, self.ADA2[:, layer, col:col + 1], t_raw, self.t_crow2, self.t_junk)
            self.t_junk = t
            self.t_ada2[layer, col // 8] = t
            return t
        return fn


def start(p):
    A = p.A
    ld = p.slot("const_in")
    lc = p.slot("ccol_in")
    t = p.AC.dma(p.CC[:, :, :], A["ccol"], lc)
    t_cc = t
    A_small = [("ident", p.ident[:, :]), ("b1", p.B1[:, :, :]), ("ng1", p.NG1[:, :, :, :])]
    for name, dst in A_small:
        t_small = p.AC.dma(dst, A[name], ld)
    lx = [p.slot(f"x{i}_in") for i in range(2)]
    lcx = [p.slot(f"ctx{i}_in") for i in range(2)]
    t_c0, t_x0 = [None] * 8, [None] * 8
    for i in range(2):
        t = p.AC.dma(p.C[:, 4 * i:4 * i + 4, :], A["ctxT"][:, 4 * i:4 * i + 4, :], lcx[i])
        t_c0[4 * i:4 * i + 4] = [t] * 4
    for i in range(2):
        t = p.AC.dma(p.X[:, 4 * i:4 * i + 4, :], A["xT"][:, 4 * i:4 * i + 4, :], lx[i])
        t_x0[4 * i:4 * i + 4] = [t] * 4
    lr = p.slot("crow_in")
    p.t_crow_in = p.AC.dma(p.crow[:, :, :], A["crow"], lr)
    l2 = p.slot("const2_in")
    for name, dst in [("b2", p.B2[:, :, :]), ("ng2", p.NG2[:, :, :, :]), ("cw0", p.CW[:, :, :])]:
        t = p.AC.dma(dst, A[name], l2)
    p.t_const2 = t
    p.cw_slot = l2
    p.GP.run(lambda e: e.memset(p.ones[:, :], 1.0))
    t_fill = p.GP.run(lambda e: e.memset(p.half[:, :], -0.5))
    p.t_const = [t_small, t_fill]
    for line in (p.PE, p.VE):
        line.wait(*p.t_const)
    t_ccs = p.act(p.CCS[:, :, :], p.CC[:, :, :], ACT.Silu, t_cc)

    for i in range(p.RR):
        p.load_next()
    CMH, CML, CMLf = (p.at(n, [128, KC, NC], d, p.BIG + o) for n, d, o in (
        ("CMH", F32R, 24576), ("CML", F32R, 32768), ("CMLf", F32, 32768)))
    p.CMH, p.CML = CMH, CML
    SQx = p.at("SQx0", [128, 8, NX], F32, p.BIG + 40960)
    SQc = p.at("SQc0", [128, 8, NC], F32, p.BIG + 57344)

    t_der = [None] * 8

    def rows(k):
        bk = 4 + k % 2
        p.k_rows = k
        p.PE.wait(p.bank_free[bk], t_ccs)
        p.process_next()
        p.process_next()
        t1 = p.ts(p.ADA1[:, 0, :, 8 + k], p.bank(bk, 0, 2), p.B1[:, 0, 8 + k:9 + k], None, ALU.add, ALU.bypass, p.t_rows)
        t2 = p.ts(p.ADA1[:, 0, :, k], p.bank(bk, 2, 4), p.B1[:, 0, k:k + 1], None, ALU.add, ALU.bypass)
        p.bank_free[bk] = t2
        t_der[k] = p.ts(p.DER1[:, 0, 0, :, k], p.ADA1[:, 0, :, 8 + k], 1.0, p.NG1[:, 0, 0, k:k + 1],
                        ALU.add, ALU.mult, t1)
        p.t_ada1[0, 0, 0] = p.t_ada1[0, 1, 0] = t2

    rows(0)
    for i in range(3):
        p.process_next()
    for n, src, t0, sq, small, rb, keep in ((NC, p.C, t_c0, SQc, 6, 3, "c"), (NX, p.X, t_x0, SQx, 6, 7, "x")):
        p.PE.wait(p.bank_free[small])
        for k in range(KC):
            t = p.act(sq[:, k, :], src[:, k, :], ACT.Square, t0[k])
            tk = p.ssq_part(sq[:, k, :], n, k == 0, small, t)
        drain(p.rinv(tk, n, 1024, rb, small))
        if keep == "c":
            t_rbc = p.t_rb
            rows(1)
    t_rbx = p.t_rb
    p.xt, p.ct = [None] * 8, [None] * 8
    gens = []
    for src, t0, n, w, h, l, lf, rb, t_rb, out in (
            (p.C, t_c0, NC, 1, CMH, CML, CMLf, 3, t_rbc, p.ct),
            (p.X, t_x0, NX, 0, p.XH, p.XL, p.XLf, 7, t_rbx, p.xt)):
        p.t_rb = t_rb
        g = p.apply(lambda k, src=src: src[:, k, :], lambda k, t0=t0: [t0[k], t_der[k]], n,
                    lambda k, w=w: p.DER1[:, 0, 0, w, k:k + 1], lambda k, w=w: p.ADA1[:, 0, w, k:k + 1],
                    lambda k, h=h: h[:, k, :], lambda k, l=l: l[:, k, :], lambda k, lf=lf: lf[:, k, :],
                    rb, None, out)
        next(g)
        gens.append(g)
    p.t_start_gens = gens
    return t_c0, t_x0, rows


def row_item(p, k, which):
    def fn(raw, t_raw):
        p.PE.wait(t_raw)
        for kk in range(KC):
            t = p.mm(p.bank(4 + k % 2, 2 * which, 2 * which + 2), raw[:, kk * 128:kk * 128 + 128],
                     p.CCS[:, kk, :], kk == 0, kk == KC - 1)
        p.t_rows = t
        return t
    return fn


def split(p, f, hi, lo, *tickets):
    t_hi = p.act(hi, f, ACT.Copy, *tickets)
    return [t_hi, p.tt(lo, f, hi.bitcast(F32), ALU.subtract, t_hi)]


def even_mixer(p, t_c0, t_x0, rows):
    A, at, B = p.A, p.at, p.BIG
    f32 = lambda n, s, o: at(n, s, F32, B + o)
    f32r = lambda n, s, o: at(n, s, F32R, B + o)
    U, Uc = f32("U", [128, 4, NX], 0), f32("Uc", [128, 4, NC], 8192)
    VA, VAc = f32("VA", [128, 4, 512], 12288), f32("VAc", [128, 2, 512], 20480)
    Q = [(f32r("QH", [128, 4, NX], 24576), f32r("QL", [128, 4, NX], 32768), f32("QLf", [128, 4, NX], 32768)),
         (f32r("KH", [128, 4, NX], 40960), f32r("KL", [128, 4, NX], 49152), f32("KLf", [128, 4, NX], 49152))]
    Qc = [(f32r("QHc", [128, 4, NC], 57344), f32r("QLc", [128, 4, NC], 61440), f32("QLcf", [128, 4, NC], 61440)),
          (f32r("KHc", [128, 4, NC], 65536), f32r("KLc", [128, 4, NC], 69632), f32("KLcf", [128, 4, NC], 69632))]
    VF, VTc = f32("VF", [128, 4, NX], 73728), f32("VTc", [128, 2, 512], 81920)
    WS, BS = f32("WS", [128, 4, 128], 86016), f32("BS", [128, 4, 128], 88064)
    MV = p.const("MV", [128, 6, 2], F32)
    ST = p.const("ST", [128, 6, 6], F32)
    LNR = p.const("LNR", [128, 2, 8], F32)
    GV = p.const("GV", [128, 4], F32)
    lw = p.slot("gmlp_in")
    for name, dst in (("w_s", WS[:, :, :]), ("b_s", BS[:, :, :]), ("gv", GV[:, :])):
        t_gmlp = p.AC.dma(dst, A[name], lw)

    t_q, t_k, t_qc, t_kc = [[None] * 4 for _ in range(4)]
    t_u, t_uc, t_vf, t_vtc = [None] * 4, [None] * 4, [None] * 4, [None] * 2
    t_mv = [None] * 6

    def gelu(dst, t_dst, n):
        def evac(i, b, t):
            t_dst[i] = p.act(dst[:, i, :], p.bank(b, 0, n), ACT.Gelu_apprx_tanh, t)
            return t_dst[i]
        return evac

    def gate(dst, base):
        def evac(i, b, t):
            o, st = dst[:, i, :], ST[:, base + i, :]
            t = p.act(o, p.bank(b), ACT.Gelu_apprx_tanh, t)
            tb = p.VE.run(lambda e: e.bn_stats(st, o), t)
            mv = MV[:, base + i, :]
            t_mv[base + i] = p.VE.run(lambda e: e.bn_aggr(mv, st), tb)
            return t
        return evac

    def parts(dst, t_dst, n, scale, order):
        H, L, Lf = dst

        def evac(i, b, t):
            o = Lf[:, i, :]
            if order:
                o = o.rearrange("p (g r c) -> p r g c", g=8, r=8)
            t1 = p.act(o, p.bank(b, 0, n), ACT.Copy, t, scale=scale)
            t_dst[i] = split(p, Lf[:, i, :], H[:, i, :], L[:, i, :], t1)
            return t1
        return evac

    def plain(dst, t_dst, n, order):
        def evac(i, b, t):
            o = dst[:, i, :]
            if order:
                o = o.rearrange("p (g r c) -> p r g c", g=8, r=8)
            t_dst[i] = p.act(o, p.bank(b, 0, n), ACT.Copy, t)
            return t_dst[i]
        return evac

    xt = lambda k: p.xt[k]
    ct = lambda k: p.ct[k]
    ch, cl = lambda k: p.CMH[:, k, :], lambda k: p.CML[:, k, :]
    xh, xl = lambda k: p.XH[:, k, :], lambda k: p.XL[:, k, :]

    g = p.gemm(4, [8], ch, cl, ct, NC, gelu(Uc, t_uc, NC), [0, 1, 2], lead=3)
    for k in range(1, KC):
        if k > 1:
            rows(k)
        for a in p.t_start_gens:
            next(a)
        for _ in range(9):
            next(g)
    for a in p.t_start_gens:
        drain(a)
    drain(g)
    TB = [0, 1, 2, 3]
    drain(p.gemm_t([2] * 4, 512, ch, cl, ct, 2, gate(VAc, 4), TB))
    drain(p.gemm_t([2] * 4, 512, ch, cl, ct, 2, plain(VTc, t_vtc, 512, False), [2, 3]))
    drain(p.gemm(4, [8], ch, cl, ct, NC, parts(Qc[0], t_qc, NC, 0.125, False), TB))
    drain(p.gemm(4, [8], ch, cl, ct, NC, parts(Qc[1], t_kc, NC, 1.0, False), TB))
    t_cm_read = (p.PE.sem, p.PE.count)

    drain(p.gemm(4, [8], xh, xl, xt, NX, gelu(U, t_u, NX), TB))
    drain(p.gemm_t([2] * 4, 512, xh, xl, xt, 4, gate(VA, 0), TB))
    p.AC.wait(t_cm_read)
    drain(p.gemm(4, [8], xh, xl, xt, NX, plain(VF, t_vf, NX, True), TB))
    drain(p.gemm(4, [8], xh, xl, xt, NX, parts(Q[0], t_q, NX, 0.125, True), TB))
    drain(p.gemm(4, [8], xh, xl, xt, NX, parts(Q[1], t_k, NX, 1.0, True), TB))
    t_xm_read = (p.PE.sem, p.PE.count)

    t = p.ts(LNR[:, 0, 0:6], MV[:, :, 1], EPS, None, ALU.add, ALU.bypass, *t_mv)
    t_r = p.pow(LNR[:, 1, 0:6], LNR[:, 0, 0:6], t)
    t_va = []
    for i in range(6):
        o = VA[:, i, :] if i < 4 else VAc[:, i - 4, :]
        t_va.append(p.ts(o, o, MV[:, i, 0:1], LNR[:, 1, i:i + 1], ALU.subtract, ALU.mult, t_r, t_mv[i]))

    YC0, YC0f = (f32r("YCH0", [128, 4, NC], 0), f32r("YCL0", [128, 4, NC], 4096)), f32("YCL0f", [128, 4, NC], 4096)
    YC1, YC1f = (f32r("YCH1", [128, 4, NC], 57344), f32r("YCL1", [128, 4, NC], 61440)), f32("YCL1f", [128, 4, NC], 61440)
    t_y, t_yc = [None] * 8, [None] * 8
    p.PE.wait(t_gmlp)
    p.VE.wait(t_gmlp)
    for c in range(2):
        nt, n, base = (2, NC, 4) if c else (4, NX, 0)
        u, tu, va = (Uc, t_uc, VAc) if c else (U, t_u, VA)
        for g in range(4):
            b = g if not c else (g + 1) % 4
            p.PE.wait(p.bank_free[b], *t_va[base:base + nt])
            for i in range(nt):
                t = p.mm(p.bank(b, i * 128, i * 128 + 128), va[:, i, g * 128:g * 128 + 128], WS[:, g, :], i == 0, i == nt - 1)
            if c:
                hi, lo, lf = YC0[0][:, g, :], YC0[1][:, g, :], YC0f[:, g, :]
                war = t_x_u
            else:
                hi, lo, lf = p.XH[:, g, :], p.XL[:, g, :], p.XLf[:, g, :]
                war = t_xm_read
            t = p.stt(lf.rearrange("p (t i) -> p t i", i=128),
                      p.bank(b, 0, n).rearrange("p (t i) -> p t i", i=128), GV[:, g:g + 1],
                      BS[:, g, :].unsqueeze(1).broadcast_to([128, nt, 128]), ALU.mult, ALU.add, t, war)
            p.bank_free[b] = t
            t = p.tt(lf, lf, u[:, g, :], ALU.mult, t, tu[g])
            if not c:
                t_x_u = t
            (t_yc if c else t_y)[g] = split(p, lf, hi, lo, t, war)
    t_gmlp_done = [p.t_last_act(), p.t_last_dve()]

    VTa, VTb = at("VTa", [128, 4, 512], F32, p.XM + 8192), at("VTb", [128, 3, 512], F32, p.XM + 24576)
    t_vt = [None] * 7
    for s in range(7):
        b = s % 4
        p.PE.wait(p.bank_free[b], t_xm_read)
        for j in range(4):
            p.PE.wait(t_vf[j])
            t = p.tr(p.bank(b, j * 128, j * 128 + 128), VF[:, j, 64 * s:64 * s + 128], j == 3)
        o = VTa[:, s, :] if s < 4 else VTb[:, s - 4, :]
        if s % 2:
            t_vt[s] = p.act(o, p.bank(b), ACT.Copy, t, t_xm_read)
        else:
            t_vt[s] = p.copy(o, p.bank(b), t, t_xm_read)
        p.bank_free[b] = t_vt[s]
    t_vf_read = t
    vt = lambda s: VTa[:, s, :] if s < 4 else VTb[:, s - 4, :]

    Yx, Yc = f32("Yx", [128, 4, 512], 8192), f32("Yc", [128, 2, 512], 16384)
    PR = f32("PR", [128, 2, 512], 20480)
    PTR = f32("PTR", [128, 2, 512], 73728)
    BI = [f32("BI0", [128, 4, 256], 77824), f32("BI1", [128, 4, 256], 86016)]
    NM, RS, RC = p.NM, p.RS, p.RC
    lb = [p.slot("rpb0_in"), p.slot("rpb1_in")]
    t_bias = {}

    def load_bias(h, *tickets):
        t_bias[h] = p.SP.dma(BI[h % 2][:, :, :], A["rpb"][h], lb[h % 2], *tickets)

    load_bias(0, t_vf_read)
    load_bias(1, t_gmlp_done, t_xm_read)

    SB, PB, YB = [0, 1, 2], [3, 4], [5, 6]
    p_free, pt_free = [t_gmlp_done] * 2, [t_vf_read] * 2
    count = [0]
    pair_done = {}
    win = [(0, 2, 0), (1, 3, 1), (3, 5, 3), (4, 6, 4)]

    def unit(kind, h, b):
        i, off = h // 2, 64 * (h % 2)
        ps = slice(off, off + 64)
        n = count[0]
        count[0] += 1
        sb, pb, slot = SB[n % 3], PB[n % 2], n % 2
        pair = (kind, i)
        par = (i + (4 if kind == "c" else 0)) % 2
        yb = YB[par]
        Pr, Pt = PR[:, slot, :], PTR[:, slot, :]
        s = {}

        def score():
            p.PE.wait(p.bank_free[sb])
            if kind == "x":
                p.PE.wait(*t_q[i], *t_k[i], *t_kc[i])
                g0 = win[b][2]
                q = [t[ps, i, 128 * b:128 * b + 128] for t in Q[0][:2]]
                p.product(p.bank(sb, 0, 256), q, [t[ps, i, 64 * g0:64 * g0 + 256] for t in Q[1][:2]], True)
                s["t"] = p.product(p.bank(sb, 256, 512), q, [t[ps, i, :] for t in Qc[1][:2]], False, True)
            else:
                p.PE.wait(*t_qc[i], *t_kc[i])
                for m in range(2):
                    s["t"] = p.product(p.bank(sb, 256 * m, 256 * m + 256), [t[ps, i, 128 * m:128 * m + 128] for t in Qc[0][:2]],
                                       [t[ps, i, :] for t in Qc[1][:2]], m == 0, m == 1)

        def soft():
            free = p_free[slot]
            if kind == "x":
                c = (h % 2) * 4 + b
                nm, rs = NM[:, par, c:c + 1], RS[:, par, c:c + 1]
                m0 = NM[:, 2 + par, c:c + 1]
                t0 = p.reduce_max(m0, p.bank(sb, 256, 512), False, s["t"])
                loc = p.bank(sb, 0, 256)
                t1 = p.ttr(loc, loc, BI[h % 2][:, b, :], 1.0, m0, ALU.add, ALU.max, nm, t0, t_bias[h])
                s["bias_read"] = t1
                t1 = p.ts(nm, nm, -1.0, None, ALU.mult, ALU.bypass, t1)
                s["e"] = p.act(Pr, p.bank(sb), ACT.Exp, t1, free, bias=nm, accum_out=rs)
                p.bank_free[sb] = s["e"]
                if b == 3 and h + 2 < 8:
                    load_bias(h + 2, s["bias_read"])
            else:
                c = (h % 2) * 2
                t1 = p.reduce_max(NM[:, par, c:c + 2], p.bank(sb).rearrange("p (m k) -> p m k", m=2), True, s["t"])
                for m in range(2):
                    s["e"] = p.act(Pr[:, 256 * m:256 * m + 256], p.bank(sb, 256 * m, 256 * m + 256), ACT.Exp, t1, free,
                                   bias=NM[:, par, c + m:c + m + 1], accum_out=RS[:, par, c + m:c + m + 1])
                p.bank_free[sb] = s["e"]

        def turn():
            p.PE.wait(p.bank_free[pb], s["e"])
            for j in range(4):
                t = p.tr(p.bank(pb, 128 * j, 128 * j + 128), Pr[:, 128 * j:128 * j + 128], j == 3)
            p_free[slot] = t
            if n % 2:
                t = p.act(Pt, p.bank(pb), ACT.Copy, t, pt_free[slot])
            else:
                t = p.copy(Pt, p.bank(pb), t, pt_free[slot])
            s["pt"] = p.bank_free[pb] = t

        def value():
            first = pair not in pair_done
            if first:
                pair_done[pair] = 0
                p.PE.wait(p.bank_free[yb])
            pair_done[pair] += 1
            p.PE.wait(s["pt"])
            hs = slice(64 * h, 64 * h + 64)
            if kind == "x":
                w0, w1, _ = win[b]
                p.PE.wait(t_vt[w0], t_vt[w1], *t_vtc)
                o = p.bank(yb, 128 * b + off, 128 * b + off + 64)
                vals = [vt(w0)[:, hs], vt(w1)[:, hs], VTc[:, 0, hs], VTc[:, 1, hs]]
                for j in range(4):
                    t = p.mm(o, Pt[:, 128 * j:128 * j + 128], vals[j], first and j == 0, j == 3)
                last = pair_done[pair] == 8
            else:
                for m in range(2):
                    o = p.bank(yb, 128 * m + off, 128 * m + off + 64)
                    for j in range(2):
                        t = p.mm(o, Pt[:, 256 * m + 128 * j:256 * m + 128 * j + 128], VTc[:, j, hs],
                                 first and m == 0 and j == 0, m == 1 and j == 1)
                last = pair_done[pair] == 2
            pt_free[slot] = t
            if last:
                k = 8 if kind == "x" else 4
                t1 = p.recip(RC[:, par, :k], RS[:, par, :k], s["e"])
                nt = k // 2
                Y = Yx if kind == "x" else Yc
                t_att[kind, i] = p.tt(Y[:, 0:nt, 128 * i:128 * i + 128].rearrange("p b (h d) -> p b h d", h=2),
                                      p.bank(yb, 0, 128 * nt).rearrange("p (b h d) -> p b h d", b=nt, h=2),
                                      RC[:, par, :k].rearrange("p (h b) -> p b h", h=2).unsqueeze(3).broadcast_to([128, nt, 2, 64]),
                                      ALU.mult, t, t1, t_gmlp_done)
                p.bank_free[yb] = t_att[kind, i]

        return score, soft, turn, value

    t_att = {}
    units = [unit("x", h, b) for h in range(8) for b in range(4)] + [unit("c", h, 0) for h in range(8)]
    drain(p.attend(units))
    t_pv = (p.PE.sem, p.PE.count)

    for kind, Y in (("x", Yx), ("c", Yc)):
        nt = 4 if kind == "x" else 2
        for j in range(4):
            b = [3, 4][j % 2]
            p.PE.wait(p.bank_free[b], t_att[kind, j])
            for m in range(nt):
                t = p.tr(p.bank(b, 128 * m, 128 * m + 128), Y[:, m, 128 * j:128 * j + 128], m == nt - 1)
            if kind == "x":
                src = p.bank(b).rearrange("p (g r c) -> p g r c", g=8, r=8)
                v = lambda T: T[:, 4 + j, :].rearrange("p (r g c) -> p g r c", g=8, r=8)
                hi, hif, lo = v(p.XH), v(p.XH).bitcast(F32), v(p.XL)
                t1 = p.act(hi, src, ACT.Copy, t, t_pv)
                t_y[4 + j] = [t1, p.tt(lo, src, hif, ALU.subtract, t1)]
                p.bank_free[b] = t_y[4 + j][1]
            else:
                hi, lo = YC1[0][:, j, :], YC1[1][:, j, :]
                t1 = p.act(hi, p.bank(b, 0, NC), ACT.Copy, t, t_pv)
                t_yc[4 + j] = [t1, p.tt(lo, p.bank(b, 0, NC), hi.bitcast(F32), ALU.subtract, t1)]
                p.bank_free[b] = t_yc[4 + j][1]
    p.t_y, p.t_yc = t_y, t_yc
    p.YC = lambda k, w: (YC0[w][:, k, :] if k < 4 else YC1[w][:, k - 4, :])


def derive1(p, layer, kind, streams):
    if (layer, kind) in p.t_der1:
        return p.t_der1[layer, kind]
    chunk = (1, 2, 4, 5)[kind]
    deps = [p.t_ada1[layer, w, chunk] for w in range(streams)]
    out = p.DER1[:, layer, kind, 0:streams, :]
    ada = p.ADA1[:, layer, 0:streams, chunk * 8:chunk * 8 + 8]
    g = p.NG1[:, layer, kind, :].unsqueeze(1).broadcast_to([128, streams, 8])
    t = p.t_der1[layer, kind] = p.stt(out, ada, 1.0 if kind % 2 == 0 else 0.0, g, ALU.add, ALU.mult, *deps)
    return t


class Stream:

    def __init__(self, p, w, n, res, t_res, small, rb):
        self.p, self.w, self.n, self.res, self.small, self.rb = p, w, n, res, small, rb
        self.t_res = list(t_res)
        self.war = None

    def places(self, y, sq):
        self.y, self.sq = y, sq
        self.t_y, self.sq_free, self.t_sum = [None] * KC, [None] * sq.shape[1], None

    def evac(self, i, b, t):
        p, n = self.p, self.n
        src = p.bank(b, 0, n)
        self.t_y[i] = p.act(self.y[:, i, :], src, ACT.Copy, t, self.war)
        if i == 0:
            t2 = self.t_sum = p.act(self.sq[:, 0, :], src, ACT.Square, t, self.war)
        else:
            s = 1 + (i - 1) % (self.sq.shape[1] - 1)
            t2 = p.act(self.sq[:, s, :], src, ACT.Square, t, self.war, self.sq_free[s])
            self.t_sum = self.sq_free[s] = p.tt(self.sq[:, 0, :], self.sq[:, 0, :], self.sq[:, s, :], ALU.add, t2, self.t_sum)
        return t2

    def post(self, layer, kind):
        p, n = self.p, self.n
        p.PE.wait(p.bank_free[self.small])
        tk = p.ssq_part(self.sq[:, 0, :], n, True, self.small, self.t_sum)
        yield
        yield from p.rinv(tk, n, 1024, self.rb, self.small)
        m = self.sq.shape[1]
        t_g = derive1(p, layer, kind, 2 if layer == 0 else 1)
        yield from p.residual(lambda k: self.y[:, k, :], self.t_y, n, lambda k: p.DER1[:, layer, kind, self.w, k:k + 1],
                              lambda k: self.res[:, k, :], self.t_res, [self.sq[:, 1 + s, :] for s in range(m - 1)],
                              self.small, self.rb, self.t_res, t_g)
        yield from p.rinv(p.t_ssq, n, 1024, self.rb, self.small)
        self.t_rb = p.t_rb

    def pre(self, g1, sh, hi, lo, lof, t_g, out, war=None):
        p = self.p
        p.t_rb = self.t_rb
        t_res = self.t_res
        yield from p.apply(lambda k: self.res[:, k, :], lambda k: [t_res[k], t_g], self.n, g1, sh,
                           lambda k: hi[:, k, :], lambda k: lo[:, k, :], lambda k: lof[:, k, :], self.rb, war, out)

    def pre1(self, layer, kind, hi, lo, lof, out, war=None):
        p = self.p
        t_g = derive1(p, layer, kind, 2 if layer == 0 or (self.w and kind == 0) or kind == 0 else 1)
        c = 0 if kind == 0 else 3
        yield from self.pre(lambda k: p.DER1[:, layer, kind, self.w, k:k + 1],
                            lambda k: p.ADA1[:, layer, self.w, 8 * c + k:8 * c + k + 1], hi, lo, lof,
                            [t_g, p.t_ada1[layer, self.w, c]], out, war)


def chain(*gens):
    for g in gens:
        yield from g


def up_conv(p, s, xh, xl, xt, HH, HL, HHf, HLf, war, lead):
    n, cw = s.n, p.CW
    t_h = [None] * FC
    late = deque()
    t_a = {}

    def conv(dst, i, b, t):
        src = p.bank(b, 0, n)
        t1 = p.act(dst, src, ACT.Identity, t, war, p.t_cw, scale=cw[:, 1, i:i + 1], bias=cw[:, 3, i:i + 1])
        t2 = p.stt(dst[:, 1:n], src[:, 0:n - 1], cw[:, 0, i:i + 1], dst[:, 1:n], ALU.mult, ALU.add, t1, p.t_cw)
        return p.stt(dst[:, 0:n - 1], src[:, 1:n], cw[:, 2, i:i + 1], dst[:, 0:n - 1], ALU.mult, ALU.add, t2)

    def silu(j, t):
        f = HLf[:, j, :]
        t = p.act(f, f, ACT.Silu, t)
        t = p.tt(f, f, HHf[:, j, :], ALU.mult, t, t_a[j])
        late.append(lambda: high(j, t))

    def high(j, t):
        t = p.act(HH[:, j, :], HLf[:, j, :], ACT.Copy, t)
        late.append(lambda: low(j, t))

    def low(j, t):
        t_h[j] = (t, p.tt(HL[:, j, :], HLf[:, j, :], HHf_of(j), ALU.subtract, t))

    def HHf_of(j):
        return HH[:, j, :].bitcast(F32)

    def evac(i, b, t):
        j = i // 2
        for _ in range(len(late)):
            late.popleft()()
        if i % 2 == 0:
            t_a[j] = t = conv(HHf[:, j, :], i, b, t)
        else:
            t = conv(HLf[:, j, :], i, b, t)
            late.append(lambda: silu(j, t))
        return t

    yield from p.gemm(2 * FC, [8], xh, xl, xt, n, evac, [0, 1, 2, 3], lead=lead)
    while late:
        late.popleft()()
    s.t_h = t_h


def down(p, s, HH, HL, evac):
    yield from p.gemm(KC, DOWN, lambda k: HH[:, k, :], lambda k: HL[:, k, :], lambda k: s.t_h[k], s.n, evac, [0, 1, 2, 3])


class Heads:

    def __init__(self, p, SQ, SW, TAB, SEL, RT, slots, t_tab):
        self.SQ, self.SW, self.TAB, self.SEL, self.RT = SQ, SW, TAB, SEL, RT
        self.slots, self.t_tab, self.turn = slots, t_tab, 0
        self.t_sq = self.t_rt = self.t_ms = self.t_rsq = None
        self.t_sw_free = [None, None]
        self.MS, self.RS = p.MS[:, 8:16], p.RSQ[:, 8:16]


def qk_tile(p, st, raw_dst, hi, lo, b, t, n, gain, rope, turned, rq, small):
    src = p.bank(b, 0, n)
    t_raw = p.act(raw_dst, src, ACT.Copy, t, st.t_tab, scale=gain)
    t_sq = p.act(st.SQ[:, :n], src, ACT.Square, t, st.t_sq)
    p.bank_free[b] = t_sq
    if rope:
        k = st.turn % 2
        st.turn += 1
        for s in range(4):
            o = s ^ 1
            t_sw = p.SP.dma(st.SW[32 * s:32 * s + 32, k, :], raw_dst[32 * o:32 * o + 32, :], st.slots[k], t_raw, st.t_sw_free[k])
    yield
    yield
    nt = n // 128
    p.PE.wait(t_sq, p.bank_free[small], st.t_tab)
    for m in range(nt):
        t = p.mm(p.bank(small, 2 * m, 2 * m + 2), st.SQ[:, 128 * m:128 * m + 128], p.BI[:, :], m == 0, m == nt - 1)
    st.t_sq = t
    c = 2 * nt
    t = p.ts(st.MS[:, :c], p.bank(small, 0, c), 1.0 / 64, EPS, ALU.mult, ALU.add, t, st.t_ms)
    p.bank_free[small] = t
    t = p.pow(st.RS[:, :c], st.MS[:, :c], t, st.t_rsq)
    st.t_ms = t
    yield
    if rope:
        t1 = p.tt(raw_dst, raw_dst, st.TAB[:, 0, :n], ALU.mult, t_raw, t_sw)
        t2 = p.tt(st.SW[:, k, :], st.SW[:, k, :], st.TAB[:, 1, :n], ALU.mult, t_sw)
        t_raw = st.t_sw_free[k] = p.tt(raw_dst, raw_dst, st.SW[:, k, :], ALU.add, t1, t2)
    yield
    if rq is not None:
        t_r = p.ts(rq, st.RS[:, :8], 0.125, None, ALU.mult, ALU.bypass, t)
        st.t_rsq = t_r
        turned.append(split(p, raw_dst, hi, lo, t_raw) + [t_r])
    else:
        p.PE.wait(p.bank_free[small], t)
        for m in range(nt):
            t = p.tr(p.bank(small, 128 * m, 128 * m + 128)[0:2, :], st.RS[:, 2 * m:2 * m + 2], m == nt - 1)
        st.t_rsq = t
        t = p.act(st.RT[0:2, :n], p.bank(small, 0, n)[0:2, :], ACT.Copy, t, st.t_rt)
        p.bank_free[small] = t
        yield
        yield
        p.PE.wait(t, p.bank_free[small])
        st.t_rt = t = p.mm(p.bank(small, 0, n), st.SEL[0:2, :], st.RT[0:2, :n], True, True)
        t = p.tt(raw_dst, raw_dst, p.bank(small, 0, n), ALU.mult, t, t_raw)
        p.bank_free[small] = t
        turned.append(split(p, raw_dst, hi, lo, t))
    yield


def odd_mixer(p, sx, xt, c_chain, CMH, CML, ct):
    A = p.A
    f32 = lambda n, s, o: p.at(n, s, F32, p.BIG + o)
    f32r = lambda n, s, o: p.at(n, s, F32R, p.BIG + o)
    QH, QL, QLf = f32r("Q1H", [128, 8, NX], 0), f32r("Q1L", [128, 8, NX], 16384), f32("Q1Lf", [128, 8, NX], 16384)
    KH, KL, KLf = f32r("K1H", [128, 2, 768], 32768), f32r("K1L", [128, 2, 768], 38912), f32("K1Lf", [128, 2, 768], 38912)
    Y = f32("Y1", [128, 4, 1024], 45056)
    PR, PTR = f32("P1", [128, 2, 768], 61440), f32("PT1", [128, 2, 768], 67584)
    RT = f32("RT1", [128, NX], 61440)
    TAB = f32("TAB1", [128, 2, NX], 73728)
    SW, SQ = f32("SW1", [128, 2, NX], 77824), f32("SQ1", [128, NX], 81920)
    V = f32("V1", [128, 6, 256], 83968)
    G1 = p.const("G1", [128, 2], F32)
    SEL = f32("SEL2", [128, 128], 67584)
    RQ = p.const("RQ", [128, 8, 8], F32)
    lc = p.slot("rope1_in")
    t_prev = (p.PE.sem, p.PE.count)
    for name, dst in (("rope1", TAB[:, :, :]), ("qk_g1", G1[:, :]), ("bi2", p.BI[:, :]), ("sel2", SEL[0:2, :])):
        t_tab = p.SP.dma(dst, A[name], lc, t_prev)
    st = Heads(p, SQ, SW, TAB, SEL, RT, [p.slot("swap0"), p.slot("swap1")], t_tab)

    def plain_v(base, t_v):
        def evac(i, b, t):
            t_v[base + i] = p.act(V[:, base + i, :], p.bank(b, 0, 256), ACT.Copy, t)
            return t_v[base + i]
        return evac

    xh, xl = (lambda k: p.XH[:, k, :]), (lambda k: p.XL[:, k, :])
    ch, cl = (lambda k: CMH[:, k, :]), (lambda k: CML[:, k, :])
    t_v, t_kx, t_kc = [None] * 6, [], []
    got = []

    def keep(i, b, t):
        got.append((b, t))
        return None

    def tiles(count, h, l, tk, n, banks, after):
        for i in range(count):
            yield from p.gemm(1, [8], h, l, tk, n, keep, [banks[i % len(banks)]])
            b, t = got.pop()
            yield from after(i, b, t)

    q_done = []

    def k_after(t_k, off, n, rope):
        return lambda i, b, t: qk_tile(p, st, KLf[:, i, off:off + n], KH[:, i, off:off + n], KL[:, i, off:off + n], b, t,
                                       n, G1[:, 1:2], rope, t_k, None, 3)

    def q_after(i0, small):
        return lambda i, b, t: qk_tile(p, st, QLf[:, i0 + i, :], QH[:, i0 + i, :], QL[:, i0 + i, :], b, t, NX,
                                       G1[:, 0:1], True, q_done, RQ[:, i0 + i, :], small)

    def front():
        yield from p.gemm(1, [8], xh, xl, xt, NX, keep, [0])
        b, t = got.pop()
        yield from k_after(t_kx, 0, NX, True)(0, b, t)
        yield from p.gemm(1, [8], xh, xl, xt, NX, keep, [1])
        b, t = got.pop()
        yield from k_after(t_kx, 0, NX, True)(1, b, t)
        yield from p.gemm_t([4] * 2, 256, xh, xl, xt, 4, plain_v(0, t_v), [0, 1, 2, 3])
        yield from tiles(1, xh, xl, xt, NX, [0], q_after(0, 3))
    weave(front(), c_chain, 6)
    drain(tiles(2, ch, cl, ct, NC, [0, 1], k_after(t_kc, NX, NC, False)))
    drain(p.gemm_t([4] * 2, 256, ch, cl, ct, 2, plain_v(4, t_v), [0, 1]))
    t_cm = (p.PE.sem, p.PE.count)

    NM, RS, RC = p.NM, p.RS, p.RC
    fill = []
    p_free, pt_free = [p.t_last_act()] * 2, [None] * 2
    later = []
    t_out = [None] * 8

    def back(i, t_y):
        p.PE.wait(p.bank_free[4], t_y)
        for m in range(4):
            t = p.tr(p.bank(4, 128 * m, 128 * m + 128), Y[:, m, 128 * i:128 * i + 128], m == 3)
        t1 = p.act(QH[:, i, :], p.bank(4), ACT.Copy, t)
        p.bank_free[4] = t2 = p.tt(QL[:, i, :], p.bank(4), QH[:, i, :].bitcast(F32), ALU.subtract, t1)
        t_out[i] = [t1, t2]

    def unit(n, i, j, m):
        slot, sb, par = n % 2, 2 * (n % 2), i % 2
        ps = slice(64 * j, 64 * j + 64)
        kt = i // 4
        c = 2 * m + j
        Pr, Pt = PR[:, slot, :], PTR[:, slot, :]
        s = {}

        def score():
            while len(q_done) <= i:
                next(fill[0])
            p.PE.wait(p.bank_free[sb], p.bank_free[sb + 1], *q_done[i], *t_kx[kt], *t_kc[kt])
            q = [T[ps, i, 128 * m:128 * m + 128] for T in (QH, QL)]
            p.product(p.bank(sb), q, [T[ps, kt, 0:512] for T in (KH, KL)], True)
            s["t"] = p.product(p.bank(sb + 1, 0, 256), q, [T[ps, kt, 512:768] for T in (KH, KL)], True, True)

        def soft():
            S = p.psum[:, 512 * sb:512 * sb + 768]
            nm = NM[:, par, c:c + 1]
            t = p.reduce_max(nm, S, False, s["t"])
            t = p.ts(nm, nm, RQ[:, i, c:c + 1], -1.0, ALU.mult, ALU.mult, t)
            s["e"] = p.act(Pr, S, ACT.Exp, t, p_free[slot], scale=RQ[:, i, c:c + 1], bias=nm,
                           accum_out=RS[:, par, c:c + 1])
            p.bank_free[sb] = p.bank_free[sb + 1] = s["e"]

        def turn():
            if later and n >= later[0][0]:
                _, a, b = later.pop(0)
                back(a, b)
            p.PE.wait(p.bank_free[4], s["e"])
            for h in range(2):
                p.PE.wait(p.bank_free[4 + h])
                for k in range(3):
                    kk = 3 * h + k
                    t = p.tr(p.bank(4 + h, 128 * k, 128 * k + 128), Pr[:, 128 * kk:128 * kk + 128], k == 2)
                o, src = Pt[:, 384 * h:384 * h + 384], p.bank(4 + h, 0, 384)
                if h == 0:
                    s["p0"] = p.bank_free[4] = p.act(o, src, ACT.Copy, t, pt_free[slot])
                else:
                    s["p1"] = p.bank_free[5] = p.copy(o, src, t, pt_free[slot])
            p_free[slot] = t

        def value():
            first, last = j == 0 and m == 0, j == 1 and m == 3
            if first:
                p.PE.wait(p.bank_free[6], *t_v)
            o = p.bank(6, 128 * m + 64 * j, 128 * m + 64 * j + 64)
            hs = slice(64 * (2 * kt + j), 64 * (2 * kt + j) + 64)
            p.PE.wait(s["p0"])
            for k in range(6):
                if k == 3:
                    p.PE.wait(s["p1"])
                t = p.mm(o, Pt[:, 128 * k:128 * k + 128], V[:, k, hs], first and k == 0, k == 5)
            pt_free[slot] = t
            if last:
                t1 = p.recip(RC[:, par, :], RS[:, par, :], s["e"])
                t2 = p.tt(Y[:, :, 128 * i:128 * i + 128].rearrange("p m (j d) -> p m j d", j=2),
                          p.bank(6).rearrange("p (m j d) -> p m j d", m=4, j=2),
                          RC[:, par, :].rearrange("p (m j) -> p m j", j=2).unsqueeze(3).broadcast_to([128, 4, 2, 64]),
                          ALU.mult, t, t1, t_cm)
                p.bank_free[6] = t2
                later.append((n + 3, i, t2))

        return score, soft, turn, value

    fill.append(tiles(7, xh, xl, xt, NX, [7], q_after(1, 7)))
    drain(p.attend([unit(8 * i + 4 * j + m, i, j, m) for i in range(8) for j in range(2) for m in range(4)],
                   fill[0], 4))
    for _, a, b in later:
        back(a, b)
    return QH, QL, t_out


PI = math.pi
MAGIC = 1.5 * 2.0 ** 23
THRESHOLDS = [k if k < 16 else math.ceil(16 * 2 ** (3 * (k - 16) / 16) - 1e-9) for k in range(1, 32)]


def pieces(x, bits, count):
    out = []
    for _ in range(count):
        e = math.floor(math.log2(x)) - bits + 1
        q = math.floor(x / 2.0 ** e) * 2.0 ** e
        out.append(q)
        x -= q
    return out + [x]


def positions(p, scratch):
    A = p.A
    base, base2 = 16384, p.crow_off + 4096
    t0 = [p.t_last_act(), p.t_last_dve(), (p.PE.sem, p.PE.count)]
    sl = p.slot("pos_in")
    PB = p.at("PB", [128, NX], I32, base)
    AN, NN = p.at("AN", [128, NX], F32, base + 2048), p.at("NN", [128, NX], F32, base + 4096)
    FQ = p.at("FQ", [128, 4], F32, base + 6144)
    p.SP.dma(PB[0:64, :], A["pos_row"], sl, *t0)
    t = p.SP.dma(FQ[0:64, :], A["freq"], sl)
    an, nn, fq = AN[0:64, :], NN[0:64, :], FQ[0:64, :]
    t = p.ts(an, PB[0:64, :], fq[:, 0:1], None, ALU.mult, ALU.bypass, t)
    yield
    for scale, parts in ((4096.0, pieces(2 * PI, 7, 4)), (1.0, pieces(2 * PI, 12, 2))):
        if scale == 1.0:
            t1 = p.ts(nn, an, 1 / (2 * PI), fq[:, 2:3], ALU.mult, ALU.add, t)
            t1 = p.ts(nn, nn, MAGIC, None, ALU.add, ALU.bypass, t1)
        else:
            t1 = p.ts(nn, an, 1 / (2 * PI * scale), MAGIC, ALU.mult, ALU.add, t)
        yield
        t1 = p.ts(nn, nn, MAGIC, None, ALU.subtract, ALU.bypass, t1)
        yield
        for c in parts:
            t1 = t = p.stt(an, nn, -c * scale, an, ALU.mult, ALU.add, t1)
            yield
    t = p.ts(an, an, fq[:, 1:2], 3.1415925, ALU.add, ALU.min, t)
    t = p.ts(an, an, -3.1415925, None, ALU.max, ALU.bypass, t)
    yield
    t = p.act(nn, an, ACT.Sin, t)
    t = p.ts(nn, nn, fq[:, 3:4], None, ALU.mult, ALU.bypass, t)
    so = p.slot("rope_out")
    p.t_rope2 = t_rope = p.SP.dma(scratch["rope"], nn, so, t)
    yield
    PQ = p.at("PQ", [128, 4, 129], I32, base)
    HI, LO = p.at("HI", [128, 4, 129], I32, base + 2080), p.at("LO", [128, 4, 129], I32, base + 4160)
    RH, RL = p.at("RH", [128, 4, 128], F32, base2), p.at("RL", [128, 4, 128], F32, base2 + 2048)
    N = p.at("NREL", [128, 4, 128], F32, base)
    t = p.SP.dma(PQ[:, :, :], A["pos_win"], sl, t_rope, t)
    t1 = p.VE.run(lambda e: e.tensor_scalar(HI[:, :, :], PQ[:, :, :], 16, None, ALU.arith_shift_right), t)
    t2 = p.VE.run(lambda e: e.tensor_scalar(LO[:, :, :], PQ[:, :, :], 65535, None, ALU.bitwise_and), t)
    yield
    t1 = p.tt(RH[:, :, :], HI[:, :, 128:129].broadcast_to([128, 4, 128]), HI[:, :, 0:128], ALU.subtract, t1)
    t2 = p.tt(RL[:, :, :], LO[:, :, 128:129].broadcast_to([128, 4, 128]), LO[:, :, 0:128], ALU.subtract, t2)
    yield
    t_n = p.stt(N[:, :, :], RH[:, :, :], 65536.0, RL[:, :, :], ALU.mult, ALU.add, t1, t2)
    TB, DT = p.at("TB", [128, 32, 6], F32, base2), p.at("DT", [128, 31, 6], F32, base2 + 1024)
    MK = p.at("MASK", [128, 2, 4, 128], BF16, base2 + 2048)
    ACC = p.at("ACC", [128, 3, 4, 128], F32, base + 2048)
    t = p.SP.dma(TB[:, :, :], A["rel_bias"], sl, t_n)
    t_dt = p.tt(DT[:, :, :], TB[:, 1:32, :], TB[:, 0:31, :], ALU.subtract, t)
    yield
    sb = [p.slot(f"bias{i}_out") for i in range(6)]
    t_pre = []
    for h in range(6):
        t_pre.append(p.SP.dma(scratch["bias"][h], A["mask_fill"], sb[h]))
    t_out = [None] * 6
    for half in range(2):
        t_acc = []
        for h in range(3):
            hh = 3 * half + h
            t_acc.append(p.ts(ACC[:, h, :, :], N[:, :, :], 0.0, TB[:, 0, hh:hh + 1], ALU.mult, ALU.add, t_n, t,
                              t_out[hh - 3] if half else None))
        yield
        for b, thr in enumerate(THRESHOLDS):
            m = MK[:, b % 2, :, :]
            t_m = p.ts(m, N[:, :, :], float(thr), None, ALU.is_ge, ALU.bypass, t_n)
            yield
            for h in range(3):
                hh = 3 * half + h
                a = ACC[:, h, :, :]
                t_acc[h] = p.stt(a, m, DT[:, b, hh:hh + 1], a, ALU.mult, ALU.add, t_m, t_dt, t_acc[h])
                yield
        for h in range(3):
            hh = 3 * half + h
            t_out[hh] = p.SP.dma(scratch["skew"][hh], ACC[:, h, :, :], sb[hh], t_acc[h], t_pre[hh])
            yield
    p.t_bias2 = t_out


def derive2(p, layer, kind):
    if (layer, kind) in p.t_der2:
        return p.t_der2[layer, kind]
    chunk = (1, 4, 7, 2, 5, 8)[kind]
    ada = p.ADA2[:, layer, chunk * 8:chunk * 8 + 8]
    out = p.DER2[:, layer, kind, :]
    if kind < 3:
        t = p.stt(out, ada, 1.0, p.NG2[:, layer, kind, :], ALU.add, ALU.mult, p.t_ada2[layer, chunk])
    else:
        t = p.ts(out, ada, 1.0 if kind == 4 else 0.5, None, ALU.mult, ALU.bypass, p.t_ada2[layer, chunk])
    p.t_der2[layer, kind] = t
    return t


class Block2:

    def __init__(self, p, s):
        self.p, self.t_res, self.small, self.rb = p, s.t_res, s.small, s.rb
        self.n = NX

    def norm(self, layer, kind, hi, lo, lof, out, war=None):
        p = self.p
        p.PE.wait(p.bank_free[self.small])
        tk = p.ssq_part(self.sum, NX, True, self.small, self.t_sum)
        yield
        yield from p.rinv(tk, NX, 1024, self.rb, self.small)
        yield from self.modulate(layer, kind, hi, lo, lof, out, war)

    def modulate(self, layer, kind, hi, lo, lof, out, war=None):
        p = self.p
        t_g = derive2(p, layer, kind)
        yield from p.apply(lambda k: p.X[:, k, :], lambda k: [self.t_res[k], t_g], NX,
                           lambda k: p.DER2[:, layer, kind, k:k + 1],
                           lambda k: p.ADA2[:, layer, 24 * kind + k:24 * kind + k + 1],
                           lambda k: hi[:, k, :], lambda k: lo[:, k, :], lambda k: lof[:, k, :], self.rb,
                           [war, p.t_ada2[layer, 3 * kind]] if war else [p.t_ada2[layer, 3 * kind]], out)

    def adder(self, layer, kind, sq, war=None):
        p = self.p
        t_g = derive2(p, layer, kind)
        free = [None] * 8

        def evac(i, b, t):
            x = p.X[:, i, :]
            t = self.t_res[i] = p.stt(x, p.bank(b), p.DER2[:, layer, kind, i:i + 1], x, ALU.mult, ALU.add, t, t_g,
                                      self.t_res[i])
            if sq is None:
                p.SP.dma(p.A["out"][:, i, :], x, p.out_slot, t)
            elif i == 0:
                self.sum = sq[:, 0, :]
                self.t_sum = p.act(self.sum, x, ACT.Square, t, war)
            else:
                m = 1 + (i - 1) % (sq.shape[1] - 1)
                t2 = p.act(sq[:, m, :], x, ACT.Square, t, war, free[m])
                self.t_sum = free[m] = p.tt(self.sum, self.sum, sq[:, m, :], ALU.add, t2, self.t_sum)
            return t
        return evac


def up_glu(p, xh, xl, xt, H, war, lead):
    HH, HL, HHf, HLf = H
    t_h = [None] * FC
    late = deque()
    t_g = {}

    def high(j, t):
        t = p.act(HH[:, j, :], HLf[:, j, :], ACT.Copy, t)
        late.append(lambda: low(j, t))

    def low(j, t):
        t_h[j] = (t, p.tt(HL[:, j, :], HLf[:, j, :], HH[:, j, :].bitcast(F32), ALU.subtract, t))

    def evac(i, b, t):
        j = i // 2
        for _ in range(len(late)):
            late.popleft()()
        if i % 2 == 0:
            t_g[j] = p.act(HLf[:, j, :], p.bank(b), ACT.Silu, t, war)
            return t_g[j]
        t = p.tt(HLf[:, j, :], HLf[:, j, :], p.bank(b), ALU.mult, t, t_g[j])
        late.append(lambda: high(j, t))
        return t

    yield from p.gemm(2 * FC, [8], xh, xl, xt, NX, evac, [0, 1, 2, 3], lead=lead)
    while late:
        late.popleft()()
    p.t_h = t_h


def mixer2(p, r, layer, xh, xl, xt, scratch):
    A = p.A
    L = str(layer)
    f32 = lambda n, s, o: p.at(n + L, s, F32, p.BIG + o)
    f32r = lambda n, s, o: p.at(n + L, s, F32R, p.BIG + o)

    def trio(name, tiles, o, cols=NX):
        return (f32r(name + "H", [128, tiles, cols], o), f32r(name + "L", [128, tiles, cols], o + 4 * tiles * cols),
                f32(name + "f", [128, tiles, cols], o + 4 * tiles * cols))

    CQ, CKV, QS, KS = trio("CQ", 2, 0), trio("CKV", 1, 8192), trio("QS", 3, 12288), trio("KS", 1, 24576)
    V, VA, Y = f32("V2", [128, 4, 384], 28672), f32("VA2", [128, 4, 384], 34816), f32("Y2", [128, 4, 1024], 40960)
    GT, KG, SQK = f32("GT", [128, NX], 57344), f32("KG", [128, 2, NX], 59392), f32("SQK", [128, 2, NX], 63488)
    SQ, PR, PTR = f32("SQ2", [128, NX], 67584), f32("P2", [128, 2, 512], 69632), f32("PT2", [128, 2, 512], 73728)
    MQ = [trio("MQa", 1, 77824), trio("MQb", 1, 81920)]
    cb = 16384 - p.BIG
    MK = [trio("MKa", 1, 86016), trio("MKb", 1, cb + 4096)]
    TK = f32("TK", [128, NX], 69632)
    K2 = f32("K2", [128, 6, 128], cb)
    G2 = f32("G2", [128, 24], cb + 3072)
    RT = f32("RT2", [128, NX], p.crow_off + 4096 - p.BIG)
    smalls = [cb + 3168]

    def small(name, cols):
        t = f32(name, [128, cols], smalls[0])
        smalls[0] += (4 * cols + 31) // 32 * 32
        assert smalls[0] <= cb + 4096
        return t

    RQ, RCQ, MSm, RSm, RQ2, ES, SS = (small(n, c) for n, c in (
        ("RQm", 24), ("RCQ", 8), ("MSm", 8), ("RSm", 8), ("RQ2", 24), ("ES", 16), ("SS", 8)))
    FOLD, TRI, M01, CAUS, ONE, SEL = (K2[:, i, :] for i in range(6))
    prev = [(p.PE.sem, p.PE.count), p.t_last_act(), p.t_last_dve()]
    sc = p.slot("mix_in" + L)
    p.SP.dma(K2[:, :, :], A["k2"], sc, *prev)
    p.SP.dma(G2[:, :], A["g2"][layer], sc)
    p.SP.dma(GT[64:128, :], scratch["rope"], sc, p.t_rope2)
    t_k2 = p.SP.dma(TK[0:64, :], scratch["rope"], sc)
    col = lambda c: G2[:, c:c + 1]

    t_one = p.VE.run(lambda e: e.memset(GT[0:64, :], 1.0), *prev)
    t_gt = p.ts(GT[:, :], GT[:, :], col(0), None, ALU.mult, ALU.bypass, t_one, t_k2)
    t_tk = p.ts(TK[0:64, :], TK[0:64, :], G2[0:64, 2:3], None, ALU.mult, ALU.bypass, t_k2)

    st = Heads(p, SQ, None, None, SEL, RT, None, t_k2)
    got = []

    def keep(i, b, t):
        got.append((b, t))
        return None

    t_cq, t_ckv = [None] * 2, [None]
    sqs = []

    def latent(i, b, t):
        src = p.bank(b)
        dst, gain = (CQ[2][:, i, :], col(3 + i)) if i < 2 else (CKV[2][:, 0, :], col(5))
        t1 = p.act(dst, src, ACT.Copy, t, t_k2, scale=gain)
        sq = (SQ[:, :], PR1[:, :], PTf[:, :])[i]
        sqs.append((sq, p.act(sq, src, ACT.Square, t)))
        if i < 2:
            t_cq[i] = split(p, dst, CQ[0][:, i, :], CQ[1][:, i, :], t1)
        else:
            t_ckv[0] = t1
        return sqs[-1][1]

    PR1, PTf = f32("SQc1", [128, NX], 73728), f32("SQc2", [128, NX], 75776)
    yield from p.gemm(3, [8], xh, xl, xt, NX, latent, [0, 1, 2], lead=3)
    p.PE.wait(p.bank_free[5], sqs[0][1], sqs[1][1])
    for i in range(2):
        for m in range(4):
            t = p.mm(p.bank(5, m, m + 1), sqs[i][0][:, 128 * m:128 * m + 128], p.ones[:, 0:1], i == 0 and m == 0,
                     i == 1 and m == 3)
    st.t_sq = t
    t = p.ts(RCQ[:, 4:8], p.bank(5, 0, 4), 1.0 / 256, EPS, ALU.mult, ALU.add, t)
    p.bank_free[5] = t
    t = p.pow(RCQ[:, 0:4], RCQ[:, 4:8], t)
    t = p.tt(RCQ[:, 4:8], RCQ[:, 0:4], RCQ[:, 0:4], ALU.mult, t)
    t = p.ts(RCQ[:, 4:8], RCQ[:, 4:8], 1.0 / 96, None, ALU.mult, ALU.bypass, t)
    t_rcq = p.ts(RCQ[:, 0:4], RCQ[:, 0:4], 96.0 ** -0.5, None, ALU.mult, ALU.bypass, t)
    p.PE.wait(p.bank_free[5])
    tk = p.ssq_part(sqs[2][0], NX, True, 5, sqs[2][1])

    def latent_kv():
        yield from p.rinv(tk, NX, 128, 6, 5)
        t = p.tt(CKV[2][:, 0, :], CKV[2][:, 0, :], p.bank(6), ALU.mult, p.t_rb, t_ckv[0])
        p.bank_free[6] = t
        t_ckv[:] = split(p, CKV[2][:, 0, :], CKV[0][:, 0, :], CKV[1][:, 0, :], t)
        yield

    t_kr = []

    def kpe(b, t):
        src = p.bank(b)
        for q in range(2):
            t_s = p.act(SQK[64:96, q, :], src[0:32, :], ACT.Square, t)
        t1 = p.tt(TK[0:64, :], src[0:64, :], TK[0:64, :], ALU.mult, t_s, t_tk)
        p.bank_free[b] = t1
        yield
        yield
        p.PE.wait(p.bank_free[6], t1)
        t = p.mm(p.bank(6), FOLD[0:64, :], TK[0:64, :], True, True)
        for q in range(2):
            t1 = p.act(KG[64:128, q, :], p.bank(6)[64:128, :], ACT.Copy, t)
        p.bank_free[6] = t1
        t_kr.extend([t_s, t1])
        yield

    t_v, t_va = [None] * 4, [None] * 4

    def vals(dst, t_dst):
        def evac(i, b, t):
            t_dst[i] = p.act(dst[:, i, :], p.bank(b, 0, 384), ACT.Copy, t)
            return t_dst[i]
        return evac

    def pe_tile():
        w, hi, lo, t_hi, t_lo = p.weights()
        p.ahead()
        p.PE.wait(p.bank_free[3], t_hi)
        o = p.bank(3)[0:64, :]
        for part, wt in ((0, hi), (1, hi), (2, lo)):
            if part == 2:
                p.PE.wait(t_lo)
            for k in range(8):
                p.PE.wait(*xt(k))
                t = p.mm(o, wt[:, 64 * k:64 * k + 64], (xl if part == 1 else xh)(k), part == 0 and k == 0,
                         part == 2 and k == 7)
                yield
        p.w_done[w] = t
        p.ahead()
        got.append((3, t))

    lk = latent_kv()

    def with_side(main, side):
        n = 0
        for _ in main:
            n += 1
            if n % 3 == 2:
                next(side, None)
            yield
        drain(side)

    yield from with_side(pe_tile(), lk)
    b, t = got.pop()
    yield from with_side(p.gemm_t([2] * 4, 384, xh, xl, xt, 4, vals(V, t_v), [0, 1, 2, 4]), kpe(b, t))

    w, hi, lo, t_hi, t_lo = p.weights()
    p.ahead()
    p.PE.wait(t_hi, t_lo, *t_ckv)
    for m in range(4):
        p.PE.wait(p.bank_free[m])
        ck = [T[:, 0, 128 * m:128 * m + 128] for T in CKV[:2]]
        t = p.product(p.bank(m, 0, 384), ck, (hi[:, 0:384], lo[:, 0:384]), True, True)
        if m == 3:
            p.w_done[w] = t
        p.bank_free[m] = vals(VA, t_va)(m, m, t)
        yield
    p.ahead()

    q_ok, k_ok = {}, {}
    s_read = {}
    head_t = {"sq": st.t_sq, "ms": None, "rs": None}

    def head(h):
        slot = h % 2
        mq, mk = MQ[slot], MK[slot]
        assert h < 2 or h - 2 in s_read
        war = s_read.get(h - 2)
        w, hi, lo, t_hi, t_lo = p.weights()
        p.ahead()
        p.PE.wait(p.bank_free[7], t_hi, *t_cq[0], *t_cq[1])
        for k in range(2):
            ws = slice(128 * k, 128 * k + 128)
            p.mm(p.bank(7), hi[:, ws], CQ[0][:, k, :], k == 0)
            yield
            p.mm(p.bank(7), hi[:, ws], CQ[1][:, k, :], False)
            yield
        p.PE.wait(t_lo)
        for k in range(2):
            t_q = p.mm(p.bank(7), lo[:, 128 * k:128 * k + 128], CQ[0][:, k, :], False, k == 1)
        yield
        p.PE.wait(p.bank_free[6], *t_ckv)
        t_k = p.product(p.bank(6)[0:64, :], (hi[:, 256:320], lo[:, 256:320]), (CKV[0][:, 0, :], CKV[1][:, 0, :]), True, True)
        p.w_done[w] = t_k
        p.ahead()
        t_sq = p.act(SQ[0:96, :], p.bank(7)[0:96, :], ACT.Square, t_q, head_t["sq"])
        t_kg = p.act(KG[0:64, slot, :], p.bank(6)[0:64, :], ACT.Copy, t_k, s_kg.get(slot), scale=G2[0:64, 1:2])
        t_sk = p.act(SQK[0:64, slot, :], p.bank(6)[0:64, :], ACT.Square, t_k, s_sqk.get(slot))
        p.bank_free[6] = t_sk
        t_q = p.tt(mq[2][:, 0, :], p.bank(7), GT[:, :], ALU.mult, t_sq, t_gt, war)
        p.bank_free[7] = t_q
        yield
        p.PE.wait(p.bank_free[5], t_sq, t_sk, *t_kr)
        for m in range(4):
            p.mm(p.bank(5, m, m + 1), SQ[0:96, 128 * m:128 * m + 128], p.ones[0:96, 0:1], m == 0)
        for m in range(4):
            t = p.mm(p.bank(5, 4 + m, 5 + m), SQK[0:96, slot, 128 * m:128 * m + 128], p.ones[0:96, 0:1], False, m == 3)
        head_t["sq"] = s_sqk[slot] = t
        q_ok[h] = split(p, mq[2][:, 0, :], mq[0][:, 0, :], mq[1][:, 0, :], t_q, war)
        t1 = p.tt(MSm[:, 0:4], p.bank(5, 0, 4), RCQ[:, 4:8], ALU.mult, t, t_rcq, head_t["ms"])
        t2 = p.ts(MSm[:, 4:8], p.bank(5, 4, 8), 1.0 / 96, EPS, ALU.mult, ALU.add, t)
        p.bank_free[5] = t2
        t1 = p.ts(MSm[:, 0:4], MSm[:, 0:4], EPS, None, ALU.add, ALU.bypass, t1)
        t = head_t["ms"] = p.pow(RSm[:, :], MSm[:, :], t1, t2, head_t["rs"])
        yield
        yield
        yield
        q_ok[h] = q_ok[h] + [p.tt(RQ[:, 4 * h:4 * h + 4], RSm[:, 0:4], RCQ[:, 0:4], ALU.mult, t)]
        p.PE.wait(p.bank_free[6], t)
        for m in range(4):
            t = p.mm(p.bank(6, 128 * m, 128 * m + 128), RSm[:, 4 + m:5 + m].broadcast_to([128, 128]), p.ident[:, :],
                     m == 0, m == 3)
        head_t["rs"] = [t, q_ok[h][-1]]
        t = p.tt(mk[2][:, 0, :], KG[:, slot, :], p.bank(6), ALU.mult, t, t_kg, t_kr[1], war)
        p.bank_free[6] = s_kg[slot] = t
        k_ok[h] = split(p, mk[2][:, 0, :], mk[0][:, 0, :], mk[1][:, 0, :], t, war)
        yield

    s_kg, s_sqk = {}, {}
    yield from head(0)
    yield from head(1)

    qs_ok, ks_ok, bq_ok, bk_ok = [], [], [None] * 2, [None] * 2

    def tile2(kind, i):
        yield from p.gemm(1, [8], xh, xl, xt, NX, keep, [7])
        b, t = got.pop()
        if kind in "qk":
            st.t_sq = [head_t["sq"], st.t_sq]
            T = QS if kind == "q" else KS
            yield from qk_tile(p, st, T[2][:, i, :], T[0][:, i, :], T[1][:, i, :], b, t, NX, col(6 if kind == "q" else 7),
                               False, qs_ok if kind == "q" else ks_ok, RQ2[:, 8 * i:8 * i + 8] if kind == "q" else None, 5)
            head_t["sq"] = st.t_sq
        else:
            T, ok = (BQ, bq_ok) if kind == "Q" else (BK, bk_ok)
            t1 = p.act(T[2][:, i, :], p.bank(b), ACT.Copy, t, t_mla, scale=0.125 if kind == "Q" else 1.0)
            p.bank_free[b] = t1
            yield
            ok[i] = split(p, T[2][:, i, :], T[0][:, i, :], T[1][:, i, :], t1)
            yield

    def mla_fill():
        yield from tile2("q", 0)
        yield from head(2)
        yield from tile2("q", 1)
        yield from head(3)
        yield from tile2("q", 2)
        yield from head(4)
        yield from tile2("k", 0)
        yield from head(5)

    NM, RS, RC = p.NM, p.RS, p.RC
    p_free, pt_free = [st_free(p)] * 2, [None] * 2
    turn_no = [0]
    t_y = {}
    PB, YB = 3, 4
    SBK = [0, 1, 2]

    def soft_unit(kind, i, j, m, fill):
        n = turn_no[0]
        turn_no[0] += 1
        slot, sb = n % 2, SBK[n % 3]
        Pr, Pt = PR[:, slot, :], PTR[:, slot, :]
        s = {}
        par = (i + (1 if kind == "w" else 0)) % 2
        c = 2 * m + j
        nm, rs = NM[:, par, c:c + 1], RS[:, par, c:c + 1]
        keys = 128 * (m + 1) if kind == "m" else (128 if m == 0 else 256)
        k0 = 0 if kind == "m" or m == 0 else 128 * (m - 1)
        h = 2 * i + j

        def score():
            if kind == "m":
                while h not in k_ok:
                    next(fill[0])
                deps = q_ok[h] + k_ok[h]
                q = [T[:, 0, 128 * m:128 * m + 128] for T in MQ[h % 2][:2]]
                k = [T[:, 0, 0:max(keys, 256)] for T in MK[h % 2][:2]]
            else:
                deps = qs_ok[i] + ks_ok[0]
                ps = slice(64 * j, 64 * j + 64)
                q = [T[ps, i, 128 * m:128 * m + 128] for T in QS[:2]]
                k = [T[ps, 0, k0:k0 + 256] for T in KS[:2]]
            p.PE.wait(p.bank_free[sb], *deps)
            s["t"] = p.product(p.bank(sb, 0, max(keys, 256)), q, k, True, True)
            if kind == "m" and m == 3:
                s_read[h] = s["t"]

        def soft():
            if kind == "m":
                S = p.bank(sb, keys - 128, keys)
                rq = RQ[:, 4 * h + m:4 * h + m + 1]
                if m:
                    m0 = NM[:, 2 + par, c:c + 1]
                    t0 = p.reduce_max(m0, p.bank(sb, 0, keys - 128), False, s["t"])
                    t = p.ttr(S, S, CAUS, 1.0, m0, ALU.add, ALU.max, nm, t0, t_k2)
                else:
                    t = p.ttr(S, S, CAUS, 1.0, -3e38, ALU.add, ALU.max, nm, s["t"], t_k2)
                t = p.ts(nm, nm, rq, -1.0, ALU.mult, ALU.mult, t)
                s["e"] = p.act(Pr[:, :keys], p.bank(sb, 0, keys), ACT.Exp, t, p_free[slot], scale=rq, bias=nm, accum_out=rs)
            else:
                S = p.bank(sb, 0, keys)
                hd = i + 3 * j
                rq = RQ2[:, 8 * i + c:8 * i + c + 1]
                b = bi[hd][:, m, 256 - keys:256]
                t = s["bias"] = p.stt(S, S, rq, b, ALU.mult, ALU.add, s["t"], t_bias[hd])
                t = p.reduce_max(nm, S, False, t)
                t = p.ts(nm, nm, G2[:, 8 + hd:9 + hd], -1.0, ALU.max, ALU.mult, t)
                t1 = p.act(ES[:, 8 * par + c:8 * par + c + 1], nm, ACT.Exp, t, es_free[par], bias=G2[:, 8 + hd:9 + hd])
                s["es"] = t1
                s["e"] = p.act(Pr[:, :keys], S, ACT.Exp, t, p_free[slot], bias=nm, accum_out=rs)
                if m == 3:
                    load_bias2(order.index(hd) + 2, s["bias"])
            p.bank_free[sb] = s["e"]

        def turn():
            p.PE.wait(p.bank_free[PB], s["e"])
            nk = keys // 128
            for k in range(nk):
                t = p.tr(p.bank(PB, 128 * k, 128 * k + 128), Pr[:, 128 * k:128 * k + 128], k == nk - 1)
            p_free[slot] = t
            if n % 2:
                t = p.act(Pt[:, :keys], p.bank(PB, 0, keys), ACT.Copy, t, pt_free[slot])
            else:
                t = p.copy(Pt[:, :keys], p.bank(PB, 0, keys), t, pt_free[slot])
            s["pt"] = p.bank_free[PB] = t

        def value():
            first, last = j == 0 and m == 0, j == 1 and m == 3
            src, tv, hs = (VA, t_va, 64 * h) if kind == "m" else (V, t_v, 64 * j)
            if first:
                p.PE.wait(p.bank_free[YB], *tv)
            p.PE.wait(s["pt"])
            o = p.bank(YB, 64 * c, 64 * c + 64)
            nk = keys // 128
            for k in range(nk):
                t = p.mm(o, Pt[:, 128 * k:128 * k + 128], src[:, k0 // 128 + k, hs:hs + 64], first and k == 0, k == nk - 1)
            pt_free[slot] = t
            if last:
                tr = s["e"]
                if kind == "w":
                    tr = es_free[par] = p.tt(RS[:, par, :], RS[:, par, :], ES[:, 8 * par:8 * par + 8], ALU.add, s["e"], s["es"])
                t1 = p.recip(RC[:, par, :], RS[:, par, :], tr)
                f = 128 * i + (384 if kind == "w" else 0)
                t2 = p.tt(Y[:, :, f:f + 128].rearrange("p m (j d) -> p m j d", j=2),
                          p.bank(YB).rearrange("p (m j d) -> p m j d", m=4, j=2),
                          RC[:, par, :].rearrange("p (m j) -> p m j", j=2).unsqueeze(3).broadcast_to([128, 4, 2, 64]),
                          ALU.mult, t, t1)
                p.bank_free[YB] = t_y[f // 128] = t2

        return score, soft, turn, value

    fill = [mla_fill()]
    units = [soft_unit("m", i, j, m, fill) for i in range(3) for j in range(2) for m in range(4)]
    yield from p.attend(units, fill[0], 8)
    drain(fill[0])
    t_mla = [(p.PE.sem, p.PE.count), p.t_last_act(), p.t_last_dve()]

    BQ, BK = trio("BQ", 2, 0), trio("BK", 2, 77824)
    BI2 = [f32("BW0", [128, 4, 256], 57344), f32("BW1", [128, 4, 256], 61440)]
    lb = [p.slot("bw0_in" + L), p.slot("bw1_in" + L)]
    order = [0, 3, 1, 4, 2, 5]
    t_bias, es_free = {}, [None, None]

    def load_bias2(k, *tickets):
        if k < 6:
            h = order[k]
            t_bias[h] = p.SP.dma(BI2[k % 2][:, :, :], scratch["bias"][h].rearrange("q (m k) -> q m k", m=4), lb[k % 2],
                                 p.t_bias2[h], *tickets)

    load_bias2(0, *t_mla)
    load_bias2(1)
    bi = {h: BI2[k % 2] for k, h in enumerate(order)}

    def win_fill():
        for kind in "QK":
            for i in range(2):
                yield from tile2(kind, i)

    units = [soft_unit("w", i, j, m, None) for i in range(3) for j in range(2) for m in range(4)]
    fill = [win_fill()]
    yield from p.attend(units, fill[0], 5)
    drain(fill[0])

    t_swa = [(p.PE.sem, p.PE.count), p.t_last_act(), p.t_last_dve()]
    LN, AT = f32("LN", [128, 8, NX], 12288), f32("AT", [128, 2, NX], 34816)
    E, LS = f32("E2", [128, 2, NX], 57344), f32("LS", [128, 2, NX], 61440)
    ln_free, at_free, e_free, ls_free = [t_swa] * 8, [t_swa] * 2, [t_swa] * 2, [t_swa] * 2

    def stick_unit(n, h, kc):
        i, ps = h // 2, slice(64 * (h % 2), 64 * (h % 2) + 64)
        zb, ab, slot = n % 2, 2 + n % 2, n % 2
        q0 = 128 * kc
        w = NX - q0
        wz = max(w, 256)
        z = p.bank(zb, wz - w, wz)
        l0 = 4 * (h % 2)
        e, ls, ln, at = E[:, slot, :w], LS[:, slot, :w], LN[:, l0 + kc, :w], AT[:, slot, :w]
        s = {}

        def score():
            p.PE.wait(p.bank_free[zb], *bq_ok[i], *bk_ok[i])
            s["t"] = p.product(p.bank(zb, 0, wz), [T[ps, i, q0:q0 + 128] for T in BK[:2]],
                               [T[ps, i, NX - wz:NX] for T in BQ[:2]], True, True)

        def soft():
            t = p.act(e, z, ACT.Abs, s["t"], e_free[slot])
            t = p.act(e, e, ACT.Exp, t, scale=-1.0)
            t = p.act(e, e, ACT.Ln, t, bias=1.0)
            t = p.stt(ls, z, 0.0, e, ALU.min, ALU.subtract, t, ls_free[slot])
            e_free[slot] = t
            s["ls"] = t
            t = p.tt(ln, ls, z, ALU.subtract, t, ln_free[l0 + kc])
            p.bank_free[zb] = t
            s["ln"] = lns[h, kc] = p.tt(LN[:, l0 + kc, 0:128], LN[:, l0 + kc, 0:128], M01, ALU.mult, t, t_k2)

        def turn():
            o = p.bank(ab, 0, w)
            p.PE.wait(p.bank_free[ab], s["ln"])
            t = p.mm(o, TRI, ln, True, kc == 3)
            for kk in range(kc + 1, 4):
                p.PE.wait(lns[h, kk])
                t = p.mm(p.bank(ab, 128 * (kk - kc), w), ONE, LN[:, l0 + kk, :NX - 128 * kk], False, kk == 3)
            if kc == 0:
                for kk in range(4):
                    ln_free[l0 + kk] = t
            t = p.tt(ls, ls, o, ALU.add, t, s["ls"])
            p.bank_free[ab] = t
            t = ls_free[slot] = p.act(at, ls, ACT.Exp, t, at_free[slot])
            s["at"] = p.tt(AT[:, slot, 0:128], AT[:, slot, 0:128], M01, ALU.mult, t)

        def value():
            first = h % 2 == 0 and kc == 3
            if first:
                p.PE.wait(p.bank_free[YB], *t_v)
            p.PE.wait(s["at"])
            for m in range(kc, 4):
                o = p.bank(YB, 128 * m + 64 * (h % 2), 128 * m + 64 * (h % 2) + 64)
                t = p.mm(o, AT[:, slot, 128 * (m - kc):128 * (m - kc) + 128], V[:, kc, 128 + 64 * h:192 + 64 * h],
                         first and m == kc, m == 3)
            at_free[slot] = t
            if h % 2 and kc == 0:
                f = 768 + 128 * i
                t2 = p.copy(Y[:, :, f:f + 128], p.bank(YB).rearrange("p (m d) -> p m d", m=4), t)
                p.bank_free[YB] = t_y[f // 128] = t2

        return score, soft, turn, value

    lns = {}
    XHc, XLc, XLfc = p.XH, p.XL, p.XLf
    t_out = [None] * 8
    JK = f32("JK", [128, 384], 65536)
    ss = {"ms": None, "jk": t_swa}

    def section(f0, f1):
        c0, c1 = f0 // 128, f1 // 128
        ts_ = [t_y[c] for c in range(c0, c1)]
        for m in range(4):
            t = p.act(JK[:, :f1 - f0], Y[:, m, f0:f1], ACT.Square, *ts_, ss["jk"], ss["ms"], accum_out=SS[:, m:m + 1])
            ss["jk"] = t
        yield
        t = p.ts(SS[:, 4:8], SS[:, 0:4], 1.0 / (f1 - f0), EPS, ALU.mult, ALU.add, t)
        t = ss["ms"] = p.pow(SS[:, 0:4], SS[:, 4:8], t)
        yield
        yield
        yield
        for m in range(4):
            t1 = p.ts(Y[:, m, f0:f1], Y[:, m, f0:f1], SS[:, m:m + 1], None, ALU.mult, ALU.bypass, t, *ts_)
        ss["ms"] = t1
        yield
        for c in range(c0, c1):
            b = 5 + c % 3
            p.PE.wait(p.bank_free[b], t1)
            for m in range(4):
                t = p.tr(p.bank(b, 128 * m, 128 * m + 128), Y[:, m, 128 * c:128 * c + 128], m == 3)
            t = p.act(XLfc[:, c, :], p.bank(b), ACT.Copy, t, t_swa, scale=col(14 + c))
            p.bank_free[b] = t
            yield
            t_out[c] = split(p, XLfc[:, c, :], XHc[:, c, :], XLc[:, c, :], t)
            yield

    fill = [chain(section(0, 384), section(384, 768))]
    units = [stick_unit(4 * h + 3 - kc, h, kc) for h in range(4) for kc in (3, 2, 1, 0)]
    yield from p.attend(units, fill[0], 2)
    drain(fill[0])
    yield from section(768, 1024)
    p.t_mix = t_out


def st_free(p):
    return [p.t_last_act(), p.t_last_dve(), (p.PE.sem, p.PE.count)]


def second_block(p, sx, scratch):
    r = Block2(p, sx)
    xh, xl, xt = (lambda k: p.XH[:, k, :]), (lambda k: p.XL[:, k, :]), (lambda k: p.XMt[k])
    f32 = lambda n, s, o: p.at(n, s, F32, p.BIG + o)
    f32r = lambda n, s, o: p.at(n, s, F32R, p.BIG + o)
    H = (f32r("H2H", [128, FC, NX], 0), f32r("H2L", [128, FC, NX], 45056),
         f32("H2Hf", [128, FC, NX], 0), f32("H2Lf", [128, FC, NX], 45056))
    SQM = f32("SQM", [128, 4, NX], 12288)
    G4 = [0, 1, 2, 3]
    hh, hl, ht = (lambda k: H[0][:, k, :]), (lambda k: H[1][:, k, :]), (lambda k: p.t_h[k])
    for layer in range(2):
        if layer == 0:
            p.t_rb = sx.t_rb
            drain(r.modulate(0, 0, p.XH, p.XL, p.XLf, p.XMt))
        drain(up_glu(p, xh, xl, xt, H, None, 3))
        drain(p.gemm(KC, DOWN, hh, hl, ht, NX, r.adder(layer, 3, p.XHf), G4))
        drain(r.norm(layer, 1, p.XH, p.XL, p.XLf, p.XMt))
        drain(mixer2(p, r, layer, xh, xl, xt, scratch))
        mt = list(p.t_mix)
        drain(p.gemm(KC, [8], xh, xl, lambda k: mt[k], NX, r.adder(layer, 4, SQM), G4, lead=3))
        drain(r.norm(layer, 2, p.XH, p.XL, p.XLf, p.XMt))
        drain(up_glu(p, xh, xl, xt, H, None, 3))
        drain(p.gemm(KC, DOWN, hh, hl, ht, NX, r.adder(layer, 5, None if layer else p.XHf), G4))
        if layer == 0:
            drain(r.norm(1, 0, p.XH, p.XL, p.XLf, p.XMt))


def make_plan(p):
    A, plan = p.A, p.plan

    def W(name, n, units=None):
        return [("W", A[name][u], n, None) for u in (units or range(A[name].shape[0]))]

    def W_down(name):
        return [("W", A[name][u, :, 0:128 * DOWN[u % 3]], 128 * DOWN[u % 3], None) for u in range(24)]

    rows1 = [(0, c, k) for c in (2, 3, 4, 5) for k in range(8)] + [(1, c, k) for c in range(6) for k in range(8)]
    a_items = deque()
    for n, (l, c, k) in enumerate(rows1):
        a_items.append(("A", A["wA1"][n], 1024, p.ada1_item(l, 8 * c + k, l == 0 or c < 2)))

    def add(ws, every, count):
        for i, w in enumerate(ws):
            plan.append(w)
            if every and i % every == every - 1:
                for _ in range(count):
                    if a_items:
                        plan.append(a_items.popleft())

    def P(k):
        plan.append(("P", A["wP"][2 * k], 1024, row_item(p, k, 0)))
        plan.append(("P", A["wP"][2 * k + 1], 1024, row_item(p, k, 1)))

    for l in range(2):
        for c in range(72):
            a_items.append(("A", A["wA2"][72 * l + c], 1024, p.ada2_item(l, c)))
    u, va, vT, vF, q, k_ = (W(n, 1024) for n in ("w_u", "w_va", "w_vT", "w_vF", "w_q", "w_k"))
    P(0)
    add(u[:3], 0, 0)
    for k in range(1, KC):
        P(k)
    add(u[3:] + va + vT + q + k_, 0, 0)
    add(u + va + vF + q + k_, 1, 1)
    out0 = W("w_out0", 1024)
    add(out0, 1, 1)
    add(out0, 0, 0)
    up, dn = W("w_up0", 1024), W_down("w_down0")
    add(up, 1, 1)
    add(dn, 1, 1)
    add(up, 0, 0)
    add(dn, 0, 0)
    k1, v1, q1 = W("w_k1", 1024), W("w_v1", 1024), W("w_q1", 1024)
    add(k1 + v1 + q1[:1], 1, 1)
    add(k1 + v1, 0, 0)
    add(q1[1:], 1, 1)
    add(W("w_out1", 1024), 1, 1)
    add(W("w_up1", 1024), 1, 1)
    add(W_down("w_down1"), 1, 1)

    def W2(name, l, n, units=None):
        return [("W", A[name][l][u][:, 0:n], n, None) for u in (units or range(A[name].shape[1]))]

    def W2_down(name, l):
        return [("W", A[name][l][u][:, 0:128 * DOWN[u % 3]], 128 * DOWN[u % 3], None) for u in range(24)]

    for l in range(2):
        add(W2("w_gu1", l, 1024), 1, 1)
        add(W2_down("w_dn1", l), 1, 1)
        add(W2("w_cq", l, 1024), 0, 0)
        add(W2("w_kpe", l, 512) + W2("w_v2", l, 768) + W2("w_va2", l, 384), 0, 0)
        heads, sec = W2("w_h", l, 320), W2("w_qk2", l, 1024)
        for w in (heads[0], heads[1], sec[0], heads[2], sec[1], heads[3], sec[2], heads[4], sec[3], heads[5]):
            add([w], 0, 0)
        add(sec[4:], 0, 0)
        add(W2("w_out2", l, 1024), 0, 0)
        add(W2("w_gu2", l, 1024), 0, 0)
        add(W2_down("w_dn2", l), 0, 0)
    assert not a_items


def program(nc, A):
    p = Prog(nc, A)
    make_plan(p)
    t_c0, t_x0, rows = start(p)
    p.t_crow = p.act(p.crow[:, :, :], p.crow[:, :, :], ACT.Silu, (p.t_crow_in))
    p.t_cw = p.t_const2
    mark = p.cst
    even_mixer(p, t_c0, t_x0, rows)
    p.cst = mark
    f32 = lambda n, s, o: p.at(n, s, F32, p.BIG + o)
    f32r = lambda n, s, o: p.at(n, s, F32R, p.BIG + o)
    sx = Stream(p, 0, NX, p.X, t_x0, 6, 7)
    sc = Stream(p, 1, NC, p.C, t_c0, 4, 5)
    G4 = [0, 1, 2, 3]

    sx.places(f32("YX1", [128, 8, NX], 24576), f32("SQX1", [128, 4, NX], 40960))
    sc.places(f32("YC1o", [128, 8, NC], 49152), f32("SQC1", [128, 4, NC], 65536))
    drain(p.gemm(KC, [8], lambda k: p.XH[:, k, :], lambda k: p.XL[:, k, :], lambda k: p.t_y[k], NX, sx.evac, G4))
    p.XMt = [None] * 8
    t_x_out = (p.PE.sem, p.PE.count)
    weave(p.gemm(KC, [8], lambda k: p.YC(k, 0), lambda k: p.YC(k, 1), lambda k: p.t_yc[k], NC, sc.evac, G4),
          chain(sx.post(0, 1), sx.pre1(0, 2, p.XH, p.XL, p.XLf, p.XMt, t_x_out)), 6)

    HX = [at for at in (f32r("HXH", [128, FC, NX], 0), f32r("HXL", [128, FC, NX], 45056),
                        f32("HXHf", [128, FC, NX], 0), f32("HXLf", [128, FC, NX], 45056))]
    HC = [at for at in (f32r("HCH", [128, FC, NC], 0), f32r("HCL", [128, FC, NC], 22528),
                        f32("HCHf", [128, FC, NC], 0), f32("HCLf", [128, FC, NC], 22528))]
    CM = [f32r("CM2H", [128, KC, NC], 45056), f32r("CM2L", [128, KC, NC], 53248),
          f32("CM2Hf", [128, KC, NC], 45056), f32("CM2Lf", [128, KC, NC], 53248)]
    xh, xl, xt = (lambda k: p.XH[:, k, :]), (lambda k: p.XL[:, k, :]), (lambda k: p.XMt[k])
    ch, cl = (lambda k: CM[0][:, k, :]), (lambda k: CM[1][:, k, :])
    war = []
    post_c = sc.post(0, 1)

    def post_then_mark():
        yield from post_c
        war.append(p.t_last_dve())
        war.append(p.t_last_act())
        war.append((p.PE.sem, p.PE.count))
    weave(up_conv(p, sx, xh, xl, xt, *HX, war, 3), post_then_mark(), 4)
    t_up = (p.PE.sem, p.PE.count)
    sx.places(p.XHf, p.XLf)
    sx.war = t_up
    drain(down(p, sx, HX[0], HX[1], sx.evac))
    t_down = (p.PE.sem, p.PE.count)
    ct = [None] * 8
    drain(sc.pre1(0, 2, CM[0], CM[1], CM[3], ct, t_down))
    weave(up_conv(p, sc, ch, cl, lambda k: ct[k], *HC, t_down, 3),
          chain(sx.post(0, 3), sx.pre1(1, 0, p.XH, p.XL, p.XLf, p.XMt)), 6)
    sc.places(CM[2], CM[3])
    sc.war = (p.PE.sem, p.PE.count)
    drain(down(p, sc, HC[0], HC[1], sc.evac))
    ct1 = [None] * 8

    QH, QL, t_out = odd_mixer(p, sx, xt, chain(sc.post(0, 3), sc.pre1(1, 0, CM[0], CM[1], CM[3], ct1)),
                              CM[0], CM[1], lambda k: ct1[k])
    sx.places(p.XHf, p.XLf)
    sx.war = None
    p.t_cw = p.SP.dma(p.CW[:, :, :], A["cw1"], p.cw_slot, p.t_last_act(), p.t_last_dve())
    drain(p.gemm(KC, [8], lambda k: QH[:, k, :], lambda k: QL[:, k, :], lambda k: t_out[k], NX, sx.evac, G4))
    drain(chain(sx.post(1, 1), sx.pre1(1, 2, p.XH, p.XL, p.XLf, p.XMt)))
    rope_d = nc.dram_tensor("rope_scratch", [64, NX], F32, kind="Internal").ap()
    bias_t = nc.dram_tensor("bias_scratch", [6, 128, 1024], F32, kind="Internal").ap()
    skew = [bass.AP(tensor=bias_t.tensor, offset=131072 * h + 1, ap=[[1025, 128], [256, 4], [1, 128]]) for h in range(6)]
    scratch = {"rope": rope_d, "bias": bias_t, "skew": skew}
    weave(up_conv(p, sx, xh, xl, xt, *HX, None, 3), positions(p, scratch), 4)
    sx.places(p.XHf, p.XLf)
    drain(down(p, sx, HX[0], HX[1], sx.evac))
    drain(sx.post(1, 3))
    p.out_slot = p.slot("out")
    second_block(p, sx, scratch)
    p.SP.wait((p.out_slot[0], p.out_slot[1]))
    finish(p)


def finish(p):
    with p.nc.Block() as block:
        for name, line in p.lines.items():
            def body(e, line=line):
                for op in line.ops:
                    op(e)
            {"tensor": block.tensor, "scalar": block.scalar, "vector": block.vector,
             "gpsimd": block.gpsimd, "sync": block.sync}[name](body)


def pack(I):
    def cols(v):
        v = np.asarray(v)
        return v.reshape(v.shape[:-1] + (-1, 128))

    def F(w, tiles=None):
        K, M = w.shape
        return w.reshape(K // 128, 128, M // 128, 128).transpose(2, 1, 0, 3).reshape(M // 128, 128, K)

    def T(w, cnt):
        K, M = w.shape
        return w.reshape(K // 128 // cnt, cnt, 128, M).transpose(0, 2, 1, 3).reshape(-1, 128, cnt * M)

    def pairs(w, a, b):
        n = w.shape[1] // 2
        K = w.shape[0]
        t = w.reshape(K, 2, n // 128, 128)[:, [a, b]]
        return t.transpose(0, 2, 1, 3).reshape(K, 2 * n)

    def D(w):
        t = w.reshape(FC, 128, KC, 128).transpose(2, 1, 0, 3)
        out = np.zeros((KC, 3, 128, 8, 128), w.dtype)
        k = 0
        for u, c in enumerate(DOWN):
            out[:, u, :, :c] = t[:, :, k:k + c]
            k += c
        return out.reshape(24, 128, 1024)

    O = {}
    c2 = lambda a, b: np.stack([a, b], -1)
    O["ccol"] = c2(cols(I["c"][0]).T, cols(I["c_ctx"]).T)
    O["ident"] = np.eye(128, dtype=np.float32)
    O["b1"] = cols(I["b_ada"]).transpose(2, 0, 1)
    O["ng1"] = cols(I["norm_g"]).transpose(3, 0, 1, 2)
    O["ctxT"] = I["ctx"][0].T.reshape(KC, 128, NC).transpose(1, 0, 2)
    O["xT"] = I["x"][0].T.reshape(KC, 128, NX).transpose(1, 0, 2)
    O["crow"] = np.broadcast_to(np.stack([I["c"][0], I["c_ctx"]])[None], (128, 2, 1024))
    O["b2"] = cols(I["b_mod_2"]).transpose(2, 0, 1)
    O["ng2"] = cols(I["norm_g_2"]).transpose(3, 0, 1, 2)
    for l in range(2):
        v = np.concatenate([I["conv_w"][l], I["conv_b"][l][None]])
        O[f"cw{l}"] = cols(v).transpose(2, 0, 1).reshape(128, 4, 2, FC).transpose(0, 1, 3, 2).reshape(128, 4, 44)
        O[f"w_up{l}"] = F(pairs(I["w_up"][l], 0, 1))
        O[f"w_down{l}"] = D(I["w_down"][l])
    wt = I["w_ada"].transpose(0, 2, 1).reshape(2, 48, 128, 1024)
    O["wA1"] = np.concatenate([wt[0, 16:], wt[1]])
    f = F(I["w_ada"][0][:, :2048])
    O["wP"] = np.stack([f[8:16], f[0:8]], 1).reshape(16, 128, 1024)
    w = I["w_in_ab"][0]
    O["w_u"], O["w_va"] = F(w[:, 0:512]), T(w[:, 512:1024], 2)
    O["w_q"], O["w_k"] = F(w[:, 1024:1536]), F(w[:, 1536:2048])
    O["w_vF"], O["w_vT"] = F(w[:, 2048:2560]), T(w[:, 2048:2560], 2)
    O["w_s"] = I["a_w_s"][0].transpose(2, 0, 1)
    O["b_s"] = np.broadcast_to(I["a_b_s"][0][None], (128, 4, 128))
    O["gv"] = cols(I["a_v_g"][0]).T
    O["w_out0"] = F(I["w_out_ab"][0])
    w = I["w_qkv_c"][0]
    heads = np.array([[h, h + 4] for h in range(4)] + [[h, h + 4] for h in range(8, 12)]).ravel()
    order = (heads[:, None] * 64 + np.arange(64)).ravel()
    O["w_q1"], O["w_k1"], O["w_v1"] = F(w[:, 0:1024][:, order]), F(w[:, 1024:1280]), T(w[:, 1280:1536], 4)
    O["w_out1"] = F(I["w_out_c"][0][order])
    O["qk_g1"] = np.tile(c2(I["c_q_g"][0], I["c_k_g"][0]), (2, 1))
    O["bi2"] = np.repeat(np.eye(2, dtype=np.float32), 64, axis=0)
    O["sel2"] = np.ascontiguousarray(O["bi2"].T)
    inv = (np.float32(10000.0) ** (-np.arange(16, dtype=np.float32) / np.float32(16))).astype(np.float32)
    t = np.arange(NX)
    ang = np.concatenate([(t // 64).astype(np.float32)[:, None] * inv, (t % 64).astype(np.float32)[:, None] * inv], 1)
    cos, sin = np.cos(ang).T, np.sin(ang).T
    O["rope1"] = np.stack([np.tile(cos, (4, 1)), np.tile(np.concatenate([-sin, sin]), (2, 1))], 1).astype(np.float32)
    rpb = I["b_rpb"][0]
    out = np.full((8, 128, 4, 256), -1e30, np.float32)
    q = np.arange(128)
    key = np.arange(256)
    for b in range(4):
        qr, qc = (q // 8) % 8, 16 * b + 8 * (q // 64) + q % 8
        kr, kc = (key // 8) % 8, 8 * (0, 1, 3, 4)[b] + 8 * (key // 64) + key % 8
        c0 = np.clip(qc - 8, 0, 48)
        ok = (kc[None] >= c0[:, None]) & (kc[None] < c0[:, None] + 16)
        dc = np.clip(kc[None] - qc[:, None], -15, 15) + 15
        dr = kr[None] - qr[:, None] + 7
        out[:, :, b, :] = np.where(ok[None], rpb[:, dr, dc], np.float32(-1e30))
    O["rpb"] = out
    J = {k[:-2]: v for k, v in I.items() if k.endswith("_2")}
    O["crow2"] = np.broadcast_to(J["c"], (128, 1024))
    wt = J["w_mod"].transpose(0, 2, 1)
    O["wA2"] = wt.reshape(144, 128, 1024)
    both = lambda f: np.stack([f(l) for l in range(2)])
    for n, a in (("1", "ffn1"), ("2", "ffn2")):
        O["w_gu" + n] = both(lambda l: F(pairs(J[f"w_{a}_gu"][l], 0, 1)))
        O["w_dn" + n] = both(lambda l: D(J[f"w_{a}_down"][l]))
    sw = np.arange(32) ^ 16
    win = J["w_in"]
    O["w_cq"] = both(lambda l: F(win[l][:, 0:384]))
    kp = np.concatenate([384 + np.arange(32), 384 + sw])
    O["w_kpe"] = both(lambda l: win[l][:, kp].reshape(8, 128, 64).transpose(1, 0, 2).reshape(1, 128, 512))
    vc = np.concatenate([np.arange(928, 1056), np.arange(1568, 1824)])
    O["w_v2"] = both(lambda l: T(win[l][:, vc], 2))
    wh = [0, 3, 1, 4, 2, 5]
    qc = np.concatenate([(416 + 64 * np.array(wh)[:, None] + np.arange(64)).ravel(), np.arange(800, 928),
                         np.arange(1056, 1568)])
    O["w_qk2"] = both(lambda l: F(win[l][:, qc]))
    hq = np.concatenate([np.arange(96), 64 + sw])
    def head(l, h):
        q = J["w_uq"][l][:, 96 * h + hq].reshape(2, 128, 128).transpose(1, 0, 2).reshape(128, 256)
        return np.concatenate([q, J["w_ukv"][l][:, 128 * h:128 * h + 64]], 1)
    O["w_h"] = both(lambda l: np.stack([head(l, h) for h in range(6)]))
    O["w_va2"] = both(lambda l: J["w_ukv"][l].reshape(128, 6, 2, 64)[:, :, 1].reshape(1, 128, 384))
    rows = np.concatenate([np.arange(384), (384 + 64 * np.array(wh)[:, None] + np.arange(64)).ravel(), np.arange(768, 1024)])
    O["w_out2"] = both(lambda l: F(J["w_out"][l][rows]))
    g2 = np.zeros((2, 128, 24), np.float32)
    for l in range(2):
        g2[l, :, 0] = J["mla_q_norm"][l][hq]
        g2[l, :64, 1] = J["mla_k_norm"][l][:64]
        g2[l, :64, 2] = J["mla_k_norm"][l][64 + np.concatenate([np.arange(32), sw])]
        g2[l, :, 3:5] = J["q_a_norm"][l].reshape(2, 128).T
        g2[l, :, 5] = J["kv_a_norm"][l]
        g2[l, :, 6] = np.tile(J["swa_q_norm"][l], 2)
        g2[l, :, 7] = np.tile(J["swa_k_norm"][l], 2)
        g2[l, :, 8:14] = J["sinks"][l][None]
        g2[l, :, 14:22] = J["out_norm"][l][rows].reshape(8, 128).T
    O["g2"] = g2
    i128 = np.arange(128)
    k2 = np.zeros((128, 6, 128), np.float32)
    m = i128 % 32
    k2[:64, 0, :] = (i128[None, :] >= 64) & (i128[:64, None] % 32 == m[None, :])
    k2[:, 1, :] = i128[:, None] > i128[None, :]
    k2[:, 2, :] = i128[:, None] < i128[None, :]
    k2[:, 3, :] = np.where(i128[None, :] > i128[:, None], -1e30, 0)
    k2[:, 4, :] = 1
    k2[:2, 5, :] = O["sel2"]
    O["k2"] = k2
    pos = J["positions"][0]
    O["pos_row"] = np.broadcast_to(pos, (64, NX))
    idx = 128 * np.arange(4)[None, :, None] + i128[:, None, None] - 127 + i128[None, None, :]
    O["pos_win"] = np.concatenate([pos[np.maximum(idx, 0)], pos[128 * np.arange(4)[None, :, None] + i128[:, None, None]]], -1)
    freq = (np.float32(10000.0) ** (-np.arange(16, dtype=np.float32) / np.float32(16))).astype(np.float32)
    fq = np.zeros((64, 4), np.float32)
    fq[:, 0] = np.tile(freq, 4)
    fq[:32, 1], fq[:32, 2] = np.pi / 2, 0.25
    fq[:, 3] = np.where(np.arange(64) // 16 == 2, -1, 1)
    O["freq"] = fq
    O["rel_bias"] = np.broadcast_to(J["rel_bias"], (128, 32, 6))
    O["mask_fill"] = np.full((128, 1024), -1e30, np.float32)
    return {k: np.ascontiguousarray(v) for k, v in O.items()}


def kernel(**inputs):
    import concourse.bacc as _bacc
    from concourse.bass_utils import run_bass_kernel_spmd as _run

    arrays = pack({k: np.asarray(v) for k, v in inputs.items()})
    nc = _bacc.Bacc("TRN2", target_bir_lowering=False, num_devices=1)
    A = {k: nc.dram_tensor(k, v.shape, mybir.dt.from_np(v.dtype), kind="ExternalInput").ap() for k, v in arrays.items()}
    A["out"] = nc.dram_tensor("out", (128, KC, NX), F32, kind="ExternalOutput").ap()
    program(nc, A)
    r = _run(nc, [arrays], core_ids=[0])
    return r.results[0]["out"].transpose(2, 1, 0).reshape(1, NX, 1024)
```

```python
import concourse.bass as bass
from concourse import mybir
import numpy as np
from collections import deque
import math

F32 = mybir.dt.float32
F32R = mybir.dt.float32r
BF16 = mybir.dt.bfloat16
I32 = mybir.dt.int32
ACT = mybir.ActivationFunctionType
ALU = mybir.AluOpType
AX = mybir.AxisListType

EPS = 1e-6
KC = 8
NX = 512
NC = 256
FC = 22
DOWN = (8, 7, 7)


INF = float("inf")


def flat(tickets):
    for t in tickets:
        if isinstance(t, list):
            yield from flat(t)
        elif t is not None:
            yield t


def when(*tickets):
    return max((t[2] for t in flat(tickets)), default=0.0)


def known(*tickets):
    return all(known(*t) if isinstance(t, list) else t is not None for t in tickets)


def until(cond):
    while not cond():
        yield cond


def size(ap):
    n = 1
    for s in ap.shape[1:]:
        n *= s
    return n


TABLES = {ACT.Exp: "exp", ACT.Ln: "ln", ACT.Silu: "silu", ACT.Sin: "silu", ACT.Gelu_apprx_tanh: "gelu"}


class Line:

    def __init__(self, sem):
        self.ops, self.sem, self.count, self.passed, self.t = [], sem, 0, {}, 0.0

    def wait(self, *tickets):
        for sem, value, t in flat(tickets):
            self.t = max(self.t, t)
            if self.passed.get(sem.name, 0) < value:
                self.passed[sem.name] = value
                self.ops.append(lambda e, s=sem, v=value: e.wait_ge(s, v))

    def put(self, fn, cost):
        self.ops.append(fn)
        self.t += cost

    def run(self, fn, *tickets, cost=100.0):
        self.wait(*tickets)
        self.count += 1
        self.t += cost
        self.ops.append(lambda e, s=self.sem: fn(e).then_inc(s, 1))
        return (self.sem, self.count, self.t + 60.0)

    def last(self):
        return (self.sem, self.count, self.t + 60.0)

    def dma(self, out, in_, slot, *tickets):
        self.wait(*tickets)
        slot[1] += 16
        self.t += 565.0 if self.sem.name == "sp_done" else 60.0
        self.ops.append(lambda e, s=slot[0]: e.dma_start(out, in_).then_inc(s, 16))
        self.bus[0] = max(self.bus[0], self.t) + size(out) * out.shape[0] * 4 / 370.0
        return (slot[0], slot[1], self.bus[0] + 2000.0)

    bus = [0.0]


class Pool:

    def claim(self, *places):
        yield from until(lambda: all(b in self.idle for b in places))
        for b in places:
            self.idle.remove(b)

    def __init__(self, *places):
        self.idle = deque(places)

    def take(self, leaving=0):
        yield
        yield from until(lambda: len(self.idle) > leaving)
        return self.idle.popleft()

    def give(self, place):
        self.idle.append(place)


class Prog:

    RW, RH = 3, 4

    def __init__(self, nc, A):
        self.nc, self.A = nc, A
        self.base = (nc.sbuf_base + 127) // 128 * 128
        self.PE, self.AC, self.VE, self.GP, self.SP = (
            Line(nc.alloc_semaphore(n)) for n in ("pe_done", "act_done", "dve_done", "pool_done", "sp_done"))
        self.lines = {"tensor": self.PE, "scalar": self.AC, "vector": self.VE, "gpsimd": self.GP, "sync": self.SP}
        self.psum = nc.alloc_psum_tensor("psum", [128, 8 * 512], F32)
        self.bank_free = [None] * 8
        self.tasks, self.born, self.now, self.quiet, self.table = [], 0, 0.0, 0, None
        self.plan, self.loaded, self.prepped, self.released = [], 0, 0, {}
        self.fifo, self.w_done, self.raw_ticket = deque(), {}, {}
        self.raw_slots = [[nc.alloc_semaphore(f"raw{i}_in"), 0] for i in range(self.RW)]
        self.a_plan, self.a_next, self.a_ticket, self.a_free = [], 0, None, None
        self.a_slot = self.slot("row_in")

        at = self.at
        self.X = at("X", [128, KC, NX], F32, 0)
        self.C = at("C", [128, KC, NC], F32, 16384)
        self.XM = 24576
        self.XH = at("XH", [128, KC, NX], F32R, self.XM)
        self.XL = at("XL", [128, KC, NX], F32R, self.XM + 16384)
        self.XHf = at("XHf", [128, KC, NX], F32, self.XM)
        self.XLf = at("XLf", [128, KC, NX], F32, self.XM + 16384)
        self.RAW = at("RAW", [128, self.RW, 1024], F32, 57344)
        self.ROW = at("ROW", [128, 1024], F32, 57344 + 4096 * self.RW)
        self.WH = at("WH", [128, self.RH, 1024], F32R, 73728)
        self.WL = at("WL", [128, self.RH, 1024], F32R, 90112)
        self.BIG = 106496
        self.cst = 196608
        const = self.const
        self.ident = const("ident", [128, 128], F32)
        self.ones = const("ones", [128, 8], F32)
        self.half = const("half", [128, 8], F32)
        self.ADA1 = const("ADA1", [128, 2, 2, 48], F32)
        self.ADA2 = const("ADA2", [128, 2, 72], F32)
        self.B1 = const("B1", [128, 2, 48], F32)
        self.B2 = const("B2", [128, 2, 72], F32)
        self.NG1 = const("NG1", [128, 2, 4, 8], F32)
        self.NG2 = const("NG2", [128, 2, 3, 8], F32)
        self.DER1 = const("DER1", [128, 2, 4, 2, 8], F32)
        self.DER2 = const("DER2", [128, 2, 6, 8], F32)
        self.CW = const("CW", [128, 4, 44], F32)
        self.CC = const("CC", [128, 8, 2], F32)
        self.NM, self.RS, self.RC = (const(n, [128, 4, 8], F32) for n in ("NM", "RS", "RC"))
        self.BI = const("BI2", [128, 2], F32)
        self.MS = const("MS", [128, 24], F32)
        self.RSQ = const("RSQ", [128, 24], F32)
        self.crow_off = self.cst
        self.crow = const("crow", [128, 2, 1024], F32)
        self.junk = const("junk", [128, 1024], BF16)
        self.t_ada1, self.t_ada2, self.t_der1, self.t_der2 = {}, {}, {}, {}
        self.norm_free = {0: [None, None], 4: [None, None]}
        self.t_junk = None

    def at(self, name, shape, dtype, off):
        return self.nc.alloc_sbuf_tensor_at(name, shape, dtype, offset=self.base + off)

    def const(self, name, shape, dtype):
        n = 1
        for s in shape[1:]:
            n *= s
        n *= 2 if dtype == BF16 else 4
        t = self.at(name, shape, dtype, self.cst)
        self.cst += (n + 31) // 32 * 32
        assert self.base + self.cst <= self.nc.sbuf_usable_end
        return t

    def slot(self, name):
        return [self.nc.alloc_semaphore(name), 0]

    def bank(self, b, lo=0, hi=512):
        return self.psum[:, b * 512 + lo:b * 512 + hi]

    def spawn(self, gen, rank):
        self.born += 1
        task = [rank, self.born, gen, None, False, self.now]
        self.tasks.append(task)
        self.tasks.sort(key=lambda t: t[:2])
        return task

    def due(self, need):
        if need is None:
            return 0.0
        if callable(need):
            v = need()
            return v if isinstance(v, float) else 0.0 if v else INF
        return when(need)

    def go(self):
        while self.tasks:
            self.now = max(self.now, self.PE.t)
            products = self.share and (self.cold or self.spent < self.share * (self.now - self.since))
            best, key, nearest, first = None, INF, None, INF
            for task in self.tasks:
                w = self.due(task[3])
                if w <= self.now:
                    v = max(w, task[5]) + 1000.0 * task[0]
                    if task[0] == 9:
                        v = -INF if products else 1e9
                    if v < key:
                        best, key = task, v
                elif w < first:
                    nearest, first = task, w
            if best is None:
                assert nearest is not None
                best, self.now = nearest, first
            before = self.PE.t
            try:
                best[3] = next(best[2])
                best[5] = self.now
            except StopIteration:
                best[4] = True
                self.tasks.remove(best)
            if best[0] == 9:
                self.spent += self.PE.t - before

    def mix(self, share):
        self.share, self.spent, self.since = share, 0.0, self.now

    share, spent, since = None, 0.0, 0.0

    def act(self, out, in_, func, *tickets, bias=None, scale=None, accum_out=None):
        kw = {k: v for k, v in (("bias", bias), ("scale", scale), ("accum_out", accum_out)) if v is not None}
        cost = 100.0 + 0.833 * size(out)
        table = TABLES.get(func, self.table)
        if table != self.table and not (self.table == "both" and table in ("exp", "ln")):
            self.table = table
            cost += 1300.0
        return self.AC.run(lambda e: e.activation(out, in_, func, **kw), *tickets, cost=cost)

    def tables(self, name):
        self.table = "both"
        self.AC.put(lambda e: e.preload_act_table_set(name), 1300.0)

    def dve(self, fn, out, *tickets):
        return self.VE.run(fn, *tickets, cost=65.0 + 1.04 * size(out))

    def tt(self, out, a, b, op, *tickets):
        return self.dve(lambda e: e.tensor_tensor(out, a, b, op), out, *tickets)

    def ts(self, out, a, s1, s2, op0, op1, *tickets):
        return self.dve(lambda e: e.tensor_scalar(out, a, s1, s2, op0, op1), out, *tickets)

    def stt(self, out, a, s, b, op0, op1, *tickets):
        return self.dve(lambda e: e.scalar_tensor_tensor(out, a, s, b, op0, op1), out, *tickets)

    def mm(self, out, lhsT, rhs, start, tick=False):
        fn = lambda e: e.matmul(out, lhsT, rhs, start=start, stop=True, skip_group_check=True)
        n = size(out)
        one = n / 2.4 + 3 if n >= 256 else 107.0
        cost = one if lhsT.dtype == F32R else (2 * one if n < 200 else 4 * n / 2.4 + 6)
        cost *= self.heat(n * (1 if lhsT.dtype == F32R else 4) * lhsT.shape[0] / 128)
        if tick:
            return self.PE.run(fn, cost=cost)
        self.PE.put(fn, cost)

    def tr(self, out, in_, tick=False):
        fn = lambda e: e.transpose(out, in_, self.ident[:, :])
        cost = 109.0 * self.heat(256)
        if tick:
            return self.PE.run(fn, cost=cost)
        self.PE.put(fn, cost)

    def heat(self, columns):
        if self.PE.t >= self.window[0]:
            idle = self.PE.t >= self.window[0] + 3413.0
            self.cold = idle or self.window[1] < 0.375 * 3413.0 * 2.4
            self.window = [(self.PE.t // 3413.0 + 1) * 3413.0, 0.0]
        self.window[1] += columns
        return 2 if self.cold else 1

    window, cold = [0.0, 0.0], True

    def load_next(self):
        i = self.loaded
        if i < len(self.plan):
            ap, n = self.plan[i]
            self.loaded += 1
            s = i % self.RW
            self.raw_ticket[i] = self.SP.dma(self.RAW[:, s, :n], ap, self.raw_slots[s],
                                             self.released.get(i - self.RW))

    def process_next(self):
        i = self.prepped
        self.prepped += 1
        n = self.plan[i][1]
        raw = self.RAW[:, i % self.RW, :n]
        h = i % self.RH
        hi, lo = self.WH[:, h, :n], self.WL[:, h, :n]
        free = self.w_done.get(i - self.RH)
        t_hi = self.act(hi, raw, ACT.Copy, self.raw_ticket[i], free)
        t_lo = self.tt(lo, raw, hi.bitcast(F32), ALU.subtract, t_hi, self.raw_ticket[i], free)
        self.fifo.append((i, hi, lo, t_hi, t_lo))
        self.released[i] = t_lo
        self.load_next()

    def can_prep(self):
        i = self.prepped
        return i in self.raw_ticket and (i < self.RH or (i - self.RH) in self.w_done)

    def prepare(self):
        while self.prepped < len(self.plan):
            yield from until(self.can_prep)
            yield [self.raw_ticket[self.prepped], self.w_done.get(self.prepped - self.RH)]
            self.process_next()

    def weights(self):
        yield from until(lambda: self.fifo)
        return self.fifo.popleft()

    def a_load(self):
        if self.a_next < len(self.a_plan):
            self.a_ticket = self.SP.dma(self.ROW[:, :], self.a_plan[self.a_next][0], self.a_slot, self.a_free)

    def a_step(self):
        if self.a_now is None:
            self.a_now = self.a_plan[self.a_next][1](self.ROW[:, :], self.a_ticket)
            self.a_next += 1
        try:
            next(self.a_now)
        except StopIteration as end:
            self.a_now, self.a_free = None, end.value
            self.a_load()

    a_now = None

    def spare(self, *tickets):
        return lambda: INF if self.quiet else max(self.VE.t + 150.0, when(*tickets))

    def rows(self):
        yield from until(lambda: self.a_ticket)
        while self.a_next < len(self.a_plan) or self.a_now:
            yield lambda: INF if self.quiet else max(self.VE.t + 150.0, when(self.a_ticket))
            if self.a_next < len(self.a_plan) or self.a_now:
                self.a_step()

    def modulation(self, table, *keys):
        while not all(k in table for k in keys):
            self.a_step()
        return [table[k] for k in keys]

    def leave(self, pool, b, ticket):
        if ticket is not None:
            self.bank_free[b] = ticket
            pool.give(b)

    def gemm(self, tiles, units, xh, xl, xt, n, evac, banks, lead=0):
        i = 0
        while i < tiles:
            g = lead if i == 0 and lead else 1
            bs = []
            for _ in range(g):
                b = yield from banks.take()
                bs.append(b)
            yield [self.bank_free[b] for b in bs]
            if g > 1:
                us = []
                for _ in range(g):
                    u = yield from self.weights()
                    us.append(u)
                self.PE.wait(*[self.bank_free[b] for b in bs])
                for k in range(units[0]):
                    yield from until(lambda: known(xt(k)))
                    yield [xt(k), us[0][3]]
                    self.PE.wait(xt(k))
                    for j in range(g):
                        w, hi, lo, t_hi, t_lo = us[j]
                        last = k == units[0] - 1
                        o = self.bank(bs[j], 0, n)
                        self.PE.wait(t_hi)
                        self.mm(o, hi[:, k * 128:k * 128 + 128], xh(k), k == 0)
                        yield
                        self.mm(o, hi[:, k * 128:k * 128 + 128], xl(k), False)
                        yield
                        self.PE.wait(t_lo)
                        t = self.mm(o, lo[:, k * 128:k * 128 + 128], xh(k), False, last)
                        if last:
                            self.w_done[w] = t
                            self.leave(banks, bs[j], evac(i + j, bs[j], t))
                        yield
            else:
                b = bs[0]
                self.PE.wait(self.bank_free[b])
                o = self.bank(b, 0, n)
                k0 = 0
                for u, cnt in enumerate(units):
                    w, hi, lo, t_hi, t_lo = yield from self.weights()
                    yield t_hi
                    self.PE.wait(t_hi)
                    for k in range(cnt):
                        yield from until(lambda: known(xt(k0 + k)))
                        yield xt(k0 + k)
                        self.PE.wait(xt(k0 + k))
                        self.mm(o, hi[:, k * 128:k * 128 + 128], xh(k0 + k), k0 + k == 0)
                        yield
                        self.mm(o, hi[:, k * 128:k * 128 + 128], xl(k0 + k), False)
                    yield t_lo
                    self.PE.wait(t_lo)
                    for k in range(cnt):
                        t = self.mm(o, lo[:, k * 128:k * 128 + 128], xh(k0 + k), False, k == cnt - 1)
                        yield
                    self.w_done[w] = t
                    k0 += cnt
                self.leave(banks, b, evac(i, b, t))
            i += g

    def gemm_t(self, units, cols, xh, xl, xt, toks, evac, banks):
        k0, bs = 0, []
        for t in range(toks):
            b = yield from banks.take()
            bs.append(b)
        yield [self.bank_free[b] for b in bs]
        self.PE.wait(*[self.bank_free[b] for b in bs])
        for u, cnt in enumerate(units):
            w, hi, lo, t_hi, t_lo = yield from self.weights()
            last = u == len(units) - 1
            for part in range(2):
                yield t_lo if part else t_hi
                self.PE.wait(t_lo if part else t_hi)
                for t in range(toks):
                    o = self.bank(bs[t], 0, cols)
                    for k in range(cnt):
                        kk = k0 + k
                        yield from until(lambda: known(xt(kk)))
                        yield xt(kk)
                        self.PE.wait(xt(kk))
                        cs = slice(k * cols, k * cols + cols)
                        ts = slice(t * 128, t * 128 + 128)
                        end = part == 1 and k == cnt - 1
                        if part == 0:
                            self.mm(o, xh(kk)[:, ts], hi[:, cs], kk == 0)
                            yield
                            self.mm(o, xl(kk)[:, ts], hi[:, cs], False)
                        else:
                            tk = self.mm(o, xh(kk)[:, ts], lo[:, cs], False, end)
                        yield
                    if last and part == 1:
                        if t == toks - 1:
                            self.w_done[w] = tk
                        self.leave(banks, bs[t], evac(t, bs[t], tk))
            if not last:
                self.w_done[w] = tk
            k0 += cnt

    def ssq_part(self, sq, n, first, small, *tickets):
        self.PE.wait(*tickets)
        nt = n // 128
        for j in range(nt):
            tk = self.mm(self.bank(small, j, j + 1), sq[:, j * 128:j * 128 + 128], self.ones[:, 0:1],
                         first and j == 0, j == nt - 1)
        return tk

    def rinv(self, tk, n, dim, rb, small, c0=0):
        t = yield from self.rsq(tk, n, dim, small, c0)
        return (yield from self.spread(t, n, rb, c0))

    def rsq(self, tk, n, dim, small, c0=0):
        nt = n // 128
        ms, rs, free = self.MS[:, c0:c0 + nt], self.RSQ[:, c0:c0 + nt], self.norm_free[c0]
        yield tk
        t = self.ts(ms, self.bank(small, 0, nt), 1.0 / dim, EPS, ALU.mult, ALU.add, tk, free[0])
        self.bank_free[small] = t
        free[0] = self.pow(rs, ms, t, free[1])
        return free[0]

    def spread(self, t, n, rb, c0=0):
        nt = n // 128
        rs, free = self.RSQ[:, c0:c0 + nt], self.norm_free[c0]
        yield [t, self.bank_free[rb]]
        self.PE.wait(t, self.bank_free[rb])
        for j in range(nt):
            tk = self.mm(self.bank(rb, j * 128, j * 128 + 128),
                         rs[:, j:j + 1].broadcast_to([128, 128]), self.ident[:, :], j == 0, j == nt - 1)
        free[1] = tk
        return tk

    def pow(self, out, in_, *tickets):
        h = self.half[:, :in_.shape[1]]
        return self.GP.run(lambda e: e.tensor_tensor(out, in_, h, ALU.pow), *tickets, cost=100.0 + 202.0 * size(out))

    def apply(self, src, t_src, n, g1, sh, t_mod, hi, lo, lof, rb, t_rb, war, out):
        r = self.bank(rb, 0, n)
        pend = None
        for k in range(KC + 1):
            if k < KC:
                yield from until(lambda: known(t_src(k), t_mod(k)))
                yield [t_rb, t_src(k), t_mod(k)]
                t = self.stt(lof(k), src(k), g1(k), r, ALU.mult, ALU.mult, t_rb, t_src(k), t_mod(k), war)
                if k == KC - 1:
                    self.bank_free[rb] = t
                t_hi = self.act(hi(k), lof(k), ACT.Identity, t, war, t_mod(k), bias=sh(k))
            if pend:
                j, tj = pend
                yield tj
                t_lo = self.stt(lo(j), lof(j), sh(j), hi(j).bitcast(F32), ALU.add, ALU.subtract, tj)
                out[j] = [tj, t_lo]
            pend = (k, t_hi) if k < KC else None

    def residual(self, y, t_y, n, gp, x, t_x, sq, small, rb, t_rb, out, t_g):
        r = self.bank(rb, 0, n)
        free = [None] * len(sq)
        yield [t_rb, t_g]
        self.PE.wait(self.bank_free[small])
        for m in range(KC):
            t = self.stt(y(m), y(m), gp(m), r, ALU.mult, ALU.mult, t_rb, t_y[m], t_g)
            if m == KC - 1:
                self.bank_free[rb] = t
            out[m] = t = self.tt(x(m), x(m), y(m), ALU.add, t, t_x[m])
            i = m % len(sq)
            t = self.act(sq[i], x(m), ACT.Square, t, free[i])
            yield t
            free[i] = t_ssq = self.ssq_part(sq[i], n, m == 0, small, t)
        return t_ssq

    def flow(self, units, rank):
        done = [0] * len(units[0])

        def one(n):
            for s, stage in enumerate(units[n]):
                yield from until(lambda: done[s] == n)
                yield from stage()
                done[s] += 1
                if s == 0 and n + 1 < len(units):
                    self.spawn(one(n + 1), rank)
        self.spawn(one(0), rank)
        return lambda: done[-1] == len(units)

    def ttr(self, out, a, b, scale, init, op0, op1, acc, *tickets):
        return self.dve(lambda e: e.tensor_tensor_reduce(out, a, b, scale, init, op0, op1, acc), out, *tickets)

    def reduce_max(self, out, in_, negate, *tickets):
        return self.dve(lambda e: e.tensor_reduce(out, in_, AX.X, ALU.max, negate=negate), in_, *tickets)

    def recip(self, out, in_, *tickets):
        return self.dve(lambda e: e.reciprocal(out, in_), out, *tickets)

    def copy(self, out, in_, *tickets):
        return self.dve(lambda e: e.tensor_copy(out, in_), out, *tickets)

    def product(self, out, a, b, first, tick=False):
        self.mm(out, a[0], b[0], first)
        self.mm(out, a[0], b[1], False)
        return self.mm(out, a[1], b[0], False, tick)

    def ada1_item(self, layer, col, both):
        def fn(raw, t_raw):
            for w in range(2 if both else 1):
                t = self.ttr(self.junk[:, :], raw, self.crow[:, w, :], 1.0, self.B1[:, layer, col:col + 1],
                             ALU.mult, ALU.add, self.ADA1[:, layer, w, col:col + 1], t_raw, self.t_crow, self.t_junk)
                self.t_junk = t
                if col % 8 == 7:
                    self.t_ada1[layer, w, col // 8] = t
                if both and w == 0:
                    yield
            if (layer, col) == (1, 47):
                t2 = self.SP.dma(self.crow[:, 0, :], self.A["crow2"], self.slot("crow2_in"), t)
                self.t_crow2 = self.act(self.crow[:, 0, :], self.crow[:, 0, :], ACT.Silu, t2)
            return t
        return fn

    def ada2_item(self, layer, col):
        def fn(raw, t_raw):
            yield from ()
            t = self.ttr(self.junk[:, :], raw, self.crow[:, 0, :], 1.0, self.B2[:, layer, col:col + 1],
                         ALU.mult, ALU.add, self.ADA2[:, layer, col:col + 1], t_raw, self.t_crow2, self.t_junk)
            self.t_junk = t
            if col % 8 == 7:
                self.t_ada2[layer, col // 8] = t
            return t
        return fn


def split(p, f, hi, lo, *tickets):
    t_hi = p.act(hi, f, ACT.Copy, *tickets)
    return [t_hi, p.tt(lo, f, hi.bitcast(F32), ALU.subtract, t_hi)]


def start(p):
    A = p.A
    BIG = p.BIG
    t_cc = p.AC.dma(p.CC[:, :, :], A["ccol"], p.slot("ccol_in"))
    small = p.slot("const_in")
    for name, dst in (("ident", p.ident[:, :]), ("b1", p.B1[:, :, :]), ("ng1", p.NG1[:, :, :, :])):
        t_small = p.AC.dma(dst, A[name], small)
    places = [BIG + 4096 * i for i in range(6)] + [BIG + 40960 + 4096 * i for i in range(10)]
    RP = [p.at(f"RP{k}", [128, 1024], F32, places[k]) for k in range(8)]
    RV = [p.at(f"RV{k}", [128, 1024], F32, places[8 + k]) for k in range(8)]
    t_rp, t_rv, t_c0, t_x0 = [None] * 8, [None] * 8, [None] * 8, [None] * 8

    def load(dst, name, i, h, out):
        out[4 * h:4 * h + 4] = [p.SP.dma(dst[:, 4 * h:4 * h + 4, :], A[name][:, 4 * h:4 * h + 4, :], p.slot(f"{name}{h}_in"))] * 4

    load(p.C, "ctxT", 0, 0, t_c0)
    load(p.C, "ctxT", 1, 1, t_c0)
    t_rp[0] = p.SP.dma(RP[0][:, :], A["wP"][0], p.slot("rp0_in"))
    t_crow = p.SP.dma(p.crow[:, :, :], A["crow"], p.slot("crow_in"))
    t_rv[0] = p.SP.dma(RV[0][:, :], A["wV"][0], p.slot("rv0_in"))
    p.cw_slot = p.slot("const2_in")

    def loads():
        soon = lambda: Line.bus[0] - 3000.0
        for k in range(1, 8):
            yield soon
            t_rp[k] = p.SP.dma(RP[k][:, :], A["wP"][k], p.slot(f"rp{k}_in"))
            yield soon
            t_rv[k] = p.SP.dma(RV[k][:, :], A["wV"][k], p.slot(f"rv{k}_in"))
            if k < 4:
                p.load_next()
        for h in range(2):
            yield soon
            load(p.X, "xT", h, h, t_x0)
        yield soon
        p.a_load()
        for name, dst in (("b2", p.B2[:, :, :]), ("ng2", p.NG2[:, :, :, :]), ("cw0", p.CW[:, :, :])):
            p.t_cw = p.SP.dma(dst, A[name], p.cw_slot)
    p.GP.run(lambda e: e.memset(p.ones[:, :], 1.0))
    t_fill = p.GP.run(lambda e: e.memset(p.half[:, :], -0.5))
    for line in (p.PE, p.VE):
        line.wait(t_small, t_fill)
    t_ccs = p.act(p.CC[:, :, :], p.CC[:, :, :], ACT.Silu, t_cc)
    p.t_crow = p.act(p.crow[:, :, :], p.crow[:, :, :], ACT.Silu, t_crow)

    CMH, CML, CMLf = (p.at(n, [128, KC, NC], d, BIG + o) for n, d, o in (
        ("CMH", F32R, 24576), ("CML", F32R, 32768), ("CMLf", F32, 32768)))
    p.CMH, p.CML = CMH, CML
    t_der, t_sh = [None] * 8, [None] * 8

    def scale_rows():
        for k in range(8):
            bk = 4
            yield from until(lambda: t_rp[k])
            yield [t_rp[k], t_ccs, p.bank_free[bk]]
            p.PE.wait(p.bank_free[bk], t_ccs, t_rp[k])
            for kk in range(KC):
                t = p.mm(p.bank(bk, 0, 2), RP[k][:, kk * 128:kk * 128 + 128], p.CC[:, kk, :], kk == 0, kk == KC - 1)
            yield t
            t = p.ts(p.ADA1[:, 0, :, 8 + k], p.bank(bk, 0, 2), p.B1[:, 0, 8 + k:9 + k], None, ALU.add, ALU.bypass, t)
            p.bank_free[bk] = t
            t_der[k] = p.ts(p.DER1[:, 0, 0, :, k], p.ADA1[:, 0, :, 8 + k], 1.0, p.NG1[:, 0, 0, k:k + 1],
                            ALU.add, ALU.mult, t)

    def shift_rows():
        for k in range(8):
            yield from until(lambda: t_rv[k])
            yield [t_rv[k], p.t_crow]
            for w in (1, 0):
                p.t_junk = t = p.ttr(p.junk[:, :], RV[k][:, :], p.crow[:, w, :], 1.0, p.B1[:, 0, k:k + 1],
                                     ALU.mult, ALU.add, p.ADA1[:, 0, w, k:k + 1], t_rv[k], p.t_crow, p.t_junk)
            t_sh[k] = t

    p.xt, p.ct = [None] * 8, [None] * 8

    def stream(n, src, t0, small, rb, c0, w, h, l, lf, out):
        free = [None] * 3
        for k in range(KC):
            s = k % 3
            yield from until(lambda: t0[k])
            yield t0[k]
            sq = lf[:, s, :]
            t = p.act(sq, src[:, k, :], ACT.Square, t0[k], free[s])
            yield t
            free[s] = tk = p.ssq_part(sq, n, k == 0, small, t)
        t_rb = yield from p.rinv(tk, n, 1024, rb, small, c0)
        yield from p.apply(lambda k: src[:, k, :], lambda k: t0[k], n,
                           lambda k: p.DER1[:, 0, 0, w, k:k + 1], lambda k: p.ADA1[:, 0, w, k:k + 1],
                           lambda k: [t_der[k], t_sh[k]], lambda k: h[:, k, :], lambda k: l[:, k, :],
                           lambda k: lf[:, k, :], rb, t_rb, None, out)

    p.spawn(loads(), 0)
    p.spawn(scale_rows(), 1)
    p.spawn(stream(NC, p.C, t_c0, 6, 3, 4, 1, CMH, CML, CMLf, p.ct), 1)
    p.spawn(shift_rows(), 2)
    p.spawn(stream(NX, p.X, t_x0, 5, 7, 0, 0, p.XH, p.XL, p.XLf, p.xt), 3)
    return t_c0, t_x0


def even_mixer(p, G, sc):
    A, at, B = p.A, p.at, p.BIG
    f32 = lambda n, s, o: at(n, s, F32, B + o)
    f32r = lambda n, s, o: at(n, s, F32R, B + o)
    U, Uc = f32("U", [128, 4, NX], 0), f32("Uc", [128, 4, NC], 8192)
    UL, UcL = f32r("UL", [128, 4, NX], 0), f32r("UcL", [128, 4, NC], 8192)
    VA, VAc = f32("VA", [128, 4, 512], 12288), f32("VAc", [128, 2, 512], 20480)
    Q = [(f32r("QH", [128, 4, NX], 24576), f32r("QL", [128, 4, NX], 32768), f32("QLf", [128, 4, NX], 32768)),
         (f32r("KH", [128, 4, NX], 40960), f32r("KL", [128, 4, NX], 49152), f32("KLf", [128, 4, NX], 49152))]
    Qc = [(f32r("QHc", [128, 4, NC], 57344), f32r("QLc", [128, 4, NC], 61440), f32("QLcf", [128, 4, NC], 61440)),
          (f32r("KHc", [128, 4, NC], 65536), f32r("KLc", [128, 4, NC], 69632), f32("KLcf", [128, 4, NC], 69632))]
    VF, VTc = f32("VF", [128, 4, NX], 73728), f32("VTc", [128, 2, 512], 81920)
    WS, BS = f32("WS", [128, 4, 128], 86016), f32("BS", [128, 4, 128], 88064)
    YC0H = f32r("YCH0", [128, 4, NC], 20480)
    YC1H, YC1L = f32r("YCH1", [128, 4, NC], 57344), f32r("YCL1", [128, 4, NC], 61440)
    MV = p.const("MV", [128, 6, 2], F32)
    ST = p.const("ST", [128, 6, 6], F32)
    LNR = p.const("LNR", [128, 2, 8], F32)
    GV = p.const("GV", [128, 4], F32)
    lw = p.slot("gmlp_in")
    for name, dst in (("w_s", WS[:, :, :]), ("b_s", BS[:, :, :]), ("gv", GV[:, :])):
        t_gmlp = p.SP.dma(dst, A[name], lw)

    t_q, t_k, t_qc, t_kc = [[None] * 4 for _ in range(4)]
    t_u, t_uc, t_vf, t_vtc = [None] * 4, [None] * 4, [None] * 4, [None] * 2
    t_mv = [None] * 6

    def gate(dst, base):
        def evac(i, b, t):
            o, st = dst[:, i, :], ST[:, base + i, :]
            t = p.act(o, p.bank(b), ACT.Gelu_apprx_tanh, t)
            tb = p.dve(lambda e: e.bn_stats(st, o), o, t)
            mv = MV[:, base + i, :]
            t_mv[base + i] = p.dve(lambda e: e.bn_aggr(mv, st), mv, tb)
            return t
        return evac

    def parts(dst, t_dst, n, scale, order, war):
        H, L, Lf = dst

        def evac(i, b, t):
            o = Lf[:, i, :]
            if order:
                o = o.rearrange("p (g r c) -> p r g c", g=8, r=8)
            t1 = p.act(o, p.bank(b, 0, n), ACT.Copy, t, war(), scale=scale)
            t_dst[i] = split(p, Lf[:, i, :], H[:, i, :], L[:, i, :], t1)
            return t1
        return evac

    def plain(dst, t_dst, n, order):
        def evac(i, b, t):
            o = dst[:, i, :]
            if order:
                o = o.rearrange("p (g r c) -> p r g c", g=8, r=8)
            t_dst[i] = p.act(o, p.bank(b, 0, n), ACT.Copy, t)
            return t_dst[i]
        return evac

    xt = lambda k: p.xt[k]
    ct = lambda k: p.ct[k]
    ch, cl = lambda k: p.CMH[:, k, :], lambda k: p.CML[:, k, :]
    xh, xl = lambda k: p.XH[:, k, :], lambda k: p.XL[:, k, :]
    none = lambda: None
    t_y, t_yc = [None] * 8, [None] * 8
    t_s, mixed = {0: [None] * 4, 1: [None] * 4}, {}

    def gmlp(c):
        nt, n, base = (2, NC, 4) if c else (4, NX, 0)
        S, va = (Uc, VAc) if c else (U, VA)
        yield from until(lambda: known(t_mv[base:base + nt]))
        yield t_mv[base:base + nt]
        lo, hi = base, base + nt
        t = p.ts(LNR[:, 0, lo:hi], MV[:, lo:hi, 1], EPS, None, ALU.add, ALU.bypass, t_mv[base:base + nt])
        t_r = p.pow(LNR[:, 1, lo:hi], LNR[:, 0, lo:hi], t)
        yield t_r
        t_va = []
        for i in range(nt):
            o = va[:, i, :]
            yield
            t_va.append(p.ts(o, o, MV[:, base + i, 0:1], LNR[:, 1, base + i:base + i + 1], ALU.subtract, ALU.mult, t_r))
        for g in range(4):
            b = yield from G.take()
            yield [p.bank_free[b], t_va]
            p.PE.wait(p.bank_free[b], t_va, t_gmlp)
            for i in range(nt):
                t = p.mm(p.bank(b, i * 128, i * 128 + 128), va[:, i, g * 128:g * 128 + 128], WS[:, g, :], i == 0, i == nt - 1)
            if g == 3:
                mixed[c] = t
            yield t
            t_s[c][g] = p.stt(S[:, g, :].rearrange("p (t i) -> p t i", i=128),
                              p.bank(b, 0, n).rearrange("p (t i) -> p t i", i=128), GV[:, g:g + 1],
                              BS[:, g, :].unsqueeze(1).broadcast_to([128, nt, 128]), ALU.mult, ALU.add, t, t_gmlp)
            p.leave(G, b, t_s[c][g])

    def gelu(c, n, t_hi_free):
        S, hi, lo = (Uc, YC0H, UcL) if c else (U, p.XH, UL)

        def rest(i, b, t):
            yield from tmps.take()
            tmp = TMPS[c][:, :n]
            t = p.act(tmp, p.bank(b, 0, n), ACT.Gelu_apprx_tanh, t, tmp_free[0])
            p.leave(G, b, t)
            yield t
            t = tmp_free[0] = p.tt(S[:, i, :], S[:, i, :], tmp, ALU.mult, t, t_s[c][i])
            tmps.give(0)
            yield from until(lambda: known(t_hi_free()))
            yield t_hi_free()
            (t_yc if c else t_y)[i] = split(p, S[:, i, :], hi[:, i, :], lo[:, i, :], t, t_hi_free())

        def evac(i, b, t):
            p.spawn(rest(i, b, t), 3)
        return evac

    VT = f32("VT", [128, 7, 512], 8192)
    TMPS = f32("TMP", [128, NX], 22528), f32("TMPc", [128, NC], 49152)
    tmps, tmp_free = Pool(0), [None]
    vt = lambda s: VT[:, s, :]
    Yx, Yc = f32("Yx", [128, 2, 4, 128], 86016), f32("Yc", [128, 2, 512], 45056)
    PRc, PTRc = f32("PRc", [128, 2, 512], 24576), f32("PTRc", [128, 2, 512], 28672)
    PR, PTR = f32("PR", [128, 2, 512], 57344), f32("PTR", [128, 2, 512], 61440)
    BI = [f32("BI%d" % i, [128, 4, 256], 73728 + 4096 * i) for i in range(2)]
    NM, RS, RC = p.NM, p.RS, p.RC
    lb = [p.slot("rpb0_in"), p.slot("rpb1_in")]
    t_bias, t_att, t_vt = {}, {}, [None] * 7
    pair_left, nm_free, rc_free, y_free = {}, {}, {}, {}
    win = [(0, 2, 0), (1, 3, 1), (3, 5, 3), (4, 6, 4)]
    YB, TB = [5, 6], Pool(7)
    places = {kind: {"p": Pool(0, 1), "pt": Pool(0, 1), "P": P, "T": T, "p_free": [None] * 2, "t_free": [None] * 2}
              for kind, P, T in (("x", PR, PTR), ("c", PRc, PTRc))}

    def windows(war):
        yield from until(lambda: known(t_vf))
        for s in range(7):
            b = yield from G.take()
            yield p.bank_free[b]
            p.PE.wait(p.bank_free[b], t_vf)
            for j in range(4):
                t = p.tr(p.bank(b, j * 128, j * 128 + 128), VF[:, j, 64 * s:64 * s + 128], j == 3)
            yield t
            if s % 2:
                t_vt[s] = p.act(vt(s), p.bank(b), ACT.Copy, t, war)
            else:
                t_vt[s] = p.copy(vt(s), p.bank(b), t, war)
            p.leave(G, b, t_vt[s])
        for h in range(2):
            load_bias(h, t)

    def load_bias(h, *tickets):
        t_bias[h] = p.SP.dma(BI[h % 2][:, :, :], A["rpb"][h], lb[h % 2], *tickets)

    def unit(kind, n, h, b, total):
        i, off = h // 2, 64 * (h % 2)
        ps = slice(off, off + 64)
        place = places[kind]
        pair = (kind, i)
        par = i % 2
        yb = YB[par]
        s = {}

        def score():
            need = (lambda: [t_q[i], t_k[i], t_kc[i], t_vt]) if kind == "x" else (lambda: [t_qc[i], t_kc[i], t_vtc])
            yield from until(lambda: known(need()))
            sb = s["b"] = yield from G.take()
            yield [need(), p.bank_free[sb]]
            p.PE.wait(p.bank_free[sb], need())
            if kind == "x":
                g0 = win[b][2]
                q = [t[ps, i, 128 * b:128 * b + 128] for t in Q[0][:2]]
                p.product(p.bank(sb, 0, 256), q, [t[ps, i, 64 * g0:64 * g0 + 256] for t in Q[1][:2]], True)
                s["t"] = p.product(p.bank(sb, 256, 512), q, [t[ps, i, :] for t in Qc[1][:2]], False, True)
            else:
                for m in range(2):
                    s["t"] = p.product(p.bank(sb, 256 * m, 256 * m + 256), [t[ps, i, 128 * m:128 * m + 128] for t in Qc[0][:2]],
                                       [t[ps, i, :] for t in Qc[1][:2]], m == 0, m == 1)

        def soft():
            yield s["t"]
            a = s["p"] = yield from place["p"].take()
            sb, fr = s["b"], place["p_free"][a]
            Pr = place["P"][:, a, :]
            if kind == "x":
                c = (h % 2) * 4 + b
                nm, rs = NM[:, par, c:c + 1], RS[:, par, c:c + 1]
                m0 = NM[:, 2 + par, c:c + 1]
                t0 = p.reduce_max(m0, p.bank(sb, 256, 512), False, s["t"], nm_free.get((par, c)))
                yield from until(lambda: h in t_bias)
                loc = p.bank(sb, 0, 256)
                t1 = p.ttr(loc, loc, BI[h % 2][:, b, :], 1.0, m0, ALU.add, ALU.max, nm, t0, t_bias[h])
                if b == 3 and h + 2 < 8:
                    load_bias(h + 2, t1)
                t1 = p.ts(nm, nm, -1.0, None, ALU.mult, ALU.bypass, t1)
                yield t1
                s["e"] = p.act(Pr, p.bank(sb), ACT.Exp, t1, fr, rc_free.get(par), bias=nm, accum_out=rs)
            else:
                c = (h % 2) * 2
                t1 = p.reduce_max(NM[:, par, c:c + 2], p.bank(sb).rearrange("p (m k) -> p m k", m=2), True, s["t"],
                                  nm_free.get((par, c)), nm_free.get((par, c + 1)))
                yield t1
                for m in range(2):
                    s["e"] = p.act(Pr[:, 256 * m:256 * m + 256], p.bank(sb, 256 * m, 256 * m + 256), ACT.Exp, t1, fr, rc_free.get(par),
                                   bias=NM[:, par, c + m:c + m + 1], accum_out=RS[:, par, c + m:c + m + 1])
            nm_free[par, c] = p.bank_free[sb] = s["e"]
            G.give(sb)

        def turn():
            yield s["e"]
            pb = yield from TB.take()
            yield p.bank_free[pb]
            p.PE.wait(p.bank_free[pb], s["e"])
            Pr = place["P"][:, s["p"], :]
            for j in range(4):
                t = p.tr(p.bank(pb, 128 * j, 128 * j + 128), Pr[:, 128 * j:128 * j + 128], j == 3)
            place["p_free"][s["p"]] = t
            place["p"].give(s["p"])
            a = s["pt"] = yield from place["pt"].take()
            Pt = place["T"][:, a, :]
            yield [t, place["t_free"][a]]
            if n % 2:
                t = p.act(Pt, p.bank(pb), ACT.Copy, t, place["t_free"][a])
            else:
                t = p.copy(Pt, p.bank(pb), t, place["t_free"][a])
            s["tt"] = p.bank_free[pb] = t
            TB.give(pb)

        def value():
            first = pair not in pair_left
            pair_left.setdefault(pair, 8 if kind == "x" else 2)
            Pt = place["T"][:, s["pt"], :]
            yield [s["tt"], p.bank_free[yb] if first else None]
            if first:
                p.PE.wait(p.bank_free[yb])
            pair_left[pair] -= 1
            p.PE.wait(s["tt"])
            hs = slice(64 * h, 64 * h + 64)
            if kind == "x":
                w0, w1, _ = win[b]
                o = p.bank(yb, 128 * b + off, 128 * b + off + 64)
                vals = [vt(w0)[:, hs], vt(w1)[:, hs], VTc[:, 0, hs], VTc[:, 1, hs]]
                for j in range(4):
                    t = p.mm(o, Pt[:, 128 * j:128 * j + 128], vals[j], first and j == 0, j == 3)
            else:
                for m in range(2):
                    o = p.bank(yb, 128 * m + off, 128 * m + off + 64)
                    for j in range(2):
                        t = p.mm(o, Pt[:, 256 * m + 128 * j:256 * m + 128 * j + 128], VTc[:, j, hs],
                                 first and m == 0 and j == 0, m == 1 and j == 1)
            place["t_free"][s["pt"]] = t
            place["pt"].give(s["pt"])
            if pair_left[pair] == 0:
                k = 8 if kind == "x" else 4
                nt = k // 2
                Y = Yx[:, par, :, :] if kind == "x" else Yc[:, :, 128 * i:128 * i + 128]
                yield t
                t1 = p.recip(RC[:, par, :k], RS[:, par, :k], s["e"], rc_free.get(par))
                rc_free[par] = t_att[pair] = p.tt(Y.rearrange("p b (h d) -> p b h d", h=2),
                                   p.bank(yb, 0, 128 * nt).rearrange("p (b h d) -> p b h d", b=nt, h=2),
                                   RC[:, par, :k].rearrange("p (h b) -> p b h", h=2).unsqueeze(3).broadcast_to([128, nt, 2, 64]),
                                   ALU.mult, t, t1, [t_s[0], y_free.get(par)] if kind == "x" else None)
                p.bank_free[yb] = t_att[pair]

        return score, soft, turn, value

    def back(kind, j, t_pv):
        nt = 4 if kind == "x" else 2
        yield from until(lambda: (kind, j) in t_att and known(t_pv()))
        b = yield from G.take()
        yield [p.bank_free[b], t_att[kind, j]]
        p.PE.wait(p.bank_free[b], t_att[kind, j])
        for m in range(nt):
            y = Yx[:, j % 2, m, :] if kind == "x" else Yc[:, m, 128 * j:128 * j + 128]
            t = p.tr(p.bank(b, 128 * m, 128 * m + 128), y, m == nt - 1)
        yield t
        if kind == "x":
            y_free[j % 2] = t
            src = p.bank(b).rearrange("p (g r c) -> p g r c", g=8, r=8)
            v = lambda T: T[:, j, :].rearrange("p (r g c) -> p g r c", g=8, r=8)
            hi, hif, lo = v(Q[0][0]), v(Q[0][0]).bitcast(F32), v(Q[0][1])
            t1 = p.act(hi, src, ACT.Copy, t)
            yield t1
            t_y[4 + j] = [t1, p.tt(lo, src, hif, ALU.subtract, t1)]
            p.leave(G, b, t_y[4 + j][1])
        else:
            hi, lo = YC1H[:, j, :], YC1L[:, j, :]
            t1 = p.act(hi, p.bank(b, 0, NC), ACT.Copy, t, t_pv())
            yield t1
            t_yc[4 + j] = [t1, p.tt(lo, p.bank(b, 0, NC), hi.bitcast(F32), ALU.subtract, t1, t_pv())]
            p.leave(G, b, t_yc[4 + j][1])

    lists = lambda t: (lambda: t)
    yield from p.gemm(4, [8], ch, cl, ct, NC, parts(Qc[1], t_kc, NC, 1.0, False, none), G, lead=3)
    G.give(3)
    yield from p.gemm(4, [8], ch, cl, ct, NC, parts(Qc[0], t_qc, NC, 0.125, False, none), G)
    yield from p.gemm_t([2] * 4, 512, ch, cl, ct, 2, plain(VTc, t_vtc, 512, False), G)
    yield from p.gemm_t([2] * 4, 512, ch, cl, ct, 2, gate(VAc, 4), G)
    p.spawn(gmlp(1), 3)
    yield from until(lambda: known(t_s[1]))
    yield from p.gemm(4, [8], ch, cl, ct, NC, gelu(1, NC, lambda: mixed.get(1)), G)
    t_cm = p.PE.last()
    yield from until(lambda: known(p.xt))
    G.give(4)
    places["c"]["p_free"], places["c"]["t_free"] = [t_cm, t_cm], [t_cm, t_cm]
    c_done = p.flow([unit("c", h, h, 0, 8) for h in range(8)], 4)
    box = {}

    def mark(cond, name):
        yield from until(cond)
        box[name] = p.PE.last()
    p.spawn(mark(c_done, "c"), 0)
    for j in range(4):
        p.spawn(back("c", j, lambda: box.get("c")), 4)

    yield from p.gemm_t([2] * 4, 512, xh, xl, xt, 4, gate(VA, 0), G)
    p.spawn(gmlp(0), 3)
    yield from p.gemm(4, [8], xh, xl, xt, NX, plain(VF, t_vf, NX, True), G)

    yc = [f32("YC1a", [128, 4, NC], 28672), f32("YC1b", [128, 4, NC], 36864)]
    sc.places(lambda k: yc[k // 4][:, k % 4, :], f32("SQC1", [128, 4, NC], 45056), None, late=True)
    YC = lambda k, w: (((YC0H, UcL) if k < 4 else (YC1H, YC1L))[w][:, k % 4, :])
    yield from until(lambda: known(t_yc))
    sc.war = [p.PE.last(), p.AC.last(), p.VE.last()]
    yield from p.gemm(KC, [8], lambda k: YC(k, 0), lambda k: YC(k, 1), lambda k: t_yc[k], NC, sc.evac, G)
    t_yc_read = p.PE.last()
    yield from G.claim(4)
    post = p.spawn(sc.post(0, 1), 2)
    p.spawn(windows([t_yc_read, mixed[0]]), 3)
    places["x"]["p_free"], places["x"]["t_free"] = [t_yc_read] * 2, [t_yc_read] * 2

    war = lambda: t_yc_read
    kq = lambda i: (lambda j, b, t: parts(Q[1], t_k, NX, 1.0, True, war)(i, b, t),
                    lambda j, b, t: parts(Q[0], t_q, NX, 0.125, True, war)(i, b, t))
    for evac in kq(0):
        yield from p.gemm(1, [8], xh, xl, xt, NX, evac, G)
    for evac in kq(1)[:1]:
        yield from p.gemm(1, [8], xh, xl, xt, NX, evac, G)
    yield from until(lambda: post[4])
    G.give(4)
    t_post = [p.PE.last(), p.AC.last(), p.VE.last()]
    war = lambda: t_post
    x_done = p.flow([unit("x", 4 * h + b, h, b, 32) for h in range(8) for b in range(4)], 5)
    for j in range(4):
        p.spawn(back("x", j, lambda: []), 4)
    p.mix(0.45)
    xm = []
    for evac in kq(1)[1:] + kq(2) + kq(3):
        yield from p.gemm(1, [8], xh, xl, xt, NX, evac, G)
    yield from p.gemm(4, [8], xh, xl, xt, NX, gelu(0, NX, lambda: xm[0] if xm else None), G)
    xm.append(p.PE.last())
    p.t_y = t_y
    p.yh = lambda k: p.XH[:, k, :] if k < 4 else Q[0][0][:, k - 4, :]
    p.yl = lambda k: UL[:, k, :] if k < 4 else Q[0][1][:, k - 4, :]
    yield from until(x_done)
    p.mix(None)


def derive1(p, layer, kind, streams):
    if (layer, kind) in p.t_der1:
        return p.t_der1[layer, kind]
    chunk = (1, 2, 4, 5)[kind]
    deps = p.modulation(p.t_ada1, *[(layer, w, chunk) for w in range(streams)])
    out = p.DER1[:, layer, kind, 0:streams, :]
    ada = p.ADA1[:, layer, 0:streams, chunk * 8:chunk * 8 + 8]
    g = p.NG1[:, layer, kind, :].unsqueeze(1).broadcast_to([128, streams, 8])
    t = p.t_der1[layer, kind] = p.stt(out, ada, 1.0 if kind % 2 == 0 else 0.0, g, ALU.add, ALU.mult, *deps)
    return t


class Stream:

    def __init__(self, p, w, n, res, t_res, small, rb):
        self.p, self.w, self.n, self.res, self.small, self.rb = p, w, n, res, small, rb
        self.t_res = list(t_res)
        self.war = None

    def places(self, y, sq, war=None, late=False):
        self.late = late
        self.y, self.sq, self.war = y, sq, war
        self.t_y, self.sq_free, self.t_sum = [None] * KC, [None] * sq.shape[1], None

    def evac(self, i, b, t):
        p, n = self.p, self.n
        src = p.bank(b, 0, n)
        self.t_y[i] = p.act(self.y(i), src, ACT.Copy, t, self.war)
        if self.late:
            return self.t_y[i]
        if i == 0:
            t2 = self.t_sum = p.act(self.sq[:, 0, :], src, ACT.Square, t, self.war)
        else:
            s = 1 + (i - 1) % (self.sq.shape[1] - 1)
            t2 = p.act(self.sq[:, s, :], src, ACT.Square, t, self.war, self.sq_free[s])
            self.t_sum = self.sq_free[s] = p.tt(self.sq[:, 0, :], self.sq[:, 0, :], self.sq[:, s, :], ALU.add, t2, self.t_sum)
        return t2

    def post(self, layer, kind):
        p, n = self.p, self.n
        t_g = derive1(p, layer, kind, 2 if layer == 0 else 1)
        p.quiet += 1
        yield self.t_sum
        p.PE.wait(p.bank_free[self.small])
        if self.late:
            free = [None] * self.sq.shape[1]
            for k in range(KC):
                s = k % len(free)
                t = p.act(self.sq[:, s, :], self.y(k), ACT.Square, self.t_y[k], free[s])
                yield t
                free[s] = tk = p.ssq_part(self.sq[:, s, :], n, k == 0, self.small, t)
        else:
            tk = p.ssq_part(self.sq[:, 0, :], n, True, self.small, self.t_sum)
        t_rb = yield from p.rinv(tk, n, 1024, self.rb, self.small, 4 * self.w)
        m = self.sq.shape[1]
        tk = yield from p.residual(self.y, self.t_y, n, lambda k: p.DER1[:, layer, kind, self.w, k:k + 1],
                                   lambda k: self.res[:, k, :], self.t_res, [self.sq[:, 1 + s, :] for s in range(m - 1)],
                                   self.small, self.rb, t_rb, self.t_res, t_g)
        self.t_r = yield from p.rsq(tk, n, 1024, self.small, 4 * self.w)
        p.quiet -= 1

    def pre1(self, layer, kind, hi, lo, lof, out, war=None):
        p = self.p
        t_g = derive1(p, layer, kind, 2 if layer == 0 or kind == 0 else 1)
        c = 0 if kind == 0 else 3
        t_mod = [t_g] + p.modulation(p.t_ada1, (layer, self.w, c))
        t_res = self.t_res
        t_rb = yield from p.spread(self.t_r, self.n, self.rb, 4 * self.w)
        yield from p.apply(lambda k: self.res[:, k, :], lambda k: t_res[k], self.n,
                           lambda k: p.DER1[:, layer, kind, self.w, k:k + 1],
                           lambda k: p.ADA1[:, layer, self.w, 8 * c + k:8 * c + k + 1], lambda k: t_mod,
                           lambda k: hi[:, k, :], lambda k: lo[:, k, :], lambda k: lof[:, k, :],
                           self.rb, t_rb, war, out)


def chain(*gens):
    for g in gens:
        yield from g


def up_conv(p, s, xh, xl, xt, HH, HL, HHf, HLf, war, banks, lead):
    n, cw = s.n, p.CW
    t_h = [None] * FC
    late = deque()
    t_a = {}

    def conv(dst, i, b, t):
        src = p.bank(b, 0, n)
        t1 = p.act(dst, src, ACT.Identity, t, war(i // 2), p.t_cw, scale=cw[:, 1, i:i + 1], bias=cw[:, 3, i:i + 1])
        t2 = p.stt(dst[:, 1:n], src[:, 0:n - 1], cw[:, 0, i:i + 1], dst[:, 1:n], ALU.mult, ALU.add, t1, p.t_cw)
        return p.stt(dst[:, 0:n - 1], src[:, 1:n], cw[:, 2, i:i + 1], dst[:, 0:n - 1], ALU.mult, ALU.add, t2)

    def silu(j, t):
        f = HLf[:, j, :]
        t = p.act(f, f, ACT.Silu, t)
        t = p.tt(f, f, HHf[:, j, :], ALU.mult, t, t_a[j])
        late.append(lambda: high(j, t))

    def high(j, t):
        t = p.act(HH[:, j, :], HLf[:, j, :], ACT.Copy, t)
        late.append(lambda: low(j, t))

    def low(j, t):
        t_h[j] = [t, p.tt(HL[:, j, :], HLf[:, j, :], HHf_of(j), ALU.subtract, t)]

    def HHf_of(j):
        return HH[:, j, :].bitcast(F32)

    def evac(i, b, t):
        j = i // 2
        for _ in range(len(late)):
            late.popleft()()
        if i % 2 == 0:
            t_a[j] = t = conv(HHf[:, j, :], i, b, t)
        else:
            t = conv(HLf[:, j, :], i, b, t)
            late.append(lambda: silu(j, t))
        return t

    yield from p.gemm(2 * FC, [8], xh, xl, xt, n, evac, banks, lead=lead)
    while late:
        late.popleft()()
    s.t_h = t_h


def down(p, s, HH, HL, banks):
    yield from p.gemm(KC, DOWN, lambda k: HH[:, k, :], lambda k: HL[:, k, :], lambda k: s.t_h[k], s.n, s.evac, banks)


class Heads:

    def __init__(self, p, SW, TAB, SEL, RT, t_tab, banks, slots=None):
        self.SW, self.TAB, self.SEL, self.RT = SW, TAB, SEL, RT
        self.t_tab, self.banks, self.slots = t_tab, banks, slots
        self.t_sw, self.t_rt, self.t_ms, self.t_rsq = [None, None], None, [None] * 2, [None] * 2
        self.sw, self.rt, self.ms = Pool(0, 1), Pool(0), Pool(0, 1)
        self.MS = [p.MS[:, 8 + 8 * i:16 + 8 * i] for i in range(2)]
        self.RS = [p.RSQ[:, 8 + 8 * i:16 + 8 * i] for i in range(2)]


def qk_tile(p, st, raw_dst, SQ, hi, lo, b, t, n, gain, rope, turned, index, rank, rq=None, war=None):
    src = p.bank(b, 0, n)
    t_raw = p.act(raw_dst, src, ACT.Copy, t, st.t_tab, war, scale=gain)
    t_sq = p.act(SQ, src, ACT.Square, t, war)
    p.spawn(qk_rest(p, st, raw_dst, hi, lo, SQ, t_raw, t_sq, n, rope, turned, index, rq), rank)
    return t_sq


def qk_rest(p, st, raw_dst, hi, lo, SQ, t_raw, t_sq, n, rope, turned, index, rq):
    if rope:
        k = yield from st.sw.take()
        for s in range(4):
            o = s ^ 1
            t_sw = p.SP.dma(st.SW[32 * s:32 * s + 32, k, :], raw_dst[32 * o:32 * o + 32, :], st.slots[k], t_raw, st.t_sw[k])
    nt = n // 128
    small = yield from st.banks.take()
    yield [t_sq, p.bank_free[small]]
    p.PE.wait(t_sq, p.bank_free[small], st.t_tab)
    for m in range(nt):
        t = p.mm(p.bank(small, 2 * m, 2 * m + 2), SQ[:, 128 * m:128 * m + 128], p.BI[:, :], m == 0, m == nt - 1)
    c = 2 * nt
    u = yield from st.ms.take()
    MS, RS = st.MS[u][:, :c], st.RS[u][:, :c]
    yield t
    t = p.ts(MS, p.bank(small, 0, c), 1.0 / 64, EPS, ALU.mult, ALU.add, t, st.t_ms[u])
    p.leave(st.banks, small, t)
    t = p.pow(RS, MS, t, st.t_rsq[u])
    st.t_ms[u] = t
    if rope:
        yield t_sw
        t1 = p.tt(raw_dst, raw_dst, st.TAB[:, 0, :n], ALU.mult, t_raw, t_sw)
        t2 = p.tt(st.SW[:, k, :], st.SW[:, k, :], st.TAB[:, 1, :n], ALU.mult, t_sw)
        t_raw = st.t_sw[k] = p.tt(raw_dst, raw_dst, st.SW[:, k, :], ALU.add, t1, t2)
        st.sw.give(k)
    yield t
    if rq is not None:
        t_r = p.ts(rq, st.RS[u][:, :8], 0.125, None, ALU.mult, ALU.bypass, t)
        st.t_rsq[u] = t_r
        st.ms.give(u)
        turned[index] = split(p, raw_dst, hi, lo, t_raw) + [t_r]
    else:
        small = yield from st.banks.take()
        yield p.bank_free[small]
        p.PE.wait(p.bank_free[small], t)
        for m in range(nt):
            t = p.tr(p.bank(small, 128 * m, 128 * m + 128)[0:2, :], st.RS[u][:, 2 * m:2 * m + 2], m == nt - 1)
        st.t_rsq[u] = t
        st.ms.give(u)
        yield t
        yield from st.rt.take()
        t = p.act(st.RT[0:2, :n], p.bank(small, 0, n)[0:2, :], ACT.Copy, t, st.t_rt)
        yield t
        p.PE.wait(t)
        st.t_rt = t = p.mm(p.bank(small, 0, n), st.SEL[0:2, :], st.RT[0:2, :n], True, True)
        st.rt.give(0)
        yield t
        t = p.tt(raw_dst, raw_dst, p.bank(small, 0, n), ALU.mult, t, t_raw)
        p.leave(st.banks, small, t)
        turned[index] = split(p, raw_dst, hi, lo, t)


def odd_mixer(p, sx, xt, x_task, c_task, CMH, CML, ct, G):
    A = p.A
    f32 = lambda n, s, o: p.at(n, s, F32, p.BIG + o)
    f32r = lambda n, s, o: p.at(n, s, F32R, p.BIG + o)
    QH, QL, QLf = f32r("Q1H", [128, 8, NX], 0), f32r("Q1L", [128, 8, NX], 16384), f32("Q1Lf", [128, 8, NX], 16384)
    KH, KL, KLf = f32r("K1H", [128, 2, 768], 32768), f32r("K1L", [128, 2, 768], 38912), f32("K1Lf", [128, 2, 768], 38912)
    QHf, KHf = f32("Q1Hf", [128, 8, NX], 0), f32("K1Hf", [128, 2, 768], 32768)
    Y = f32("Y1", [128, 4, 1024], 45056)
    PR, PTR = f32("P1", [128, 2, 768], 61440), f32("PT1", [128, 2, 768], 67584)
    RT = f32("RT1", [128, NX], 61440)
    TAB = f32("TAB1", [128, 2, NX], 73728)
    SW = f32("SW1", [128, 2, NX], 77824)
    V = f32("V1", [128, 6, 256], 83968)
    G1 = p.const("G1", [128, 2], F32)
    SEL = f32("SEL2", [128, 128], 67584)
    RQ = p.const("RQ", [128, 8, 8], F32)
    lc = p.slot("rope1_in")
    t_prev = p.PE.last()
    for name, dst in (("rope1", TAB[:, :, :]), ("qk_g1", G1[:, :]), ("bi2", p.BI[:, :]), ("sel2", SEL[0:2, :])):
        t_tab = p.SP.dma(dst, A[name], lc, t_prev)
    st = Heads(p, SW, TAB, SEL, RT, t_tab, G, [p.slot("swap0"), p.slot("swap1")])

    def plain_v(base, t_v):
        def evac(i, b, t):
            t_v[base + i] = p.act(V[:, base + i, :], p.bank(b, 0, 256), ACT.Copy, t)
            return t_v[base + i]
        return evac

    xh, xl = (lambda k: p.XH[:, k, :]), (lambda k: p.XL[:, k, :])
    ch, cl = (lambda k: CMH[:, k, :]), (lambda k: CML[:, k, :])
    t_v, t_kx, t_kc, t_q = [None] * 6, [None] * 2, [None] * 2, [None] * 8

    def keys(out, off, n, rope, i0=0):
        def evac(i, b, t):
            i += i0
            return qk_tile(p, st, KLf[:, i, off:off + n], KHf[:, i, off:off + n], KH[:, i, off:off + n], KL[:, i, off:off + n], b, t,
                           n, G1[:, 1:2], rope, out, i, 2)
        return evac

    def queries(i0):
        def evac(i, b, t):
            i += i0
            return qk_tile(p, st, QLf[:, i, :], QHf[:, i, :], QH[:, i, :], QL[:, i, :], b, t, NX, G1[:, 0:1], True,
                           t_q, i, 2, RQ[:, i, :])
        return evac

    yield from p.gemm(2, [8], ch, cl, ct, NC, keys(t_kc, NX, NC, False), G, lead=2)
    yield from p.gemm_t([4] * 2, 256, ch, cl, ct, 2, plain_v(4, t_v), G)
    t_cm = p.PE.last()
    yield from p.gemm(2, [8], xh, xl, xt, NX, keys(t_kx, 0, NX, True), G, lead=2)
    yield from until(lambda: x_task[4])
    G.give(7)
    yield from p.gemm_t([4] * 2, 256, xh, xl, xt, 4, plain_v(0, t_v), G)
    yield from p.gemm(1, [8], xh, xl, xt, NX, queries(0), G)
    yield from until(lambda: c_task[4] and known(t_kx, t_kc))
    t_front = [p.PE.last(), p.AC.last(), p.VE.last()]
    yield from G.claim(0, 1, 2, 3)
    S2, T = Pool(0, 2), Pool(4, 5)

    NM, RS, RC = p.NM, p.RS, p.RC
    p_free, pt_free, pp, ptp = [t_front] * 2, [t_front] * 2, Pool(0, 1), Pool(0, 1)
    t_out, nm_free, rc_free = [None] * 8, {}, {}

    def back(i, t_y):
        b = yield from T.take()
        yield [p.bank_free[b], t_y]
        p.PE.wait(p.bank_free[b], t_y)
        for m in range(4):
            t = p.tr(p.bank(b, 128 * m, 128 * m + 128), Y[:, m, 128 * i:128 * i + 128], m == 3)
        yield t
        t1 = p.act(QH[:, i, :], p.bank(b), ACT.Copy, t)
        yield t1
        p.bank_free[b] = t2 = p.tt(QL[:, i, :], p.bank(b), QH[:, i, :].bitcast(F32), ALU.subtract, t1)
        T.give(b)
        t_out[i] = [t1, t2]

    def unit(n, i, j, m):
        par = i % 2
        ps = slice(64 * j, 64 * j + 64)
        kt = i // 4
        c = 2 * m + j
        s = {}

        def score():
            yield from until(lambda: known(t_q[i], t_v))
            sb = s["b"] = yield from S2.take()
            yield [p.bank_free[sb], p.bank_free[sb + 1], t_q[i]]
            p.PE.wait(p.bank_free[sb], p.bank_free[sb + 1], t_q[i], t_kx[kt], t_kc[kt])
            q = [T_[ps, i, 128 * m:128 * m + 128] for T_ in (QH, QL)]
            p.product(p.bank(sb), q, [T_[ps, kt, 0:512] for T_ in (KH, KL)], True)
            s["t"] = p.product(p.bank(sb + 1, 0, 256), q, [T_[ps, kt, 512:768] for T_ in (KH, KL)], True, True)

        def soft():
            yield s["t"]
            a = s["p"] = yield from pp.take()
            Pr = PR[:, a, :]
            sb = s["b"]
            S = p.psum[:, 512 * sb:512 * sb + 768]
            nm = NM[:, par, c:c + 1]
            t = p.reduce_max(nm, S, False, s["t"], nm_free.get((par, c)))
            t = p.ts(nm, nm, RQ[:, i, c:c + 1], -1.0, ALU.mult, ALU.mult, t)
            yield t
            s["e"] = p.act(Pr, S, ACT.Exp, t, p_free[a], rc_free.get(par), scale=RQ[:, i, c:c + 1], bias=nm,
                           accum_out=RS[:, par, c:c + 1])
            nm_free[par, c] = p.bank_free[sb] = p.bank_free[sb + 1] = s["e"]
            S2.give(sb)

        def turn():
            yield s["e"]
            Pr = PR[:, s["p"], :]
            a = s["pt"] = yield from ptp.take()
            Pt = PTR[:, a, :]
            for h in range(2):
                b = yield from T.take()
                yield p.bank_free[b]
                p.PE.wait(p.bank_free[b], s["e"])
                for k in range(3):
                    kk = 3 * h + k
                    t = p.tr(p.bank(b, 128 * k, 128 * k + 128), Pr[:, 128 * kk:128 * kk + 128], k == 2)
                o, src = Pt[:, 384 * h:384 * h + 384], p.bank(b, 0, 384)
                if h == 1:
                    p_free[s["p"]] = t
                    pp.give(s["p"])
                    yield t
                if h == 0:
                    s["p0"] = p.bank_free[b] = p.act(o, src, ACT.Copy, t, pt_free[a])
                else:
                    s["p1"] = p.bank_free[b] = p.copy(o, src, t, pt_free[a])
                T.give(b)

        def value():
            first, last = j == 0 and m == 0, j == 1 and m == 3
            Pt = PTR[:, s["pt"], :]
            yield [s["p0"], s["p1"], p.bank_free[6] if first else None]
            if first:
                p.PE.wait(p.bank_free[6], t_v)
            o = p.bank(6, 128 * m + 64 * j, 128 * m + 64 * j + 64)
            hs = slice(64 * (2 * kt + j), 64 * (2 * kt + j) + 64)
            p.PE.wait(s["p0"], s["p1"])
            for k in range(6):
                t = p.mm(o, Pt[:, 128 * k:128 * k + 128], V[:, k, hs], first and k == 0, k == 5)
            pt_free[s["pt"]] = t
            ptp.give(s["pt"])
            if last:
                yield t
                t1 = p.recip(RC[:, par, :], RS[:, par, :], s["e"], rc_free.get(par))
                t2 = rc_free[par] = p.tt(Y[:, :, 128 * i:128 * i + 128].rearrange("p m (j d) -> p m j d", j=2),
                          p.bank(6).rearrange("p (m j d) -> p m j d", m=4, j=2),
                          RC[:, par, :].rearrange("p (m j) -> p m j", j=2).unsqueeze(3).broadcast_to([128, 4, 2, 64]),
                          ALU.mult, t, t1, t_cm)
                p.bank_free[6] = t2
                p.spawn(back(i, t2), 3)

        return score, soft, turn, value

    done = p.flow([unit(8 * i + 4 * j + m, i, j, m) for i in range(8) for j in range(2) for m in range(4)], 4)
    p.mix(0.2)
    yield from p.gemm(7, [8], xh, xl, xt, NX, queries(1), G)
    yield from until(done)
    p.mix(None)
    for b in range(4):
        G.give(b)
    yield from G.claim(7)
    return QH, QL, t_out


PI = math.pi
MAGIC = 1.5 * 2.0 ** 23
THRESHOLDS = [k if k < 16 else math.ceil(16 * 2 ** (3 * (k - 16) / 16) - 1e-9) for k in range(1, 32)]


def pieces(x, bits, count):
    out = []
    for _ in range(count):
        e = math.floor(math.log2(x)) - bits + 1
        q = math.floor(x / 2.0 ** e) * 2.0 ** e
        out.append(q)
        x -= q
    return out + [x]


def positions(p, scratch):
    A = p.A
    base, base2 = 16384, p.crow_off + 4096
    t0 = [p.AC.last(), p.VE.last(), p.PE.last()]
    sl = p.slot("pos_in")
    PB = p.at("PB", [128, NX], I32, base)
    AN, NN = p.at("AN", [128, NX], F32, base + 2048), p.at("NN", [128, NX], F32, base + 4096)
    FQ = p.at("FQ", [128, 4], F32, base + 6144)
    p.SP.dma(PB[0:64, :], A["pos_row"], sl, *t0)
    t = p.SP.dma(FQ[0:64, :], A["freq"], sl)
    yield p.spare(t)
    an, nn, fq = AN[0:64, :], NN[0:64, :], FQ[0:64, :]
    t = p.ts(an, PB[0:64, :], fq[:, 0:1], None, ALU.mult, ALU.bypass, t)
    yield p.spare()
    for scale, parts in ((4096.0, pieces(2 * PI, 7, 4)), (1.0, pieces(2 * PI, 12, 2))):
        if scale == 1.0:
            t1 = p.ts(nn, an, 1 / (2 * PI), fq[:, 2:3], ALU.mult, ALU.add, t)
            t1 = p.ts(nn, nn, MAGIC, None, ALU.add, ALU.bypass, t1)
        else:
            t1 = p.ts(nn, an, 1 / (2 * PI * scale), MAGIC, ALU.mult, ALU.add, t)
        yield p.spare()
        t1 = p.ts(nn, nn, MAGIC, None, ALU.subtract, ALU.bypass, t1)
        yield p.spare()
        for c in parts:
            t1 = t = p.stt(an, nn, -c * scale, an, ALU.mult, ALU.add, t1)
            yield p.spare()
    t = p.ts(an, an, fq[:, 1:2], 3.1415925, ALU.add, ALU.min, t)
    t = p.ts(an, an, -3.1415925, None, ALU.max, ALU.bypass, t)
    yield p.spare()
    t = p.act(nn, an, ACT.Sin, t)
    t = p.ts(nn, nn, fq[:, 3:4], None, ALU.mult, ALU.bypass, t)
    so = p.slot("rope_out")
    p.t_rope2 = t_rope = p.SP.dma(scratch["rope"], nn, so, t)
    yield p.spare()
    PQ = p.at("PQ", [128, 4, 129], I32, base)
    HI, LO = p.at("HI", [128, 4, 129], I32, base + 2080), p.at("LO", [128, 4, 129], I32, base + 4160)
    RH, RL = p.at("RH", [128, 4, 128], F32, base2), p.at("RL", [128, 4, 128], F32, base2 + 2048)
    N = p.at("NREL", [128, 4, 128], F32, base)
    t = p.SP.dma(PQ[:, :, :], A["pos_win"], sl, t_rope, t)
    yield p.spare(t)
    t1 = p.dve(lambda e: e.tensor_scalar(HI[:, :, :], PQ[:, :, :], 16, None, ALU.arith_shift_right), HI[:, :, :], t)
    t2 = p.dve(lambda e: e.tensor_scalar(LO[:, :, :], PQ[:, :, :], 65535, None, ALU.bitwise_and), LO[:, :, :], t)
    yield p.spare()
    t1 = p.tt(RH[:, :, :], HI[:, :, 128:129].broadcast_to([128, 4, 128]), HI[:, :, 0:128], ALU.subtract, t1)
    t2 = p.tt(RL[:, :, :], LO[:, :, 128:129].broadcast_to([128, 4, 128]), LO[:, :, 0:128], ALU.subtract, t2)
    yield p.spare()
    t_n = p.stt(N[:, :, :], RH[:, :, :], 65536.0, RL[:, :, :], ALU.mult, ALU.add, t1, t2)
    TB, DT = p.at("TB", [128, 32, 6], F32, base2), p.at("DT", [128, 31, 6], F32, base2 + 1024)
    MK = p.at("MASK", [128, 2, 4, 128], BF16, base2 + 2048)
    ACC = p.at("ACC", [128, 3, 4, 128], F32, base + 2048)
    t = p.SP.dma(TB[:, :, :], A["rel_bias"], sl, t_n)
    yield p.spare(t)
    t_dt = p.tt(DT[:, :, :], TB[:, 1:32, :], TB[:, 0:31, :], ALU.subtract, t)
    yield p.spare()
    sb = [p.slot(f"bias{i}_out") for i in range(6)]
    t_pre = []
    for h in range(6):
        t_pre.append(p.SP.dma(scratch["bias"][h], A["mask_fill"], sb[h]))
    t_out = [None] * 6
    for half in range(2):
        t_acc = []
        for h in range(3):
            hh = 3 * half + h
            t_acc.append(p.ts(ACC[:, h, :, :], N[:, :, :], 0.0, TB[:, 0, hh:hh + 1], ALU.mult, ALU.add, t_n, t,
                              t_out[hh - 3] if half else None))
        yield p.spare()
        for b, thr in enumerate(THRESHOLDS):
            m = MK[:, b % 2, :, :]
            t_m = p.ts(m, N[:, :, :], float(thr), None, ALU.is_ge, ALU.bypass, t_n)
            yield p.spare()
            for h in range(3):
                hh = 3 * half + h
                a = ACC[:, h, :, :]
                t_acc[h] = p.stt(a, m, DT[:, b, hh:hh + 1], a, ALU.mult, ALU.add, t_m, t_dt, t_acc[h])
                yield p.spare()
        for h in range(3):
            hh = 3 * half + h
            t_out[hh] = p.SP.dma(scratch["skew"][hh], ACC[:, h, :, :], sb[hh], t_acc[h], t_pre[hh])
            yield p.spare()
    p.t_bias2 = t_out


def derive2(p, layer, kind):
    if (layer, kind) in p.t_der2:
        return p.t_der2[layer, kind]
    chunk = (1, 4, 7, 2, 5, 8)[kind]
    deps = p.modulation(p.t_ada2, (layer, chunk))
    ada = p.ADA2[:, layer, chunk * 8:chunk * 8 + 8]
    out = p.DER2[:, layer, kind, :]
    if kind < 3:
        t = p.stt(out, ada, 1.0, p.NG2[:, layer, kind, :], ALU.add, ALU.mult, deps)
    else:
        t = p.ts(out, ada, 1.0 if kind == 4 else 0.5, None, ALU.mult, ALU.bypass, deps)
    p.t_der2[layer, kind] = t
    return t


class Block2:

    def __init__(self, p, s):
        self.p, self.t_res, self.small, self.rb = p, s.t_res, s.small, s.rb
        self.t_r = s.t_r

    def norm(self, layer, kind, hi, lo, lof, out, war=None):
        p = self.p
        t_g = derive2(p, layer, kind)
        p.quiet += 1
        yield self.t_sum
        p.PE.wait(p.bank_free[self.small])
        tk = p.ssq_part(self.sum, NX, True, self.small, self.t_sum)
        yield self.t_last
        tk = p.ssq_part(self.last, NX, False, self.small, self.t_last)
        self.t_r = yield from p.rsq(tk, NX, 1024, self.small)
        yield from self.modulate(layer, kind, hi, lo, lof, out, war)
        p.quiet -= 1

    def modulate(self, layer, kind, hi, lo, lof, out, war=None):
        p = self.p
        t_mod = [derive2(p, layer, kind)] + p.modulation(p.t_ada2, (layer, 3 * kind))
        t_rb = yield from p.spread(self.t_r, NX, self.rb)
        yield from p.apply(lambda k: p.X[:, k, :], lambda k: self.t_res[k], NX,
                           lambda k: p.DER2[:, layer, kind, k:k + 1],
                           lambda k: p.ADA2[:, layer, 24 * kind + k:24 * kind + k + 1], lambda k: t_mod,
                           lambda k: hi[:, k, :], lambda k: lo[:, k, :], lambda k: lof[:, k, :], self.rb, t_rb, war, out)

    def adder(self, layer, kind, sq, war=None):
        p = self.p
        t_g = derive2(p, layer, kind)
        free = [None] * 8

        def evac(i, b, t):
            x = p.X[:, i, :]
            t = self.t_res[i] = p.stt(x, p.bank(b), p.DER2[:, layer, kind, i:i + 1], x, ALU.mult, ALU.add, t, t_g,
                                      self.t_res[i])
            if sq is None:
                p.SP.dma(p.A["out"][:, i, :], x, p.outputs[0], t)
            elif i == 0:
                self.sum = sq[:, 0, :]
                self.t_sum = p.act(self.sum, x, ACT.Square, t, war)
            elif i == KC - 1:
                self.last = sq[:, 1, :]
                self.t_last = p.act(self.last, x, ACT.Square, t, war, free[1])
            else:
                m = 1 + (i - 1) % 2
                t2 = p.act(sq[:, m, :], x, ACT.Square, t, war, free[m])
                self.t_sum = free[m] = p.tt(self.sum, self.sum, sq[:, m, :], ALU.add, t2, self.t_sum)
            return t
        return evac


def up_glu(p, xh, xl, xt, H, war, banks, lead):
    HH, HL, HHf, HLf = H
    t_h = [None] * FC
    late = deque()
    t_g = {}

    def high(j, t):
        t = p.act(HH[:, j, :], HLf[:, j, :], ACT.Copy, t)
        late.append(lambda: low(j, t))

    def low(j, t):
        t_h[j] = [t, p.tt(HL[:, j, :], HLf[:, j, :], HH[:, j, :].bitcast(F32), ALU.subtract, t)]

    def evac(i, b, t):
        j = i // 2
        for _ in range(len(late)):
            late.popleft()()
        if i % 2 == 0:
            t_g[j] = p.act(HLf[:, j, :], p.bank(b), ACT.Silu, t, war)
            return t_g[j]
        t = p.tt(HLf[:, j, :], HLf[:, j, :], p.bank(b), ALU.mult, t, t_g[j])
        late.append(lambda: high(j, t))
        return t

    yield from p.gemm(2 * FC, [8], xh, xl, xt, NX, evac, banks, lead=lead)
    while late:
        late.popleft()()
    p.t_h = t_h


def mixer2(p, G, layer, xh, xl, xt, x_task, scratch):
    A = p.A
    L = str(layer)
    at = lambda n, s, d, o: p.at(n + L, s, d, o)
    f32 = lambda n, s, o: at(n, s, F32, p.BIG + o)
    f32r = lambda n, s, o: at(n, s, F32R, p.BIG + o)

    def trio(name, tiles, o, cols=NX):
        return (f32r(name + "H", [128, tiles, cols], o), f32r(name + "L", [128, tiles, cols], o + 4 * tiles * cols),
                f32(name + "f", [128, tiles, cols], o + 4 * tiles * cols), f32(name + "g", [128, tiles, cols], o))

    CQ, CKV, QS, KS = trio("CQ", 2, 0), trio("CKV", 1, 8192), trio("QS", 3, 12288), trio("KS", 1, 24576)
    V, VA, Y = f32("V2", [128, 4, 384], 28672), f32("VA2", [128, 4, 384], 34816), f32("Y2", [128, 4, 1024], 40960)
    BW = [f32("BW0", [128, 4, 256], 57344), f32("BW1", [128, 4, 256], 61440)]
    PR, PTR = f32("P2", [128, 2, 512], 65536), f32("PT2", [128, 2, 512], 69632)
    GT, KR = f32("GT", [128, NX], 73728), f32("KR", [128, NX], 75776)
    MQ = [trio("MQa", 1, 77824), trio("MQb", 1, 81920)]
    cb = 16384 - p.BIG
    MK = [trio("MKa", 1, 86016), trio("MKb", 1, cb + 4096)]
    BQ, BK = trio("BQ", 2, 0), [trio("BKa", 1, 8192), trio("BKb", 1, 73728)]
    W4 = [at("W%d" % i, [128, NX], F32, p.XM + o) for i, o in enumerate((11264, 13312, 27648, 29696))]
    LN = [at("LN%d" % i, [128, 1280], F32, p.XM + o) for i, o in enumerate((6144, 22528))]
    lo_of = (0, 512, 896, 1152)
    K2 = f32("K2", [128, 6, 128], cb)
    G2 = f32("G2", [128, 24], cb + 3072)
    RT = f32("RT2", [128, NX], p.crow_off + 4096 - p.BIG)
    JK = f32("JK", [128, 384], p.crow_off + 6144 - p.BIG)
    smalls = [cb + 3168]

    def small(name, cols):
        t = f32(name, [128, cols], smalls[0])
        smalls[0] += (4 * cols + 31) // 32 * 32
        assert smalls[0] <= cb + 4096
        return t

    RQ, RCQ, MSm, RSm, RQ2, ES, SS, KE = (small(n, c) for n, c in (
        ("RQm", 24), ("RCQ", 8), ("MSm", 8), ("RSm", 8), ("RQ2", 24), ("ES", 16), ("SS", 8), ("KE", 4)))
    FOLD, TRI, M01, CAUS, ONE, SEL = (K2[:, i, :] for i in range(6))
    prev = [p.PE.last(), p.AC.last(), p.VE.last()]
    sc = p.slot("mix_in" + L)
    p.SP.dma(K2[:, :, :], A["k2"], sc, *prev)
    p.SP.dma(G2[:, :], A["g2"][layer], sc)
    p.SP.dma(GT[64:128, :], scratch["rope"], sc, p.t_rope2)
    t_k2 = p.SP.dma(KR[0:64, :], scratch["rope"], sc)
    col = lambda c: G2[:, c:c + 1]
    t_gt, t_tk = [], []

    def tables():
        yield t_k2
        t_one = p.dve(lambda e: e.memset(GT[0:64, :], 1.0), GT[0:64, :], *prev)
        t_gt.append(p.ts(GT[:, :], GT[:, :], col(0), None, ALU.mult, ALU.bypass, t_one, t_k2))
        t_tk.append(p.ts(KR[0:64, :], KR[0:64, :], G2[0:64, 2:3], None, ALU.mult, ALU.bypass, t_k2))
    p.spawn(tables(), 2)
    st = Heads(p, None, None, SEL, RT, t_k2, G)

    t_cq, t_ckv, t_rcq = [None] * 2, [None], []
    sqs = []

    def latent(i, b, t):
        src = p.bank(b)
        T, k, gain = (CQ, i, col(3 + i)) if i < 2 else (CKV, 0, col(5))
        t1 = p.act(T[2][:, k, :], src, ACT.Copy, t, t_k2, scale=gain)
        sqs.append((T[3][:, k, :], t1))
        sqs[i] = (sqs[i][0], t1, p.act(sqs[i][0], src, ACT.Square, t))
        if i == 1:
            p.spawn(latent_q(), 1)
        if i == 2:
            p.spawn(latent_kv(), 1)
        return sqs[i][2]

    def latent_q():
        b = yield from G.take()
        yield [sqs[0][2], sqs[1][2], p.bank_free[b]]
        p.PE.wait(p.bank_free[b], sqs[0][2], sqs[1][2])
        for i in range(2):
            for m in range(4):
                t = p.mm(p.bank(b, m, m + 1), sqs[i][0][:, 128 * m:128 * m + 128], p.ones[:, 0:1], i == 0 and m == 0,
                         i == 1 and m == 3)
        yield t
        t = p.ts(RCQ[:, 4:8], p.bank(b, 0, 4), 1.0 / 256, EPS, ALU.mult, ALU.add, t)
        p.leave(G, b, t)
        for i in range(2):
            t_cq[i] = split(p, CQ[2][:, i, :], CQ[0][:, i, :], CQ[1][:, i, :], sqs[i][1], t)
        t = p.pow(RCQ[:, 0:4], RCQ[:, 4:8], t)
        yield t
        t = p.tt(RCQ[:, 4:8], RCQ[:, 0:4], RCQ[:, 0:4], ALU.mult, t)
        t = p.ts(RCQ[:, 4:8], RCQ[:, 4:8], 1.0 / 96, None, ALU.mult, ALU.bypass, t)
        t_rcq.append(p.ts(RCQ[:, 0:4], RCQ[:, 0:4], 96.0 ** -0.5, None, ALU.mult, ALU.bypass, t))

    def latent_kv():
        b = yield from G.take()
        yield [sqs[2][2], p.bank_free[b]]
        p.PE.wait(p.bank_free[b])
        tk = p.ssq_part(sqs[2][0], NX, True, b, sqs[2][2])
        t = yield from p.rsq(tk, NX, 128, b, 4)
        G.give(b)
        b = yield from G.take()
        t = yield from p.spread(t, NX, b, 4)
        yield t
        t = p.tt(CKV[2][:, 0, :], CKV[2][:, 0, :], p.bank(b), ALU.mult, t, sqs[2][1])
        p.leave(G, b, t)
        t_ckv[0] = split(p, CKV[2][:, 0, :], CKV[0][:, 0, :], CKV[1][:, 0, :], t)

    t_kr = [None] * 2

    def kpe(b, t):
        src = p.bank(b)
        SQ = MQ[0][2][0:32, 0, :]
        t_s = p.act(SQ, src[0:32, :], ACT.Square, t)
        yield from until(lambda: t_tk)
        t1 = p.tt(KR[0:64, :], src[0:64, :], KR[0:64, :], ALU.mult, t_s, t_tk)
        p.leave(G, b, t1)
        b = yield from G.take()
        yield [t_s, p.bank_free[b]]
        p.PE.wait(p.bank_free[b], t_s)
        for m in range(4):
            t = p.mm(p.bank(b, m, m + 1), SQ[:, 128 * m:128 * m + 128], p.ones[0:32, 0:1], m == 0, m == 3)
        yield t
        t_kr[0] = p.ts(KE[:, :], p.bank(b, 0, 4), 1.0 / 96, EPS, ALU.mult, ALU.add, t)
        p.leave(G, b, t_kr[0])
        b = yield from G.take()
        yield [t1, p.bank_free[b]]
        p.PE.wait(p.bank_free[b], t1)
        t = p.mm(p.bank(b), FOLD[0:64, :], KR[0:64, :], True, True)
        yield t
        t_kr[1] = p.act(KR[64:128, :], p.bank(b)[64:128, :], ACT.Copy, t)
        p.leave(G, b, t_kr[1])

    t_v, t_va = [None] * 4, [None] * 4

    def vals(dst, t_dst):
        def evac(i, b, t):
            t_dst[i] = p.act(dst[:, i, :], p.bank(b, 0, 384), ACT.Copy, t)
            return t_dst[i]
        return evac

    yield from p.gemm(3, [8], xh, xl, xt, NX, latent, G, lead=3)
    b = yield from G.take()
    w, hi, lo, t_hi, t_lo = yield from p.weights()
    yield [p.bank_free[b], t_hi, t_lo]
    p.PE.wait(p.bank_free[b], t_hi, t_lo)
    o = p.bank(b)[0:64, :]
    for part, wt in ((0, hi), (1, hi), (2, lo)):
        for k in range(8):
            p.PE.wait(xt(k))
            t = p.mm(o, wt[:, 64 * k:64 * k + 64], (xl if part == 1 else xh)(k), part == 0 and k == 0,
                     part == 2 and k == 7)
            yield
    p.w_done[w] = t
    p.spawn(kpe(b, t), 2)
    yield from until(lambda: x_task[4])
    for b in (6, 7):
        G.give(b)
    yield from p.gemm_t([2] * 4, 384, xh, xl, xt, 4, vals(V, t_v), G)

    yield from until(lambda: known(t_ckv))
    w, hi, lo, t_hi, t_lo = yield from p.weights()
    yield [t_ckv, t_lo]
    for m in range(4):
        b = yield from G.take()
        yield p.bank_free[b]
        p.PE.wait(t_hi, t_lo, t_ckv, p.bank_free[b])
        ck = [T[:, 0, 128 * m:128 * m + 128] for T in CKV[:2]]
        t = p.product(p.bank(b, 0, 384), ck, (hi[:, 0:384], lo[:, 0:384]), True, True)
        if m == 3:
            p.w_done[w] = t
        p.leave(G, b, vals(VA, t_va)(m, b, t))
        yield

    q_ok, k_ok, s_read = {}, {}, {}
    ms_free, ms = [None, None], Pool(0)

    def head(h):
        yield from until(lambda: h < 2 or h - 2 in s_read)
        w, hi, lo, t_hi, t_lo = yield from p.weights()
        yield from until(lambda: known(t_cq, t_ckv))
        bq = yield from G.take()
        yield [p.bank_free[bq], t_hi, t_lo, t_cq]
        p.PE.wait(p.bank_free[bq], t_hi, t_lo, t_cq)
        for k in range(2):
            ws = slice(128 * k, 128 * k + 128)
            p.mm(p.bank(bq), hi[:, ws], CQ[0][:, k, :], k == 0)
            p.mm(p.bank(bq), hi[:, ws], CQ[1][:, k, :], False)
            yield
        for k in range(2):
            t_q = p.mm(p.bank(bq), lo[:, 128 * k:128 * k + 128], CQ[0][:, k, :], False, k == 1)
        bk = yield from G.take()
        yield [p.bank_free[bk], t_ckv]
        p.PE.wait(p.bank_free[bk], t_ckv)
        t_k = p.product(p.bank(bk)[0:64, :], (hi[:, 256:320], lo[:, 256:320]), (CKV[0][:, 0, :], CKV[1][:, 0, :]), True, True)
        p.w_done[w] = t_k
        p.spawn(head_rest(h, bq, bk, t_q, t_k), 2)
        if h == 5:
            t_latent.append(t_k)

    def head_rest(h, bq, bk, t_q, t_k):
        mq, mk = MQ[h % 2], MK[h % 2]
        war = s_read.get(h - 2)
        SQ, SK = mq[3][:, 0, :], mk[3][:, 0, :]
        yield from until(lambda: t_gt and known(t_kr))
        t_sq = p.act(SQ[0:96, :], p.bank(bq)[0:96, :], ACT.Square, t_q, war)
        t_sk = p.act(SK[0:64, :], p.bank(bk)[0:64, :], ACT.Square, t_k, war)
        t_kg = p.act(mk[2][0:64, 0, :], p.bank(bk)[0:64, :], ACT.Copy, t_k, war, scale=G2[0:64, 1:2])
        p.leave(G, bk, t_kg)
        t_kc = p.act(mk[2][64:128, 0, :], KR[64:128, :], ACT.Copy, t_kr, war)
        if h == 5:
            t_latent.append(t_kc)
        yield t_sq
        t_q = p.tt(mq[2][:, 0, :], p.bank(bq), GT[:, :], ALU.mult, t_sq, t_gt, war)
        p.leave(G, bq, t_q)
        if h == 5:
            t_latent.append(t_q)
        b = yield from G.take()
        yield [t_sk, p.bank_free[b]]
        p.PE.wait(p.bank_free[b], t_sq, t_sk)
        for m in range(4):
            p.mm(p.bank(b, m, m + 1), SQ[0:96, 128 * m:128 * m + 128], p.ones[0:96, 0:1], m == 0)
        for m in range(4):
            t = p.mm(p.bank(b, 4 + m, 5 + m), SK[0:64, 128 * m:128 * m + 128], p.ones[0:64, 0:1], False, m == 3)
        yield from ms.take()
        yield from until(lambda: t_rcq)
        yield t
        t1 = p.tt(MSm[:, 0:4], p.bank(b, 0, 4), RCQ[:, 4:8], ALU.mult, t, t_rcq, ms_free[0])
        t2 = p.stt(MSm[:, 4:8], p.bank(b, 4, 8), 1.0 / 96, KE[:, :], ALU.mult, ALU.add, t, t_kr)
        p.leave(G, b, t2)
        t1 = p.ts(MSm[:, 0:4], MSm[:, 0:4], EPS, None, ALU.add, ALU.bypass, t1)
        t = ms_free[0] = p.pow(RSm[:, :], MSm[:, :], t1, t2, ms_free[1])
        q_split = split(p, mq[2][:, 0, :], mq[0][:, 0, :], mq[1][:, 0, :], t_q, t2, war)
        b = yield from G.take()
        yield [t, p.bank_free[b]]
        t_rq = p.tt(RQ[:, 4 * h:4 * h + 4], RSm[:, 0:4], RCQ[:, 0:4], ALU.mult, t)
        q_ok[h] = q_split + [t_rq]
        p.PE.wait(p.bank_free[b], t)
        for m in range(4):
            t = p.mm(p.bank(b, 128 * m, 128 * m + 128), RSm[:, 4 + m:5 + m].broadcast_to([128, 128]), p.ident[:, :],
                     m == 0, m == 3)
        ms_free[1] = [t, t_rq]
        ms.give(0)
        yield t
        t = p.tt(mk[2][:, 0, :], mk[2][:, 0, :], p.bank(b), ALU.mult, t, t_kg, t_kc, war)
        p.leave(G, b, t)
        k_ok[h] = split(p, mk[2][:, 0, :], mk[0][:, 0, :], mk[1][:, 0, :], t, war)

    t_latent = []
    qs_ok, ks_ok, bq_ok, bk_ok = [None] * 3, [None], [None] * 2, [None] * 2

    def tiles(kind, i):
        def evac(_, b, t):
            if kind in "qk":
                T, ok = (QS, qs_ok) if kind == "q" else (KS, ks_ok)
                return qk_tile(p, st, T[2][:, i, :], T[3][:, i, :], T[0][:, i, :], T[1][:, i, :], b, t, NX, col(6 if kind == "q" else 7),
                               False, ok, i, 2, RQ2[:, 8 * i:8 * i + 8] if kind == "q" else None)
            T, k, ok = (BQ, i, bq_ok) if kind == "Q" else (BK[i], 0, bk_ok)
            t1 = p.act(T[2][:, k, :], p.bank(b), ACT.Copy, t, t_latent, scale=0.125 if kind == "Q" else 1.0)
            p.spawn(late_split(T, k, ok, i, t1), 2)
            return t1

        def late_split(T, k, ok, i, t1):
            yield t1
            ok[i] = split(p, T[2][:, k, :], T[0][:, k, :], T[1][:, k, :], t1)
        yield from p.gemm(1, [8], xh, xl, xt, NX, evac, G)

    yield from head(0)
    yield from tiles("q", 0)
    yield from head(1)
    yield from tiles("k", 0)
    yield from G.claim(0, 1, 2, 3)
    B4, YP = Pool(0, 1, 2, 3), Pool(4, 5)
    pp, ptp, p_free, pt_free = Pool(0, 1), Pool(0, 1), [None] * 2, [None] * 2
    NM, RS, RC = p.NM, p.RS, p.RC
    nm_free, rc_free, es_free, y_of, t_y = {}, {}, [None, None], {}, {}
    order = [0, 3, 1, 4, 2, 5]
    lb = [p.slot("bw0_in" + L), p.slot("bw1_in" + L)]
    t_bias = {}
    bi = {h: BW[k % 2] for k, h in enumerate(order)}

    def load_bias2(k, *tickets):
        if k < 6:
            h = order[k]
            t_bias[h] = p.SP.dma(BW[k % 2][:, :, :], scratch["bias"][h].rearrange("q (m k) -> q m k", m=4), lb[k % 2],
                                 p.t_bias2[h], *tickets)

    load_bias2(0, *prev)
    load_bias2(1)

    def soft_unit(kind, n, i, j, m):
        s = {}
        par = i % 2
        cc = 2 * m + j
        row = par + (2 if kind == "w" else 0)
        nm, rs = NM[:, row, cc:cc + 1], RS[:, row, cc:cc + 1]
        keys = 128 * (m + 1) if kind == "m" else (128 if m == 0 else 256)
        k0 = 0 if kind == "m" or m == 0 else 128 * (m - 1)
        h = 2 * i + j
        first, last = j == 0 and m == 0, j == 1 and m == 3

        def score():
            if kind == "m":
                yield from until(lambda: h in k_ok)
                deps = [q_ok[h], k_ok[h]]
                q = [T[:, 0, 128 * m:128 * m + 128] for T in MQ[h % 2][:2]]
                k = [T[:, 0, 0:max(keys, 256)] for T in MK[h % 2][:2]]
            else:
                yield from until(lambda: known(qs_ok[i], ks_ok[0]))
                deps = [qs_ok[i], ks_ok[0]]
                ps = slice(64 * j, 64 * j + 64)
                q = [T[ps, i, 128 * m:128 * m + 128] for T in QS[:2]]
                k = [T[ps, 0, k0:k0 + 256] for T in KS[:2]]
            sb = s["b"] = yield from B4.take(1)
            yield [p.bank_free[sb], deps]
            p.PE.wait(p.bank_free[sb], deps)
            s["t"] = p.product(p.bank(sb, 0, max(keys, 256)), q, k, True, True)
            if kind == "m" and m == 3:
                s_read[h] = s["t"]

        def soft():
            a = s["p"] = yield from pp.take()
            yield s["t"]
            sb, Pr, fr = s["b"], PR[:, s["p"], :], p_free[a]
            t0 = [s["t"], nm_free.get((row, cc))]
            if kind == "m":
                S = p.bank(sb, keys - 128, keys)
                rq = RQ[:, 4 * h + m:4 * h + m + 1]
                if m:
                    m0 = MX[:, par, cc:cc + 1]
                    t = p.reduce_max(m0, p.bank(sb, 0, keys - 128), False, t0)
                    t = p.ttr(S, S, CAUS, 1.0, m0, ALU.add, ALU.max, nm, t, t_k2)
                else:
                    t = p.ttr(S, S, CAUS, 1.0, -3e38, ALU.add, ALU.max, nm, t0, t_k2)
                t = p.ts(nm, nm, rq, -1.0, ALU.mult, ALU.mult, t)
                yield t
                s["e"] = p.act(Pr[:, :keys], p.bank(sb, 0, keys), ACT.Exp, t, fr, rc_free.get(row), scale=rq, bias=nm,
                               accum_out=rs)
            else:
                S = p.bank(sb, 0, keys)
                hd = i + 3 * j
                rq = RQ2[:, 8 * i + cc:8 * i + cc + 1]
                yield t_bias[hd]
                b = bi[hd][:, m, 256 - keys:256]
                t = p.stt(S, S, rq, b, ALU.mult, ALU.add, t0, t_bias[hd])
                if m == 3:
                    load_bias2(order.index(hd) + 2, t)
                t = p.reduce_max(nm, S, False, t)
                t = p.ts(nm, nm, G2[:, 8 + hd:9 + hd], -1.0, ALU.max, ALU.mult, t)
                yield t
                s["es"] = p.act(ES[:, 8 * par + cc:8 * par + cc + 1], nm, ACT.Exp, t, es_free[par], bias=G2[:, 8 + hd:9 + hd])
                s["e"] = p.act(Pr[:, :keys], S, ACT.Exp, t, fr, rc_free.get(row), bias=nm, accum_out=rs)
            nm_free[row, cc] = p.bank_free[sb] = s["e"]
            B4.give(sb)

        def turn():
            yield s["e"]
            b = yield from B4.take()
            yield p.bank_free[b]
            p.PE.wait(p.bank_free[b], s["e"])
            nk = keys // 128
            for k in range(nk):
                t = p.tr(p.bank(b, 128 * k, 128 * k + 128), PR[:, s["p"], 128 * k:128 * k + 128], k == nk - 1)
            p_free[s["p"]] = t
            pp.give(s["p"])
            a = s["pt"] = yield from ptp.take()
            yield [t, pt_free[a]]
            o = PTR[:, a, :keys]
            if n % 2:
                t = p.act(o, p.bank(b, 0, keys), ACT.Copy, t, pt_free[a])
            else:
                t = p.copy(o, p.bank(b, 0, keys), t, pt_free[a])
            s["tt"] = t
            p.leave(B4, b, t)

        def value():
            src, tv, hs = (VA, t_va, 64 * h) if kind == "m" else (V, t_v, 64 * j)
            if first:
                y_of[kind] = yield from YP.take()
            yb = y_of[kind]
            yield [s["tt"], p.bank_free[yb]]
            if first:
                p.PE.wait(p.bank_free[yb], tv)
            p.PE.wait(s["tt"])
            o = p.bank(yb, 64 * cc, 64 * cc + 64)
            nk = keys // 128
            for k in range(nk):
                t = p.mm(o, PTR[:, s["pt"], 128 * k:128 * k + 128], src[:, k0 // 128 + k, hs:hs + 64], first and k == 0, k == nk - 1)
            pt_free[s["pt"]] = t
            ptp.give(s["pt"])
            if last:
                yield t
                tr = s["e"]
                if kind == "w":
                    tr = es_free[par] = p.tt(RS[:, row, :], RS[:, row, :], ES[:, 8 * par:8 * par + 8], ALU.add, s["e"], s["es"])
                t1 = p.recip(RC[:, row, :], RS[:, row, :], tr, rc_free.get(row))
                f = 128 * i + (384 if kind == "w" else 0)
                t2 = p.tt(Y[:, :, f:f + 128].rearrange("p m (j d) -> p m j d", j=2),
                          p.bank(yb).rearrange("p (m j d) -> p m j d", m=4, j=2),
                          RC[:, row, :].rearrange("p (m j) -> p m j", j=2).unsqueeze(3).broadcast_to([128, 4, 2, 64]),
                          ALU.mult, t, t1)
                rc_free[row] = t_y[f // 128] = t2
                p.leave(YP, yb, t2)

        return score, soft, turn, value

    w4, w_free, ln_free = Pool(0, 1, 2, 3), [None] * 4, [None, None]
    lns = {}

    def stick_unit(n, h, kc):
        i, ps = h // 2, slice(64 * (h % 2), 64 * (h % 2) + 64)
        w = NX - 128 * kc
        wz = max(w, 256)
        L_ = LN[h % 2]
        ln = L_[:, lo_of[kc]:lo_of[kc] + w]
        s = {}

        def score():
            yield from until(lambda: known(bq_ok[i], bk_ok[i]))
            zb = s["b"] = yield from B4.take(1)
            yield [p.bank_free[zb], bq_ok[i], bk_ok[i]]
            p.PE.wait(p.bank_free[zb], bq_ok[i], bk_ok[i])
            s["t"] = p.product(p.bank(zb, 0, wz), [T[ps, 0, 128 * kc:128 * kc + 128] for T in BK[i][:2]],
                               [T[ps, i, NX - wz:NX] for T in BQ[:2]], True, True)

        def soft():
            a = s["w"] = yield from w4.take()
            yield s["t"]
            e, z = W4[a][:, :w], p.bank(s["b"], wz - w, wz)
            t = p.act(e, z, ACT.Abs, s["t"], w_free[a], t_xm)
            t = p.act(e, e, ACT.Exp, t, scale=-1.0)
            t = p.act(e, e, ACT.Ln, t, bias=1.0)
            yield t
            t = p.stt(ln, z, 0.0, e, ALU.max, ALU.add, t, ln_free[h % 2], t_xm)
            lns[h, kc] = p.tt(ln[:, 0:128], ln[:, 0:128], M01, ALU.mult, t, t_k2)

        def turn():
            zb = s["b"]
            yield lns[h, kc]
            p.PE.wait(lns[h, kc])
            t = p.mm(p.bank(zb, wz - w, wz), TRI, ln, False, kc == 3)
            for kk in range(kc + 1, 4):
                p.PE.wait(lns[h, kk])
                wk = NX - 128 * kk
                t = p.mm(p.bank(zb, wz - wk, wz), ONE, L_[:, lo_of[kk]:lo_of[kk] + wk], False, kk == 3)
            if kc == 0:
                ln_free[h % 2] = t
            yield t
            at = W4[s["w"]]
            t = p.act(at[:, :w], p.bank(zb, wz - w, wz), ACT.Exp, t)
            p.leave(B4, zb, t)
            yield t
            s["at"] = p.tt(at[:, 0:128], at[:, 0:128], M01, ALU.mult, t)

        def value():
            first = h % 2 == 0 and kc == 3
            if first:
                y_of["s"] = yield from YP.take()
            yb = y_of["s"]
            yield [s["at"], p.bank_free[yb]]
            if first:
                p.PE.wait(p.bank_free[yb], t_v)
            p.PE.wait(s["at"])
            for m in range(kc, 4):
                o = p.bank(yb, 128 * m + 64 * (h % 2), 128 * m + 64 * (h % 2) + 64)
                t = p.mm(o, W4[s["w"]][:, 128 * (m - kc):128 * (m - kc) + 128], V[:, kc, 128 + 64 * h:192 + 64 * h],
                         first and m == kc, m == 3)
            w_free[s["w"]] = t
            w4.give(s["w"])
            if h % 2 and kc == 0:
                yield t
                f = 768 + 128 * i
                t2 = p.copy(Y[:, :, f:f + 128], p.bank(yb).rearrange("p (m d) -> p m d", m=4), t)
                t_y[f // 128] = t2
                p.leave(YP, yb, t2)

        return score, soft, turn, value

    t_out = [None] * 8
    oh = lambda k: p.XH[:, k, :] if k < 3 else QS[0][:, k - 3, :] if k < 6 else BQ[0][:, k - 6, :]
    ol = lambda k: p.XL[:, k, :] if k < 3 else QS[1][:, k - 3, :] if k < 6 else BQ[1][:, k - 6, :]
    olf = lambda k: p.XLf[:, k, :] if k < 3 else QS[2][:, k - 3, :] if k < 6 else BQ[2][:, k - 6, :]
    jk, jk_free, ss_free = Pool(0), [None], [None, None]

    def section(f0, f1, c, war):
        c0, c1 = f0 // 128, f1 // 128
        yield from until(lambda: all(k in t_y for k in range(c0, c1)) and known(war()))
        ts_ = [t_y[k] for k in range(c0, c1)]
        yield from jk.take()
        for m in range(4):
            yield ts_
            t = p.act(JK[:, :f1 - f0], Y[:, m, f0:f1], ACT.Square, ts_, jk_free[0], ss_free, accum_out=SS[:, m:m + 1])
            jk_free[0] = t
        yield t
        t = p.ts(SS[:, 4:8], SS[:, 0:4], 1.0 / (f1 - f0), EPS, ALU.mult, ALU.add, t)
        t = ss_free[0] = p.pow(SS[:, 0:4], SS[:, 4:8], t)
        yield t
        for m in range(4):
            yield
            t1 = p.ts(Y[:, m, f0:f1], Y[:, m, f0:f1], SS[:, m:m + 1], None, ALU.mult, ALU.bypass, t, ts_)
        ss_free[1] = t1
        jk.give(0)
        for k in range(c0, c1):
            b = yield from B4.take()
            yield [p.bank_free[b], t1]
            p.PE.wait(p.bank_free[b], t1)
            for m in range(4):
                t = p.tr(p.bank(b, 128 * m, 128 * m + 128), Y[:, m, 128 * k:128 * k + 128], m == 3)
            yield t
            t = p.act(olf(k), p.bank(b), ACT.Copy, t, war(), scale=col(14 + k))
            p.leave(B4, b, t)
            yield t
            t_out[k] = split(p, olf(k), oh(k), ol(k), t, war())

    MX = small("MX", 16)[:, :].rearrange("p (r c) -> p r c", r=2)
    p.tables("natural_log_exp_and_others")
    m_done = p.flow([soft_unit("m", 8 * i + 4 * j + m, i, j, m) for i in range(3) for j in range(2) for m in range(4)], 3)
    w_done = p.flow([soft_unit("w", 8 * i + 4 * j + m, i, j, m) for i in range(3) for j in range(2) for m in range(4)], 6)
    p.mix(0.3)
    yield from tiles("q", 1)
    yield from head(2)
    yield from tiles("q", 2)
    yield from head(3)
    yield from head(4)
    yield from head(5)
    yield from until(lambda: len(t_latent) == 3)
    for kind in "QK":
        for i in range(2):
            yield from tiles(kind, i)
    t_xm = [p.PE.last()]
    w_end = []

    def w_mark():
        yield from until(w_done)
        w_end.append(p.PE.last())
    p.spawn(w_mark(), 0)
    p.spawn(section(0, 384, 0, lambda: t_xm), 4)
    p.spawn(section(384, 768, 1, lambda: w_end or None), 4)
    yield from until(m_done)
    s_done = p.flow([stick_unit(4 * h + 3 - kc, h, kc) for h in range(4) for kc in (3, 2, 1, 0)], 3)
    s_end = []

    def s_mark():
        yield from until(s_done)
        s_end.append(p.PE.last())
    p.spawn(s_mark(), 0)
    p.spawn(section(768, 1024, 2, lambda: s_end or None), 4)

    def handover():
        yield from until(lambda: known(t_out))
        yield from B4.claim(0, 1, 2, 3)
        p.mix(None)
        for b in range(4):
            G.give(b)
    p.spawn(handover(), 0)
    return oh, ol, t_out


def second_block(p, sx, G, pos, scratch):
    r = Block2(p, sx)
    xh, xl = (lambda k: p.XH[:, k, :]), (lambda k: p.XL[:, k, :])
    f32 = lambda n, s, o: p.at(n, s, F32, p.BIG + o)
    f32r = lambda n, s, o: p.at(n, s, F32R, p.BIG + o)
    H = (f32r("H2H", [128, FC, NX], 0), f32r("H2L", [128, FC, NX], 45056),
         f32("H2Hf", [128, FC, NX], 0), f32("H2Lf", [128, FC, NX], 45056))
    SQM = f32("SQM", [128, 3, NX], 28672)
    hh, hl, ht = (lambda k: H[0][:, k, :]), (lambda k: H[1][:, k, :]), (lambda k: p.t_h[k])

    def norm(layer, kind, fresh=True):
        out = p.XMt = [None] * 8
        gen = (r.norm if fresh else r.modulate)(layer, kind, p.XH, p.XL, p.XLf, out)
        return (lambda k: out[k]), p.spawn(gen, 1)

    xt, task = norm(0, 0, False)
    for layer in range(2):
        yield from up_glu(p, xh, xl, xt, H, None, G, 3)
        yield from p.gemm(KC, DOWN, hh, hl, ht, NX, r.adder(layer, 3, p.XHf), G)
        xt, task = norm(layer, 1)
        yield from until(lambda: pos[4])
        oh, ol, t_out = yield from mixer2(p, G, layer, xh, xl, xt, task, scratch)
        yield from p.gemm(KC, [8], oh, ol, lambda k: t_out[k], NX, r.adder(layer, 4, SQM), G, lead=2)
        yield from G.claim(6, 7)
        xt, task = norm(layer, 2)
        yield from up_glu(p, xh, xl, xt, H, None, G, 3)
        yield from p.gemm(KC, DOWN, hh, hl, ht, NX, r.adder(layer, 5, None if layer else p.XHf), G)
        if layer == 0:
            xt, task = norm(1, 0)


def make_plan(p):
    A, plan, rows = p.A, p.plan, p.a_plan

    def W(name, n=1024, lo=0, hi=None):
        plan.extend((A[name][u], n) for u in range(A[name].shape[0])[lo:hi])

    def W_down(name):
        plan.extend((A[name][u, :, 0:128 * DOWN[u % 3]], 128 * DOWN[u % 3]) for u in range(24))

    cols = [(0, c, k) for c in (2, 3, 4, 5) for k in range(8)] + [(1, c, k) for c in range(6) for k in range(8)]
    for n, (l, c, k) in enumerate(cols):
        rows.append((A["wA1"][n], p.ada1_item(l, 8 * c + k, l == 0 or c < 2)))
    for l in range(2):
        for c in range(72):
            rows.append((A["wA2"][72 * l + c], p.ada2_item(l, c)))
    for name in ("w_k", "w_q", "w_vT", "w_va", "w_u", "w_va", "w_vF", "w_out0"):
        W(name)
    for i in range(4):
        W("w_k", lo=i, hi=i + 1)
        W("w_q", lo=i, hi=i + 1)
    W("w_u")
    W("w_out0")
    for _ in range(2):
        W("w_up0")
        W_down("w_down0")
    for _ in range(2):
        W("w_k1")
        W("w_v1")
    W("w_q1")
    W("w_out1")
    W("w_up1")
    W_down("w_down1")

    def W2(name, l, n=1024, lo=0, hi=None):
        plan.extend((A[name][l][u][:, 0:n], n) for u in range(A[name].shape[1])[lo:hi])

    def W2_down(name, l):
        plan.extend((A[name][l][u][:, 0:128 * DOWN[u % 3]], 128 * DOWN[u % 3]) for u in range(24))

    for l in range(2):
        W2("w_gu1", l)
        W2_down("w_dn1", l)
        W2("w_cq", l)
        W2("w_kpe", l, 512)
        W2("w_v2", l, 768)
        W2("w_va2", l, 384)
        for name, i in (("w_h", 0), ("w_qk2", 0), ("w_h", 1), ("w_qk2", 3), ("w_qk2", 1), ("w_h", 2), ("w_qk2", 2),
                        ("w_h", 3), ("w_h", 4), ("w_h", 5)):
            W2(name, l, 320 if name == "w_h" else 1024, i, i + 1)
        W2("w_qk2", l, lo=4)
        W2("w_out2", l)
        W2("w_gu2", l)
        W2_down("w_dn2", l)


def program(nc, A):
    p = Prog(nc, A)
    make_plan(p)
    t_c0, t_x0 = start(p)
    p.spawn(body(p, t_c0, t_x0), 9)
    p.spawn(p.prepare(), 2)
    p.spawn(p.rows(), 7)
    p.go()
    for slot in p.outputs:
        p.SP.wait((slot[0], slot[1], 0.0))
    finish(p)


def body(p, t_c0, t_x0):
    nc, A = p.nc, p.A
    f32 = lambda n, s, o: p.at(n, s, F32, p.BIG + o)
    f32r = lambda n, s, o: p.at(n, s, F32R, p.BIG + o)
    G = Pool(0, 1, 2)
    p.outputs = [p.slot("out")]
    mark = p.cst
    sx = Stream(p, 0, NX, p.X, t_x0, 6, 7)
    sc = Stream(p, 1, NC, p.C, t_c0, 4, 5)
    yield from even_mixer(p, G, sc)
    p.cst = mark
    yield from G.claim(4)

    HX = [f32r("HXH", [128, FC, NX], 0), f32r("HXL", [128, FC, NX], 45056),
          f32("HXHf", [128, FC, NX], 0), f32("HXLf", [128, FC, NX], 45056)]
    HC = [f32r("HCH", [128, FC, NC], 0), f32r("HCL", [128, FC, NC], 22528),
          f32("HCHf", [128, FC, NC], 0), f32("HCLf", [128, FC, NC], 22528)]
    CM = [f32r("CM2H", [128, KC, NC], 45056), f32r("CM2L", [128, KC, NC], 53248),
          f32("CM2Hf", [128, KC, NC], 45056), f32("CM2Lf", [128, KC, NC], 53248)]
    xh, xl, xt = (lambda k: p.XH[:, k, :]), (lambda k: p.XL[:, k, :]), (lambda k: p.XMt[k])
    ch, cl = (lambda k: CM[0][:, k, :]), (lambda k: CM[1][:, k, :])

    t_mix = [p.AC.last(), p.VE.last(), p.PE.last()]
    yx = f32("YX1", [128, 8, NX], 61440)
    sx.places(lambda k: yx[:, k, :], f32("SQX1", [128, 4, NX], 77824), t_mix)
    ct = [None] * 8
    p.spawn(sc.pre1(0, 2, CM[0], CM[1], CM[3], ct, t_mix), 3)
    yield from p.gemm(KC, [8], p.yh, p.yl, lambda k: p.t_y[k], NX, sx.evac, G, lead=3)
    p.XMt = [None] * 8
    x_task = p.spawn(chain(sx.post(0, 1), sx.pre1(0, 2, p.XH, p.XL, p.XLf, p.XMt, p.PE.last())), 1)
    yield from up_conv(p, sc, ch, cl, lambda k: ct[k], *HC, lambda j: None, G, 0)
    assert x_task[4]
    yc = f32("YC2", [128, 8, NC], 73728)
    sc.places(lambda k: yc[:, k, :], f32("SQC2", [128, 4, NC], 81920), [p.PE.last(), p.VE.last(), p.AC.last()])
    yield from down(p, sc, HC[0], HC[1], G)
    c_post = p.spawn(sc.post(0, 3), 2)
    t_post = []

    def war(j):
        assert j < 14 or c_post[4]
        if j >= 14 and not t_post:
            t_post.extend([p.PE.last(), p.VE.last(), p.AC.last()])
        return list(t_post)
    yield from up_conv(p, sx, xh, xl, xt, *HX, war, G, 0)
    sx.places(lambda k: p.XHf[:, k, :], p.XLf, p.PE.last())
    yield from down(p, sx, HX[0], HX[1], G)
    ct = [None] * 8
    c_task = p.spawn(sc.pre1(1, 0, CM[0], CM[1], CM[3], ct, p.PE.last()), 0)
    p.XMt = [None] * 8
    x_task = p.spawn(chain(sx.post(0, 3), sx.pre1(1, 0, p.XH, p.XL, p.XLf, p.XMt)), 1)

    QH, QL, t_out = yield from odd_mixer(p, sx, xt, x_task, c_task, CM[0], CM[1], lambda k: ct[k], G)
    sx.places(lambda k: p.XHf[:, k, :], p.XLf)
    p.t_cw = p.SP.dma(p.CW[:, :, :], A["cw1"], p.cw_slot, p.AC.last(), p.VE.last())
    rope_d = nc.dram_tensor("rope_scratch", [64, NX], F32, kind="Internal").ap()
    bias_t = nc.dram_tensor("bias_scratch", [6, 128, 1024], F32, kind="Internal").ap()
    skew = [bass.AP(tensor=bias_t.tensor, offset=131072 * h + 1, ap=[[1025, 128], [256, 4], [1, 128]]) for h in range(6)]
    scratch = {"rope": rope_d, "bias": bias_t, "skew": skew}
    pos = p.spawn(positions(p, scratch), 6)
    yield from p.gemm(KC, [8], lambda k: QH[:, k, :], lambda k: QL[:, k, :], lambda k: t_out[k], NX, sx.evac, G)
    p.XMt = [None] * 8
    p.spawn(chain(sx.post(1, 1), sx.pre1(1, 2, p.XH, p.XL, p.XLf, p.XMt)), 1)
    yield from up_conv(p, sx, xh, xl, xt, *HX, lambda j: None, G, 3)
    sx.places(lambda k: p.XHf[:, k, :], p.XLf)
    yield from down(p, sx, HX[0], HX[1], G)
    p.XMt = [None] * 8
    t = p.spawn(sx.post(1, 3), 1)
    yield from until(lambda: t[4])
    yield from second_block(p, sx, G, pos, scratch)


def finish(p):
    with p.nc.Block() as block:
        for name, line in p.lines.items():
            def body(e, line=line):
                for op in line.ops:
                    op(e)
            {"tensor": block.tensor, "scalar": block.scalar, "vector": block.vector,
             "gpsimd": block.gpsimd, "sync": block.sync}[name](body)


def pack(I):
    def cols(v):
        v = np.asarray(v)
        return v.reshape(v.shape[:-1] + (-1, 128))

    def F(w, tiles=None):
        K, M = w.shape
        return w.reshape(K // 128, 128, M // 128, 128).transpose(2, 1, 0, 3).reshape(M // 128, 128, K)

    def T(w, cnt):
        K, M = w.shape
        return w.reshape(K // 128 // cnt, cnt, 128, M).transpose(0, 2, 1, 3).reshape(-1, 128, cnt * M)

    def pairs(w, a, b):
        n = w.shape[1] // 2
        K = w.shape[0]
        t = w.reshape(K, 2, n // 128, 128)[:, [a, b]]
        return t.transpose(0, 2, 1, 3).reshape(K, 2 * n)

    def D(w):
        t = w.reshape(FC, 128, KC, 128).transpose(2, 1, 0, 3)
        out = np.zeros((KC, 3, 128, 8, 128), w.dtype)
        k = 0
        for u, c in enumerate(DOWN):
            out[:, u, :, :c] = t[:, :, k:k + c]
            k += c
        return out.reshape(24, 128, 1024)

    O = {}
    c2 = lambda a, b: np.stack([a, b], -1)
    O["ccol"] = c2(cols(I["c"][0]).T, cols(I["c_ctx"]).T)
    O["ident"] = np.eye(128, dtype=np.float32)
    O["b1"] = cols(I["b_ada"]).transpose(2, 0, 1)
    O["ng1"] = cols(I["norm_g"]).transpose(3, 0, 1, 2)
    O["ctxT"] = I["ctx"][0].T.reshape(KC, 128, NC).transpose(1, 0, 2)
    O["xT"] = I["x"][0].T.reshape(KC, 128, NX).transpose(1, 0, 2)
    O["crow"] = np.broadcast_to(np.stack([I["c"][0], I["c_ctx"]])[None], (128, 2, 1024))
    O["b2"] = cols(I["b_mod_2"]).transpose(2, 0, 1)
    O["ng2"] = cols(I["norm_g_2"]).transpose(3, 0, 1, 2)
    for l in range(2):
        v = np.concatenate([I["conv_w"][l], I["conv_b"][l][None]])
        O[f"cw{l}"] = cols(v).transpose(2, 0, 1).reshape(128, 4, 2, FC).transpose(0, 1, 3, 2).reshape(128, 4, 44)
        O[f"w_up{l}"] = F(pairs(I["w_up"][l], 0, 1))
        O[f"w_down{l}"] = D(I["w_down"][l])
    wt = I["w_ada"].transpose(0, 2, 1).reshape(2, 48, 128, 1024)
    O["wA1"] = np.concatenate([wt[0, 16:], wt[1]])
    f = F(I["w_ada"][0][:, :2048])
    O["wP"], O["wV"] = f[8:16], wt[0, 0:8]
    w = I["w_in_ab"][0]
    O["w_u"], O["w_va"] = F(w[:, 0:512]), T(w[:, 512:1024], 2)
    O["w_q"], O["w_k"] = F(w[:, 1024:1536]), F(w[:, 1536:2048])
    O["w_vF"], O["w_vT"] = F(w[:, 2048:2560]), T(w[:, 2048:2560], 2)
    O["w_s"] = I["a_w_s"][0].transpose(2, 0, 1)
    O["b_s"] = np.broadcast_to(I["a_b_s"][0][None], (128, 4, 128))
    O["gv"] = cols(I["a_v_g"][0]).T
    O["w_out0"] = F(I["w_out_ab"][0])
    w = I["w_qkv_c"][0]
    heads = np.array([[h, h + 4] for h in range(4)] + [[h, h + 4] for h in range(8, 12)]).ravel()
    order = (heads[:, None] * 64 + np.arange(64)).ravel()
    O["w_q1"], O["w_k1"], O["w_v1"] = F(w[:, 0:1024][:, order]), F(w[:, 1024:1280]), T(w[:, 1280:1536], 4)
    O["w_out1"] = F(I["w_out_c"][0][order])
    O["qk_g1"] = np.tile(c2(I["c_q_g"][0], I["c_k_g"][0]), (2, 1))
    O["bi2"] = np.repeat(np.eye(2, dtype=np.float32), 64, axis=0)
    O["sel2"] = np.ascontiguousarray(O["bi2"].T)
    inv = (np.float32(10000.0) ** (-np.arange(16, dtype=np.float32) / np.float32(16))).astype(np.float32)
    t = np.arange(NX)
    ang = np.concatenate([(t // 64).astype(np.float32)[:, None] * inv, (t % 64).astype(np.float32)[:, None] * inv], 1)
    cos, sin = np.cos(ang).T, np.sin(ang).T
    O["rope1"] = np.stack([np.tile(cos, (4, 1)), np.tile(np.concatenate([-sin, sin]), (2, 1))], 1).astype(np.float32)
    rpb = I["b_rpb"][0]
    out = np.full((8, 128, 4, 256), -1e30, np.float32)
    q = np.arange(128)
    key = np.arange(256)
    for b in range(4):
        qr, qc = (q // 8) % 8, 16 * b + 8 * (q // 64) + q % 8
        kr, kc = (key // 8) % 8, 8 * (0, 1, 3, 4)[b] + 8 * (key // 64) + key % 8
        c0 = np.clip(qc - 8, 0, 48)
        ok = (kc[None] >= c0[:, None]) & (kc[None] < c0[:, None] + 16)
        dc = np.clip(kc[None] - qc[:, None], -15, 15) + 15
        dr = kr[None] - qr[:, None] + 7
        out[:, :, b, :] = np.where(ok[None], rpb[:, dr, dc], np.float32(-1e30))
    O["rpb"] = out
    J = {k[:-2]: v for k, v in I.items() if k.endswith("_2")}
    O["crow2"] = np.broadcast_to(J["c"], (128, 1024))
    wt = J["w_mod"].transpose(0, 2, 1)
    O["wA2"] = wt.reshape(144, 128, 1024)
    both = lambda f: np.stack([f(l) for l in range(2)])
    for n, a in (("1", "ffn1"), ("2", "ffn2")):
        O["w_gu" + n] = both(lambda l: F(pairs(J[f"w_{a}_gu"][l], 0, 1)))
        O["w_dn" + n] = both(lambda l: D(J[f"w_{a}_down"][l]))
    sw = np.arange(32) ^ 16
    win = J["w_in"]
    O["w_cq"] = both(lambda l: F(win[l][:, 0:384]))
    kp = np.concatenate([384 + np.arange(32), 384 + sw])
    O["w_kpe"] = both(lambda l: win[l][:, kp].reshape(8, 128, 64).transpose(1, 0, 2).reshape(1, 128, 512))
    vc = np.concatenate([np.arange(928, 1056), np.arange(1568, 1824)])
    O["w_v2"] = both(lambda l: T(win[l][:, vc], 2))
    wh = [0, 3, 1, 4, 2, 5]
    qc = np.concatenate([(416 + 64 * np.array(wh)[:, None] + np.arange(64)).ravel(), np.arange(800, 928),
                         np.arange(1056, 1568)])
    O["w_qk2"] = both(lambda l: F(win[l][:, qc]))
    hq = np.concatenate([np.arange(96), 64 + sw])
    def head(l, h):
        q = J["w_uq"][l][:, 96 * h + hq].reshape(2, 128, 128).transpose(1, 0, 2).reshape(128, 256)
        return np.concatenate([q, J["w_ukv"][l][:, 128 * h:128 * h + 64]], 1)
    O["w_h"] = both(lambda l: np.stack([head(l, h) for h in range(6)]))
    O["w_va2"] = both(lambda l: J["w_ukv"][l].reshape(128, 6, 2, 64)[:, :, 1].reshape(1, 128, 384))
    rows = np.concatenate([np.arange(384), (384 + 64 * np.array(wh)[:, None] + np.arange(64)).ravel(), np.arange(768, 1024)])
    O["w_out2"] = both(lambda l: F(J["w_out"][l][rows]))
    g2 = np.zeros((2, 128, 24), np.float32)
    for l in range(2):
        g2[l, :, 0] = J["mla_q_norm"][l][hq]
        g2[l, :64, 1] = J["mla_k_norm"][l][:64]
        g2[l, :64, 2] = J["mla_k_norm"][l][64 + np.concatenate([np.arange(32), sw])]
        g2[l, :, 3:5] = J["q_a_norm"][l].reshape(2, 128).T
        g2[l, :, 5] = J["kv_a_norm"][l]
        g2[l, :, 6] = np.tile(J["swa_q_norm"][l], 2)
        g2[l, :, 7] = np.tile(J["swa_k_norm"][l], 2)
        g2[l, :, 8:14] = J["sinks"][l][None]
        g2[l, :, 14:22] = J["out_norm"][l][rows].reshape(8, 128).T
    O["g2"] = g2
    i128 = np.arange(128)
    k2 = np.zeros((128, 6, 128), np.float32)
    m = i128 % 32
    k2[:64, 0, :] = (i128[None, :] >= 64) & (i128[:64, None] % 32 == m[None, :])
    k2[:, 1, :] = -1.0 * (i128[:, None] >= i128[None, :])
    k2[:, 2, :] = i128[:, None] < i128[None, :]
    k2[:, 3, :] = np.where(i128[None, :] > i128[:, None], -1e30, 0)
    k2[:, 4, :] = -1
    k2[:2, 5, :] = O["sel2"]
    O["k2"] = k2
    pos = J["positions"][0]
    O["pos_row"] = np.broadcast_to(pos, (64, NX))
    idx = 128 * np.arange(4)[None, :, None] + i128[:, None, None] - 127 + i128[None, None, :]
    O["pos_win"] = np.concatenate([pos[np.maximum(idx, 0)], pos[128 * np.arange(4)[None, :, None] + i128[:, None, None]]], -1)
    freq = (np.float32(10000.0) ** (-np.arange(16, dtype=np.float32) / np.float32(16))).astype(np.float32)
    fq = np.zeros((64, 4), np.float32)
    fq[:, 0] = np.tile(freq, 4)
    fq[:32, 1], fq[:32, 2] = np.pi / 2, 0.25
    fq[:, 3] = np.where(np.arange(64) // 16 == 2, -1, 1)
    O["freq"] = fq
    O["rel_bias"] = np.broadcast_to(J["rel_bias"], (128, 32, 6))
    O["mask_fill"] = np.full((128, 1024), -1e30, np.float32)
    return {k: np.ascontiguousarray(v) for k, v in O.items()}


def kernel(**inputs):
    import concourse.bacc as _bacc
    from concourse.bass_utils import run_bass_kernel_spmd as _run

    arrays = pack({k: np.asarray(v) for k, v in inputs.items()})
    nc = _bacc.Bacc("TRN2", target_bir_lowering=False, num_devices=1)
    A = {k: nc.dram_tensor(k, v.shape, mybir.dt.from_np(v.dtype), kind="ExternalInput").ap() for k, v in arrays.items()}
    A["out"] = nc.dram_tensor("out", (128, KC, NX), F32, kind="ExternalOutput").ap()
    program(nc, A)
    r = _run(nc, [arrays], core_ids=[0])
    return r.results[0]["out"].transpose(2, 1, 0).reshape(1, NX, 1024)
```
